# Optimizing a Trainium2 kernel written in Bass

```python
import jax, jax.numpy as jnp
from jax import lax
import numpy as np
import math

D_MODEL = 2048
BATCH = 1
SEQ = 256
DEPTH = 2

PLE_DIM = 256
D_FF = 4 * D_MODEL
EPS = 1e-6
NEG = -1e30
FORCE_BONUS = 1e6

LRU_WIDTH = D_MODEL // 2
LRU_HEADS = 16
LRU_HEAD_DIM = LRU_WIDTH // LRU_HEADS
CONV_WIDTH = 4
LRU_C = 8.0
POOL_WIDTH = D_MODEL // 2
POOL_WINDOWS = (2, 4, 8, 16)
POOL_GROUPS = len(POOL_WINDOWS)
POOL_GROUP_DIM = POOL_WIDTH // POOL_GROUPS
AB_IN = 2 * LRU_WIDTH + POOL_WIDTH
AB_MIX = LRU_WIDTH + POOL_WIDTH

N_HEADS = 16
HEAD_DIM = D_MODEL // N_HEADS
N_KV = 4
HPG = N_HEADS // N_KV
KV_WIDTH = N_KV * HEAD_DIM
CMP_LEN = 32
CMP_STRIDE = 16
CMP_HIDDEN = 512
SEL_LEN = 64
SEL_TOPN = 16
WINDOW = 512
N_BRANCH = 3
Q_BLOCK = 32
C_MIX = N_HEADS * HEAD_DIM
C_IN = C_MIX + 6 * KV_WIDTH + N_BRANCH * N_HEADS

N_EVEN = (DEPTH + 1) // 2
N_ODD = DEPTH // 2


def rmsnorm(x, g):
    xf = x.astype(jnp.float32)
    y = xf * lax.rsqrt(jnp.mean(xf * xf, axis=-1, keepdims=True) + EPS)
    return (y * g.astype(jnp.float32)).astype(x.dtype)

def alibi_slopes():
    h = jnp.arange(1, N_HEADS + 1, dtype=jnp.float32)
    return jnp.exp2(-8.0 * h / N_HEADS).reshape(N_KV, HPG)

def causal_conv(x, w, b):
    S = x.shape[1]
    xp = jnp.pad(x, ((0, 0), (CONV_WIDTH - 1, 0), (0, 0)))
    out = b
    for k in range(CONV_WIDTH):
        out = out + xp[:, k:k + S] * w[k]
    return out

def _lin_combine(c1, c2):
    a1, b1 = c1
    a2, b2 = c2
    return a1 * a2, a2 * b1 + b2

def rg_lru(x, w_r, b_r, w_i, b_i, lam):
    B, S, W = x.shape
    xf = x.astype(jnp.float32)
    xh = xf.reshape(B, S, LRU_HEADS, LRU_HEAD_DIM)
    r = jax.nn.sigmoid(jnp.einsum('bshi,hij->bshj', xh, w_r.astype(jnp.float32)).reshape(B, S, W) + b_r.astype(jnp.float32))
    i = jax.nn.sigmoid(jnp.einsum('bshi,hij->bshj', xh, w_i.astype(jnp.float32)).reshape(B, S, W) + b_i.astype(jnp.float32))
    log_a = -LRU_C * r * jax.nn.softplus(-lam.astype(jnp.float32))
    a = jnp.exp(log_a)
    bvals = jnp.sqrt(-jnp.expm1(2.0 * log_a)) * (i * xf)
    _, h = lax.associative_scan(_lin_combine, (a, bvals), axis=1)
    return h.astype(x.dtype)

def pool_mixer(u, w, scale):
    B, S, _ = u.shape
    ug = u.astype(jnp.float32).reshape(B, S, POOL_GROUPS, POOL_GROUP_DIM)
    cs = jnp.cumsum(ug, axis=1)
    t = jnp.arange(S)
    outs = []
    for g, win in enumerate(POOL_WINDOWS):
        c = cs[:, :, g]
        prev = jnp.pad(c, ((0, 0), (win, 0), (0, 0)))[:, :S]
        cnt = jnp.minimum(t + 1, win).astype(jnp.float32)[None, :, None]
        outs.append((c - prev) / cnt - ug[:, :, g])
    d = jnp.stack(outs, axis=2)
    y = jnp.einsum('bsgi,gij->bsgj', d, w.astype(jnp.float32)).reshape(B, S, POOL_WIDTH)
    return (y * scale.astype(jnp.float32)).astype(u.dtype)

def ab_mixer(hn, w_in, conv_w, conv_b, w_r, b_r, w_i, b_i, lam, pool_w, pool_scale, w_out):
    z = hn @ w_in
    xr, gate, u = jnp.split(z, [LRU_WIDTH, 2 * LRU_WIDTH], axis=-1)
    xr = causal_conv(xr, conv_w, conv_b)
    y_lru = rg_lru(xr, w_r, b_r, w_i, b_i, lam) * jax.nn.gelu(gate)
    y_pool = pool_mixer(u, pool_w, pool_scale)
    return jnp.concatenate([y_lru, y_pool], axis=-1) @ w_out

def compress(kv, pos, w1, w2):
    S = kv.shape[1]
    n_cmp = (S - CMP_LEN) // CMP_STRIDE + 1
    idx = jnp.arange(n_cmp)[:, None] * CMP_STRIDE + jnp.arange(CMP_LEN)[None, :]
    blocks = kv[:, idx] + pos[None, None, :, None, :]
    hid = jax.nn.gelu(jnp.einsum('bnlgd,ldf->bngf', blocks, w1))
    return jnp.einsum('bngf,fd->bngd', hid, w2)

def nsa_mixer(hn, w_in, pos_k, w1_k, w2_k, pos_v, w1_v, w2_v, w_out):
    B, S, _ = hn.shape
    z = hn @ w_in
    splits = np.cumsum([C_MIX] + [KV_WIDTH] * 6).tolist()
    q, kc, vc, ks, vs, kw, vw, gl = jnp.split(z, splits, axis=-1)
    q = q.reshape(B, S, N_KV, HPG, HEAD_DIM) * (HEAD_DIM ** -0.5)
    kv_shape = (B, S, N_KV, HEAD_DIM)
    kc, vc, ks, vs, kw, vw = [a.reshape(kv_shape) for a in (kc, vc, ks, vs, kw, vw)]
    gates = jax.nn.sigmoid(gl.astype(jnp.float32)).reshape(B, S, N_BRANCH, N_KV, HPG)

    k_cmp = compress(kc, pos_k, w1_k, w2_k).astype(jnp.float32)
    v_cmp = compress(vc, pos_v, w1_v, w2_v).astype(jnp.float32)
    n_cmp = k_cmp.shape[1]
    n_sel = S // SEL_LEN
    top_n = min(SEL_TOPN, n_sel)
    cmp_start = jnp.arange(n_cmp) * CMP_STRIDE
    cmp_end = cmp_start + CMP_LEN - 1
    sel_start = jnp.arange(n_sel) * SEL_LEN
    ov = ((cmp_start[:, None] < sel_start[None, :] + SEL_LEN) & (cmp_start[:, None] + CMP_LEN > sel_start[None, :])).astype(jnp.float32)
    ks_blocks = ks.reshape(B, n_sel, SEL_LEN, N_KV, HEAD_DIM).transpose(0, 3, 1, 2, 4)
    vs_blocks = vs.reshape(B, n_sel, SEL_LEN, N_KV, HEAD_DIM).transpose(0, 3, 1, 2, 4)
    kw_pad = jnp.pad(kw, ((0, 0), (WINDOW, 0), (0, 0), (0, 0)))
    vw_pad = jnp.pad(vw, ((0, 0), (WINDOW, 0), (0, 0), (0, 0)))
    slopes = alibi_slopes()
    n_qblk = S // Q_BLOCK
    q_blocks = q.reshape(B, n_qblk, Q_BLOCK, N_KV, HPG, HEAD_DIM).swapaxes(0, 1)
    g_blocks = gates.reshape(B, n_qblk, Q_BLOCK, N_BRANCH, N_KV, HPG).swapaxes(0, 1)
    bi = jnp.arange(B)[:, None, None, None]
    gi = jnp.arange(N_KV)[None, :, None, None]
    jj = jnp.arange(n_sel)

    def one_block(args):
        blk, qb, gb = args
        t0 = blk * Q_BLOCK
        t = t0 + jnp.arange(Q_BLOCK)
        qf = qb.astype(jnp.float32)
        dist_c = (t[:, None] - cmp_end[None, :]).astype(jnp.float32)
        valid_c = dist_c >= 0
        s_c = jnp.einsum('bqghd,bngd->bghqn', qf, k_cmp) - slopes[None, :, :, None, None] * dist_c
        s_c = jnp.where(valid_c, s_c, NEG)
        p_c = jnp.where(valid_c, jax.nn.softmax(s_c, axis=-1), 0.0)
        o_c = jnp.einsum('bghqn,bngd->bqghd', p_c, v_cmp)
        imp = jnp.einsum('bghqn,nm->bgqm', p_c, ov)
        cur = t // SEL_LEN
        forced = (jj[None, :] == 0) | (jj[None, :] == cur[:, None]) | (jj[None, :] == cur[:, None] - 1)
        causal_s = sel_start[None, :] <= t[:, None]
        imp = jnp.where(forced, imp + FORCE_BONUS, imp)
        imp = jnp.where(causal_s, imp, NEG)
        _, idx = lax.top_k(imp, top_n)
        k_g = ks_blocks[bi, gi, idx].astype(jnp.float32)
        v_g = vs_blocks[bi, gi, idx].astype(jnp.float32)
        pos = idx[..., None] * SEL_LEN + jnp.arange(SEL_LEN)
        dist_s = (t[None, None, :, None, None] - pos).astype(jnp.float32)[:, :, None]
        s_s = jnp.einsum('bqghd,bgqnkd->bghqnk', qf, k_g) - slopes[None, :, :, None, None, None] * dist_s
        s_s = jnp.where(dist_s >= 0, s_s, NEG).reshape(B, N_KV, HPG, Q_BLOCK, top_n * SEL_LEN)
        p_s = jax.nn.softmax(s_s, axis=-1).reshape(B, N_KV, HPG, Q_BLOCK, top_n, SEL_LEN)
        o_s = jnp.einsum('bghqnk,bgqnkd->bqghd', p_s, v_g)
        kwb = lax.dynamic_slice_in_dim(kw_pad, t0, WINDOW + Q_BLOCK, axis=1).astype(jnp.float32)
        vwb = lax.dynamic_slice_in_dim(vw_pad, t0, WINDOW + Q_BLOCK, axis=1).astype(jnp.float32)
        s_pos = t0 - WINDOW + jnp.arange(WINDOW + Q_BLOCK)
        dist_w = t[:, None] - s_pos[None, :]
        valid_w = (dist_w >= 0) & (dist_w < WINDOW) & (s_pos[None, :] >= 0)
        s_w = jnp.einsum('bqghd,bkgd->bghqk', qf, kwb) - slopes[None, :, :, None, None] * dist_w.astype(jnp.float32)
        p_w = jax.nn.softmax(jnp.where(valid_w, s_w, NEG), axis=-1)
        o_w = jnp.einsum('bghqk,bkgd->bqghd', p_w, vwb)
        o = gb[:, :, 0, :, :, None] * o_c + gb[:, :, 1, :, :, None] * o_s + gb[:, :, 2, :, :, None] * o_w
        return o.astype(hn.dtype)

    o = lax.map(one_block, (jnp.arange(n_qblk), q_blocks, g_blocks))
    o = o.swapaxes(0, 1).reshape(B, S, C_MIX)
    return o @ w_out

def first_inputs(seed: int = 0) -> dict:
    key = jax.random.key(seed)
    keys = iter(jax.random.split(key, 48))

    def nrm(shape, scale):
        return jax.random.normal(next(keys), shape, jnp.float32) * scale

    def gain(shape):
        return 1.0 + nrm(shape, 0.05)

    u = jax.random.uniform(next(keys), (N_EVEN, LRU_WIDTH), jnp.float32, 0.9, 0.999)
    s = u ** (1.0 / LRU_C)
    lam = jnp.log(s) - jnp.log1p(-s)
    return {
        'x': nrm((BATCH, SEQ, D_MODEL), 1.0),
        'p': nrm((DEPTH, BATCH, SEQ, PLE_DIM), 1.0),
        'ln_mix_g': gain((DEPTH, D_MODEL)),
        'ab_w_in': nrm((N_EVEN, D_MODEL, AB_IN), D_MODEL ** -0.5),
        'ab_conv_w': nrm((N_EVEN, CONV_WIDTH, LRU_WIDTH), CONV_WIDTH ** -0.5),
        'ab_conv_b': nrm((N_EVEN, LRU_WIDTH), 0.01),
        'ab_w_rgate': nrm((N_EVEN, LRU_HEADS, LRU_HEAD_DIM, LRU_HEAD_DIM), LRU_HEAD_DIM ** -0.5),
        'ab_b_rgate': nrm((N_EVEN, LRU_WIDTH), 0.1),
        'ab_w_igate': nrm((N_EVEN, LRU_HEADS, LRU_HEAD_DIM, LRU_HEAD_DIM), LRU_HEAD_DIM ** -0.5),
        'ab_b_igate': nrm((N_EVEN, LRU_WIDTH), 0.1),
        'ab_lambda': lam,
        'ab_pool_w': nrm((N_EVEN, POOL_GROUPS, POOL_GROUP_DIM, POOL_GROUP_DIM), POOL_GROUP_DIM ** -0.5),
        'ab_pool_scale': gain((N_EVEN, POOL_WIDTH)),
        'ab_w_out': nrm((N_EVEN, AB_MIX, D_MODEL), AB_MIX ** -0.5),
        'c_w_in': nrm((N_ODD, D_MODEL, C_IN), D_MODEL ** -0.5),
        'c_cmp_pos_k': nrm((N_ODD, CMP_LEN, HEAD_DIM), 0.02),
        'c_cmp_w1_k': nrm((N_ODD, CMP_LEN, HEAD_DIM, CMP_HIDDEN), (CMP_LEN * HEAD_DIM) ** -0.5),
        'c_cmp_w2_k': nrm((N_ODD, CMP_HIDDEN, HEAD_DIM), CMP_HIDDEN ** -0.5),
        'c_cmp_pos_v': nrm((N_ODD, CMP_LEN, HEAD_DIM), 0.02),
        'c_cmp_w1_v': nrm((N_ODD, CMP_LEN, HEAD_DIM, CMP_HIDDEN), (CMP_LEN * HEAD_DIM) ** -0.5),
        'c_cmp_w2_v': nrm((N_ODD, CMP_HIDDEN, HEAD_DIM), CMP_HIDDEN ** -0.5),
        'c_w_out': nrm((N_ODD, C_MIX, D_MODEL), C_MIX ** -0.5),
        'ln_mlp_g': gain((DEPTH, D_MODEL)),
        'mlp_w_up': nrm((DEPTH, D_MODEL, D_FF), D_MODEL ** -0.5),
        'mlp_w_down': nrm((DEPTH, D_FF, D_MODEL), D_FF ** -0.5),
        'ln_ple_g': gain((DEPTH, D_MODEL)),
        'ple_w_gate': nrm((DEPTH, D_MODEL, D_MODEL), D_MODEL ** -0.5),
        'ple_w_proj': nrm((DEPTH, PLE_DIM, D_MODEL), PLE_DIM ** -0.5),
        'ln_final_g': gain((D_MODEL,)),
    }

def first_block(x, p, ln_mix_g, ab_w_in, ab_conv_w, ab_conv_b, ab_w_rgate, ab_b_rgate, ab_w_igate, ab_b_igate, ab_lambda, ab_pool_w, ab_pool_scale, ab_w_out, c_w_in, c_cmp_pos_k, c_cmp_w1_k, c_cmp_w2_k, c_cmp_pos_v, c_cmp_w1_v, c_cmp_w2_v, c_w_out, ln_mlp_g, mlp_w_up, mlp_w_down, ln_ple_g, ple_w_gate, ple_w_proj, ln_final_g):
    h = x
    for i in range(DEPTH):
        j = i // 2
        hn = rmsnorm(h, ln_mix_g[i])
        if i % 2 == 0:
            h = h + ab_mixer(hn, ab_w_in[j], ab_conv_w[j], ab_conv_b[j], ab_w_rgate[j], ab_b_rgate[j], ab_w_igate[j], ab_b_igate[j], ab_lambda[j], ab_pool_w[j], ab_pool_scale[j], ab_w_out[j])
        else:
            h = h + nsa_mixer(hn, c_w_in[j], c_cmp_pos_k[j], c_cmp_w1_k[j], c_cmp_w2_k[j], c_cmp_pos_v[j], c_cmp_w1_v[j], c_cmp_w2_v[j], c_w_out[j])
        hn = rmsnorm(h, ln_mlp_g[i])
        h = h + jnp.square(jax.nn.relu(hn @ mlp_w_up[i])) @ mlp_w_down[i]
        gate = jax.nn.sigmoid(rmsnorm(h, ln_ple_g[i]) @ ple_w_gate[i])
        h = h + gate * (p[i] @ ple_w_proj[i])
    return rmsnorm(h, ln_final_g)


HEAD_DIM_2 = 128
N_HEADS_2 = D_MODEL // HEAD_DIM_2
A_Q_HEADS = N_HEADS_2 // 2
A_KV_HEADS = A_Q_HEADS // 4
A_HALF_WINDOW = 128
B_HEADS = N_HEADS_2 - A_Q_HEADS
B_CONFIGS = ((128, 1), (512, 4), (2048, 16))
C_HEADS = N_HEADS_2
GRID_W = 64
NA_KH = 8
NA_KW = 16
RMS_EPS = 1e-5
NEG_2 = -1e30

A_Q_COLS = A_Q_HEADS * HEAD_DIM_2
A_KV_COLS = A_KV_HEADS * HEAD_DIM_2
B_COLS = B_HEADS * HEAD_DIM_2
AB_WIDTH = A_Q_COLS + B_COLS
AB_SPLITS = (A_Q_COLS,
             A_Q_COLS + A_KV_COLS,
             A_Q_COLS + 2 * A_KV_COLS,
             A_Q_COLS + 2 * A_KV_COLS + B_COLS,
             A_Q_COLS + 2 * A_KV_COLS + 2 * B_COLS,
             A_Q_COLS + 2 * A_KV_COLS + 3 * B_COLS)
AB_IN_COLS = A_Q_COLS + 2 * A_KV_COLS + 3 * B_COLS + AB_WIDTH
C_WIDTH = C_HEADS * HEAD_DIM_2
C_IN_COLS = 4 * C_WIDTH


def _rmsnorm(x, g):
    xf = x.astype(jnp.float32)
    y = xf * lax.rsqrt(jnp.mean(xf * xf, axis=-1, keepdims=True) + RMS_EPS)
    return (y * g.astype(jnp.float32)).astype(x.dtype)

def _alibi_slopes(n):
    return jnp.exp2(-8.0 * jnp.arange(1, n + 1, dtype=jnp.float32) / n)

def _banded_attention(q, k, v, half, dist_scale, slopes, sink=None):
    n, L, hq, dh = q.shape
    hkv = k.shape[2]
    g = hq // hkv
    blk = half
    nb = -(-L // blk)
    lp = nb * blk
    qp = jnp.pad(q, ((0, 0), (0, lp - L), (0, 0), (0, 0)))
    kvpad = ((0, 0), (blk, lp - L + blk), (0, 0), (0, 0))
    kp = jnp.pad(k, kvpad).reshape(n, nb + 2, blk, hkv, dh)
    vp = jnp.pad(v, kvpad).reshape(n, nb + 2, blk, hkv, dh)
    kw = jnp.concatenate([kp[:, :-2], kp[:, 1:-1], kp[:, 2:]], axis=2)
    vw = jnp.concatenate([vp[:, :-2], vp[:, 1:-1], vp[:, 2:]], axis=2)
    qb = qp.reshape(n, nb, blk, hkv, g, dh)
    s = jnp.einsum('nbqkgd,nbskd->nbkgqs', qb, kw).astype(jnp.float32) * (dh ** -0.5)
    rel = jnp.arange(3 * blk)[None, :] - blk - jnp.arange(blk)[:, None]
    kpos = jnp.arange(nb)[:, None] * blk - blk + jnp.arange(3 * blk)[None, :]
    valid = (jnp.abs(rel) <= half)[None] & ((kpos >= 0) & (kpos < L))[:, None, :]
    dist = (jnp.abs(rel) * dist_scale).astype(jnp.float32)
    bias = -slopes.astype(jnp.float32).reshape(hkv, g)[:, :, None, None] * dist
    s = jnp.where(valid[None, :, None, None], s + bias, NEG_2)
    m = jnp.max(s, axis=-1)
    if sink is not None:
        sk = sink.astype(jnp.float32).reshape(hkv, g)[None, None, :, :, None]
        m = jnp.maximum(m, sk)
    e = jnp.exp(s - m[..., None])
    denom = jnp.sum(e, axis=-1)
    if sink is not None:
        denom = denom + jnp.exp(sk - m)
    p = e / denom[..., None]
    o = jnp.einsum('nbkgqs,nbskd->nbqkgd', p.astype(v.dtype), vw).reshape(n, lp, hq, dh)[:, :L]
    lse = (m + jnp.log(denom)).transpose(0, 1, 4, 2, 3).reshape(n, lp, hq)[:, :L]
    return o, lse

def _dilated_mixture(q, k, v, slopes):
    b, s, h, dh = q.shape
    outs, lses = [], []
    for window, d in B_CONFIGS:
        ls = s // d

        def fold(t):
            return t.reshape(b, ls, d, h, dh).transpose(0, 2, 1, 3, 4).reshape(b * d, ls, h, dh)

        o, lse = _banded_attention(fold(q), fold(k), fold(v), window // (2 * d), d, slopes)
        outs.append(o.reshape(b, d, ls, h, dh).transpose(0, 2, 1, 3, 4).reshape(b, s, h, dh))
        lses.append(lse.reshape(b, d, ls, h).transpose(0, 2, 1, 3).reshape(b, s, h))
    w = jax.nn.softmax(jnp.stack(lses), axis=0)
    out = jnp.einsum('cbsh,cbshd->bshd', w, jnp.stack(outs).astype(jnp.float32))
    return out.astype(q.dtype)

def _neighbourhood_attention(q, k, v, rpb):
    b, s, h, dh = q.shape
    rows = s // GRID_W
    kh = min(NA_KH, rows)
    kw = NA_KW
    qg = q.reshape(b, rows, GRID_W, h, dh).transpose(1, 0, 2, 3, 4)
    kg = k.reshape(b, rows, GRID_W, h, dh)
    vg = v.reshape(b, rows, GRID_W, h, dh)
    col = jnp.arange(GRID_W)
    col_start = jnp.clip(col - kw // 2, 0, GRID_W - kw)
    col_mask = (col[None, :] >= col_start[:, None]) & (col[None, :] < col_start[:, None] + kw)
    dc = jnp.clip(col[None, :] - col[:, None] + NA_KW - 1, 0, 2 * NA_KW - 2)
    rpb_cols = rpb[:, :, dc]
    scale = dh ** -0.5

    def one_row(args):
        r, q_r = args
        r0 = jnp.clip(r - kh // 2, 0, rows - kh)
        k_r = lax.dynamic_slice_in_dim(kg, r0, kh, axis=1)
        v_r = lax.dynamic_slice_in_dim(vg, r0, kh, axis=1)
        dr = r0 + jnp.arange(kh) - r + NA_KH - 1
        bias = rpb_cols[:, dr].transpose(0, 2, 1, 3).astype(jnp.float32)
        sc = jnp.einsum('bqhd,bkwhd->bhqkw', q_r, k_r).astype(jnp.float32) * scale + bias[None]
        sc = jnp.where(col_mask[None, None, :, None, :], sc, NEG_2)
        p = jax.nn.softmax(sc.reshape(b, h, GRID_W, kh * GRID_W), axis=-1).reshape(b, h, GRID_W, kh, GRID_W)
        return jnp.einsum('bhqkw,bkwhd->bqhd', p.astype(v.dtype), v_r)

    out = lax.map(one_row, (jnp.arange(rows), qg))
    return out.transpose(1, 0, 2, 3, 4).reshape(b, s, h, dh)

def _layer_ab(x, ln, w_in, sink, w_out):
    b, s, _ = x.shape
    hn = _rmsnorm(x, ln)
    proj = hn @ w_in
    aq, ak, av, bq, bk, bv, z = jnp.split(proj, AB_SPLITS, axis=-1)
    slopes = _alibi_slopes(A_Q_HEADS + B_HEADS)
    ya, _ = _banded_attention(aq.reshape(b, s, A_Q_HEADS, HEAD_DIM_2),
                              ak.reshape(b, s, A_KV_HEADS, HEAD_DIM_2),
                              av.reshape(b, s, A_KV_HEADS, HEAD_DIM_2),
                              A_HALF_WINDOW, 1, slopes[:A_Q_HEADS], sink)
    yb = _dilated_mixture(bq.reshape(b, s, B_HEADS, HEAD_DIM_2),
                          bk.reshape(b, s, B_HEADS, HEAD_DIM_2),
                          bv.reshape(b, s, B_HEADS, HEAD_DIM_2),
                          slopes[A_Q_HEADS:])
    y = jnp.concatenate([ya.reshape(b, s, A_Q_COLS), yb.reshape(b, s, B_COLS)], axis=-1)
    y = y * jax.nn.silu(z)
    return x + y @ w_out

def _layer_c(x, ln, w_in, rpb, w_out):
    b, s, _ = x.shape
    hn = _rmsnorm(x, ln)
    proj = hn @ w_in
    cq, ck, cv, z = jnp.split(proj, 4, axis=-1)
    y = _neighbourhood_attention(cq.reshape(b, s, C_HEADS, HEAD_DIM_2),
                                 ck.reshape(b, s, C_HEADS, HEAD_DIM_2),
                                 cv.reshape(b, s, C_HEADS, HEAD_DIM_2), rpb)
    y = y.reshape(b, s, C_WIDTH) * jax.nn.silu(z)
    return x + y @ w_out

def second_inputs(seed: int = 0) -> dict:
    key = jax.random.key(seed)
    ks = jax.random.split(key, 11)
    n_even = (DEPTH + 1) // 2
    n_odd = DEPTH // 2
    d = D_MODEL
    f32 = jnp.float32
    x = jax.random.normal(ks[0], (BATCH, SEQ, d), f32)
    ln_ab = 1.0 + 0.02 * jax.random.normal(ks[1], (n_even, d), f32)
    w_in_ab = jax.random.normal(ks[2], (n_even, d, AB_IN_COLS), f32) * d ** -0.5
    sink_a = 0.5 * jax.random.normal(ks[3], (n_even, A_Q_HEADS), f32)
    w_out_ab = jax.random.normal(ks[4], (n_even, AB_WIDTH, d), f32) * AB_WIDTH ** -0.5
    ln_c = 1.0 + 0.02 * jax.random.normal(ks[5], (n_odd, d), f32)
    w_in_c = jax.random.normal(ks[6], (n_odd, d, C_IN_COLS), f32) * d ** -0.5
    rpb_c = 0.1 * jax.random.normal(ks[7], (n_odd, C_HEADS, 2 * NA_KH - 1, 2 * NA_KW - 1), f32)
    w_out_c = jax.random.normal(ks[8], (n_odd, C_WIDTH, d), f32) * C_WIDTH ** -0.5
    ln_f = 1.0 + 0.02 * jax.random.normal(ks[9], (d,), f32)
    return {"x": x, "ln_ab": ln_ab, "w_in_ab": w_in_ab, "sink_a": sink_a, "w_out_ab": w_out_ab,
            "ln_c": ln_c, "w_in_c": w_in_c, "rpb_c": rpb_c, "w_out_c": w_out_c, "ln_f": ln_f}

def second_block(x, ln_ab, w_in_ab, sink_a, w_out_ab, ln_c, w_in_c, rpb_c, w_out_c, ln_f):
    for layer in range(DEPTH):
        i = layer // 2
        if layer % 2 == 0:
            x = _layer_ab(x, ln_ab[i], w_in_ab[i], sink_a[i], w_out_ab[i])
        else:
            x = _layer_c(x, ln_c[i], w_in_c[i], rpb_c[i], w_out_c[i])
    return _rmsnorm(x, ln_f)


def setup_inputs(seed=0):
    out = dict(first_inputs(seed))
    for name, value in second_inputs(seed + 1).items():
        if name != "x":
            out[name + "_2"] = value
    return out


def reference(
    x, p, ln_mix_g, ab_w_in, ab_conv_w, ab_conv_b, ab_w_rgate, ab_b_rgate, ab_w_igate,
    ab_b_igate, ab_lambda, ab_pool_w, ab_pool_scale, ab_w_out, c_w_in, c_cmp_pos_k, c_cmp_w1_k,
    c_cmp_w2_k, c_cmp_pos_v, c_cmp_w1_v, c_cmp_w2_v, c_w_out, ln_mlp_g, mlp_w_up, mlp_w_down,
    ln_ple_g, ple_w_gate, ple_w_proj, ln_final_g, ln_ab_2, w_in_ab_2, sink_a_2, w_out_ab_2,
    ln_c_2, w_in_c_2, rpb_c_2, w_out_c_2, ln_f_2,
):
    x = first_block(
        x, p, ln_mix_g, ab_w_in, ab_conv_w, ab_conv_b, ab_w_rgate, ab_b_rgate, ab_w_igate,
        ab_b_igate, ab_lambda, ab_pool_w, ab_pool_scale, ab_w_out, c_w_in, c_cmp_pos_k,
        c_cmp_w1_k, c_cmp_w2_k, c_cmp_pos_v, c_cmp_w1_v, c_cmp_w2_v, c_w_out, ln_mlp_g,
        mlp_w_up, mlp_w_down, ln_ple_g, ple_w_gate, ple_w_proj, ln_final_g,
    )
    return second_block(
        x, ln_ab_2, w_in_ab_2, sink_a_2, w_out_ab_2, ln_c_2, w_in_c_2, rpb_c_2, w_out_c_2,
        ln_f_2,
    )


_drawn_inputs = setup_inputs


def setup_inputs(seed=0):
    import zlib

    import numpy as np

    out = dict(_drawn_inputs(seed))
    spreads = {}
    factors = {'ab_conv_b': 3.252,
     'ab_b_rgate': 8.0,
     'ab_b_igate': 6.57,
     'c_cmp_pos_k': 8.0,
     'c_cmp_pos_v': 8.0,
     'ln_ple_g': 7.008,
     'ln_ab_2': 7.061,
     'sink_a_2': 8.0,
     'ln_c_2': 8.0,
     'rpb_c_2': 6.201,
     'ln_f_2': 2.854}
    for name, (base, spread) in spreads.items():
        noise = np.random.default_rng([zlib.crc32(name.encode()), seed]).standard_normal(out[name].shape)
        drawn = base * np.exp(spread * noise) if base else spread * noise
        out[name] = __import__('jax').numpy.asarray(drawn.astype(out[name].dtype))
    for name, factor in factors.items():
        out[name] = (out[name] * factor).astype(out[name].dtype)
    return out
```

```python
from contextlib import ExitStack

import numpy as np

import concourse.bass as bass
from concourse import mybir

ALU = mybir.AluOpType
ACT = mybir.ActivationFunctionType
AX_X = mybir.AxisListType.X
F32 = mybir.dt.float32
F32R = mybir.dt.float32r

P = 128
S = 256
TOK = S // P
D = 2048
KT = D // P
NW = 512
GT = 4
NCH = D // NW
HD = 128
NH = 16
QSCALE = float(HD) ** -0.5
RAW, RING = 2, 4
AHEAD = 3
LRU = 1024
LT = LRU // P
PADC = 3
PADP = 16
NCMP = 15
NKV = 4
CL = 32
HID = 512
C_GATES = D + 6 * 512
NB3 = 3
W_C = C_GATES + NB3 * NH

ORDER = [("ab_in", 6), ("ab_out", 4), ("proj0", 1), ("mlp0", 32), ("gate0", 4),
         ("c_in", 10), ("c_tail", 1), ("cmp_k", 2), ("cmp_v", 2), ("c_out", 4), ("proj1", 1),
         ("mlp1", 32), ("gate1", 4),
         ("ab2_in", 13), ("ab2_out", 4), ("c2_in", 16), ("c2_out", 4)]
CHUNK0 = {}
NC = 0
for _name, _n in ORDER:
    CHUNK0[_name] = NC
    NC += _n

ACC0 = {}
_a = 0
for _name, _n in ORDER:
    ACC0[_name] = _a
    _a += 4 if _name.startswith("proj") else 0 if _name.startswith("cmp") else _n

TILE0 = {}
_t = 0
for _name, _n in [("ab_out_none", 0), ("mlp0", 5), ("gate0", 1), ("c_in", 1), ("c_out", 1), ("mlp1", 5),
                  ("gate1", 1), ("ab2_in", 1), ("ab2_out", 1), ("c2_in", 1), ("c2_out", 1)]:
    TILE0[_name] = _t * KT
    _t += _n


def build(nc, A, out):
    ctx = ExitStack()

    def sb(name, shape, dt=F32, stack=None):
        return (stack or ctx).enter_context(nc.sbuf_tensor(name, shape, dt))

    def overlay(*tensors):
        with ExitStack() as stack:
            return [sb(*t, stack=stack) for t in tensors]

    def bank(name):
        return ctx.enter_context(nc.psum_tensor(name, [P, 512], F32))

    def sem(name):
        return ctx.enter_context(nc.semaphore(name))

    raw = sb("raw", [P, RAW, GT, NW])
    w_hi = sb("w_hi", [P, RING, GT, NW], F32R)
    w_lo = sb("w_lo", [P, RING, GT, NW], F32R)
    h = sb("h", [P, TOK, D])
    ident = sb("ident", [P, P])
    gains = sb("gains", [P, 8, KT])
    stat = sb("stat", [P, 3, TOK])
    rstd = sb("rstd", [P, TOK])
    small = sb("small", [P, 8, 2, TOK])
    sinks = sb("sinks", [P, 8])
    bias_c = sb("bias_c", [P, NH, TOK, NCMP])
    valid_c = sb("valid_c", [P, TOK, NCMP])
    mask3 = sb("mask3", [P, S])
    kcmpT = sb("kcmpT", [P, NKV * NCMP])
    vcmp = sb("vcmp", [NCMP, NKV, HD])
    stv = sb("stv", [NCMP, HD])

    z0, xr, xc, gateT, pool_w = overlay(
        ("z0", [P, TOK, 3072]), ("xr", [P, LT, PADC + S]), ("xc", [P, LT, S]), ("gateT", [P, LT, S]),
        ("pool_w", [P, LT, S]))
    _, xT = overlay(("z0_", [P, TOK, 3072]), ("xT", [P, KT, S]))
    uT, pw0, pw1 = overlay(("uT", [P, LT, PADP + S]), ("pw0", [P, LT, PADP + S]), ("pw1", [P, LT - 2, PADP + S]))
    z1, cT, chid, chidT, cw2, posT = overlay(
        ("z1", [P, TOK, W_C]), ("cT", [P, 2, NKV, S]), ("chid", [NKV * NCMP, HID]),
        ("chidT", [P, HID // P, NKV * NCMP]), ("cw2", [P, 2, HID // P, HD]), ("posT", [P, 2, CL]))
    z2, = overlay(("z2", [P, TOK, 6656]))
    z3, = overlay(("z3", [P, TOK, 8192]))
    hidT_hi, hidT_lo, hid, proj = overlay(
        ("hidT_hi", [P, KT, S], F32R), ("hidT_lo", [P, KT, S], F32R), ("hid", [P, TOK, D]), ("proj", [P, TOK, D]))
    pT_hi, pT_lo, pT = overlay(("pT_hi", [P, 2, S], F32R), ("pT_lo", [P, 2, S], F32R), ("pT", [P, 2, S]))
    gfull, = overlay(("gfull", [P, D]))
    sb("region_z", [P, 16384])

    aT_hi, aT_lo = overlay(("aT_hi", [P, KT, S], F32R), ("aT_lo", [P, KT, S], F32R))
    rg, ig, dec, th = overlay(("rg", [P, LT, S]), ("ig", [P, LT, S]), ("dec", [P, LT, S]), ("th", [P, LT, S]))
    blk, blk_hi, blk_lo = overlay(
        ("blk", [P, CL, BW]), ("blk_hi", [P, CL, BW], F32R), ("blk_lo", [P, CL, BW], F32R))
    stq, stk, bias, qkT, prob, prT = overlay(
        ("stq", [P, TOK, 4 * HD]), ("stk", [P, TOK, 4 * HD]), ("bias", [P, 4, TOK, S]), ("qkT", [P, 2, 2 * S]),
        ("prob", [P, 2, TOK, S + 2]), ("prT", [P, 2, TOK, S]))
    sb("region_a", [P, 8192])

    bd = sb("bd", [P, 2, LT, P])
    vecs = sb("vecs", [P, 9, LT])
    soft = sb("soft", [P, 4, LT])
    invcnt = sb("invcnt", [P, 4, PADP])

    acc = [bank(f"acc{t}") for t in range(TOK)]
    tp = [bank(f"tp{t}") for t in range(2)]
    pa = ctx.enter_context(nc.psum_tensor("pa", [P, 4, 512], F32))

    landed = [sem(f"landed{i}") for i in range(RAW)]
    hi_done = sem("hi_done")
    split_done = sem("split_done")
    group_used = sem("group_used")
    acc0_done = sem("acc0_done")
    acc1_done = sem("acc1_done")
    acc_free = [sem(f"acc_free{t}") for t in range(TOK)]
    tp_done = sem("tp_done")
    thi_done = sem("thi_done")
    tlo_done = sem("tlo_done")
    h_done = sem("h_done")
    relu_done = sem("relu_done")
    hid_done = sem("hid_done")
    sig_done = sem("sig_done")
    gp_done = sem("gp_done")
    sq_done = sem("sq_done")
    ms_done = sem("ms_done")
    root_done = sem("root_done")
    rstd_done = sem("rstd_done")
    z_done = sem("z_done")
    const_in = sem("const_in")
    bd_zero = sem("bd_zero")
    bd_in = sem("bd_in")
    dve_chain = sem("dve_chain")
    soft_exp = sem("soft_exp")
    x_hi = sem("x_hi")
    x_lo = sem("x_lo")
    m_tp = sem("m_tp")
    m_ev_act = sem("m_ev_act")
    m_ev_dve = sem("m_ev_dve")
    conv_done = sem("conv_done")
    gates_mm = sem("gates_mm")
    gates_sg = sem("gates_sg")
    decay_done = sem("decay_done")
    lru_dve = sem("lru_dve")
    lru_root = sem("lru_root")
    mix_hi = sem("mix_hi")
    mix_lo = sem("mix_lo")
    pads_zero = sem("pads_zero")
    pool_step = sem("pool_step")
    pool_mm = sem("pool_mm")
    p_in = sem("p_in")
    p_hi = sem("p_hi")
    p_lo = sem("p_lo")
    proj_done = sem("proj_done")
    cmp_in = sem("cmp_in")
    c_tp = sem("c_tp")
    c_ev = sem("c_ev")
    blk_done = sem("blk_done")
    blk_hi_done = sem("blk_hi_done")
    blk_lo_done = sem("blk_lo_done")
    chid_done = sem("chid_done")
    chid_tp = sem("chid_tp")
    chid_ev = sem("chid_ev")
    cmp_mm = sem("cmp_mm")
    cmp_ev = sem("cmp_ev")
    bias_in = sem("bias_in")
    bias_ok = sem("bias_ok")
    staged = sem("staged")
    qk_tp = sem("qk_tp")
    qk_ev = sem("qk_ev")
    s_mm = sem("s_mm")
    sink_in = sem("sink_in")
    max_done = sem("max_done")
    biased = sem("biased")
    neg_done = sem("neg_done")
    exp_done = sem("exp_done")
    pmask = sem("pmask")
    rden_done = sem("rden_done")
    coef_done = sem("coef_done")
    p_tp = sem("p_tp")
    p_ev = sem("p_ev")
    pv_mm = sem("pv_mm")
    y_done = sem("y_done")
    g_in = sem("g_in")
    fin_done = sem("fin_done")
    rpb_out = sem("rpb_out")
    out_done = sem("out_done")

    wstream = A["wstream"]
    units_before = {"attn1": 0, "attn2a": 48, "attn2b": 56, "attn3": 64}
    rounds_before = {"attn1": 0, "attn2a": 4, "attn2b": 6, "attn3": 8}


    def split_act(act, C, n):
        act.wait_ge(landed[n % RAW], (C * 2 + n // RAW + 1) * 16)
        if not isinstance(C, int) or C * GT + n >= RING:
            act.wait_ge(group_used, C * GT + (n - RING + 1))
        act.activation(w_hi[:, n % RING], raw[:, n % RAW], ACT.Copy).then_inc(hi_done, 1)

    def split_dve(dve, C, n):
        dve.wait_ge(hi_done, C * GT + (n + 1))
        dve.tensor_tensor(w_lo[:, n % RING], raw[:, n % RAW], w_hi[:, n % RING].bitcast(F32),
                          ALU.subtract).then_inc(split_done, 1)


    def pe_group(pe, C, A0, n, lhs, tiles=None, then=None, width=NW):
        hi, lo = lhs
        pe.wait_ge(split_done, C * GT + (n + 1))
        for t in range(TOK):
            if n == 0 and not (isinstance(A0, int) and A0 == 0):
                pe.wait_ge(acc_free[t], A0)
            for i in range(GT):
                kt = GT * n + i
                if tiles is not None and t == 0:
                    pe.wait_ge(tlo_done, tiles + (kt + 1))
                for a, w in ((hi, w_hi), (hi, w_lo), (lo, w_hi)):
                    mm = pe.matmul(acc[t][:, 0:width], a[:, kt, t * P:(t + 1) * P], w[:, n, i, 0:width],
                                   start=(kt == 0 and a is hi and w is w_hi),
                                   stop=(kt == KT - 1 and a is lo))
                if t == 0 and then is not None:
                    then(i)
            if t == 0 and n == GT - 1:
                mm.then_inc(acc0_done, 1)
        mm.then_inc(group_used, 1)

    def pe_chunk(pe, C, A0, lhs, width=NW):
        for n in range(GT):
            pe_group(pe, C, A0, n, lhs, width=width)

    def pe_tile(pe, T0, kt, src, ready):
        if ready is not None:
            ready(kt)
        if not (isinstance(T0, int) and T0 + kt < 2):
            pe.wait_ge(tlo_done, T0 + (kt - 1))
        for t in range(TOK):
            mm = pe.transpose(tp[kt % 2][:, t * P:(t + 1) * P], src[:, t, kt * P:(kt + 1) * P], ident[:, :])
        mm.then_inc(tp_done, 1)

    def pe_first(pe, C, A0, T0, lhs, src, ready):
        for kt in range(GT):
            pe_tile(pe, T0, kt, src, ready)
        for n in range(GT):
            def then(i, n=n):
                if n < GT - 1:
                    pe_tile(pe, T0, GT * (n + 1) + i, src, ready)
            pe_group(pe, C, A0, n, lhs, tiles=T0, then=then)


    def act_tiles(act, T0, hi, gain):
        for kt in range(KT):
            act.wait_ge(tp_done, T0 + (kt + 1))
            act.activation(hi[:, kt], tp[kt % 2][:, 0:S], ACT.Copy,
                           scale=1.0 if gain is None else gains[:, gain, kt:kt + 1]).then_inc(thi_done, 1)

    def dve_tiles(dve, T0, hi, lo, gain):
        for kt in range(KT):
            dve.wait_ge(thi_done, T0 + (kt + 1))
            dve.scalar_tensor_tensor(
                out=lo[:, kt], in0=tp[kt % 2][:, 0:S], scalar=1.0 if gain is None else gains[:, gain, kt:kt + 1],
                in1=hi[:, kt].bitcast(F32), op0=ALU.mult, op1=ALU.subtract).then_inc(tlo_done, 1)


    def dve_means(dve, m, eps):
        dve.wait_ge(sq_done, TOK * (m + 1))
        dve.tensor_scalar(stat[:, 1], stat[:, 0], 1.0 / D, eps, ALU.mult, ALU.add).then_inc(ms_done, 1)

    def act_root(act, m):
        act.wait_ge(ms_done, m + 1)
        act.activation(stat[:, 2], stat[:, 1], ACT.Sqrt).then_inc(root_done, 1)

    def dve_rstd(dve, m):
        dve.wait_ge(root_done, m + 1)
        dve.reciprocal(rstd[:, :], stat[:, 2]).then_inc(rstd_done, 1)


    def act_project(act, C, A0, m, dst, func=ACT.Copy, width=NW):
        for t in range(TOK):
            if t == 0:
                act.wait_ge(acc0_done, A0 + 1)
                act.wait_ge(rstd_done, m + 1)
            else:
                act.wait_ge(group_used, C * GT + GT)
            act.activation(dst(t), acc[t][:, 0:width], func, scale=rstd[:, t:t + 1]).then_inc(acc_free[t], 1)

    def dve_residual(dve, C, A0, col):
        for t in range(TOK):
            if t == 0:
                dve.wait_ge(acc0_done, A0 + 1)
            else:
                dve.wait_ge(group_used, C * GT + GT)
            part = h[:, t, bass.ds(col, NW)]
            dve.tensor_tensor(part, acc[t][:, :], part, ALU.add).then_inc(acc_free[t], 1)


    class Attention:
        def __init__(self, name, rounds, units, z, q_col, k_parts, v_col, unit0, cmp0, stage0, round0,
                     silu_col=None, y_col=None, sink=False, masked=False, table=None):
            self.name, self.rounds, self.units, self.z = name, rounds, units, z
            self.q_col, self.k_parts, self.v_col = q_col, k_parts, v_col
            self.unit0, self.cmp0, self.stage0, self.round0 = unit0, cmp0, stage0, round0
            self.silu_col, self.y_col, self.sink, self.masked, self.table = silu_col, y_col, sink, masked, table
            self.n = len(units)
            self.full = [u[0] == "full" for u in units]
            self.stages = 1 + len(k_parts) + (name == "attn1")

        def U(self, i, u):
            return i * self.n + (self.unit0 + u)

        def M(self, i, u):
            n = u - sum(self.full[0:u])
            return i * (self.n - sum(self.full)) + (self.cmp0 + n)

    units1 = []
    for hh in range(4):
        units1 += [("cmp", hh, None, None, 0), ("full", hh, 0, (D + 3 * 512, HD), 1), ("full", hh, 1, (D + 5 * 512, HD), 2)]
    attn1 = Attention("attn1", NKV, units1, z1, 0, [(D + 2 * 512, HD, HD), (D + 4 * 512, HD, HD)], None,
                      unit0=0, cmp0=0, stage0=0, round0=0, table=A["bias1"])
    attn2a = Attention("attn2a", 2, [("full", hh, 0, (1280, HD), None) for hh in range(4)], z2, 0, [(1024, HD, HD)], None,
                       unit0=48, cmp0=16, stage0=16, round0=4, silu_col=4608, y_col=0, sink=True,
                       table=A["bias2"])
    attn2b = Attention("attn2b", 2, [("full", hh, hh, (3584 + hh * HD, 512), None) for hh in range(4)], z2, 1536,
                       [(2560, 512, 512)], None, unit0=56, cmp0=16, stage0=20, round0=6, silu_col=5632,
                       y_col=1024, table=A["bias2"])
    attn3 = Attention("attn3", 4, [("full", hh, hh, (4096 + hh * HD, 512), None) for hh in range(4)], z3, 0,
                      [(2048, 512, 512)], None, unit0=64, cmp0=16, stage0=24, round0=8, silu_col=6144,
                      y_col=0, masked=True, table=A["bias3"])
    MASKED0 = 0

    def keys(at, u):
        return S if at.full[u] else NCMP

    def some(eng, s, value, least=1):
        if not isinstance(value, int) or value >= least:
            eng.wait_ge(s, value)

    def pool_round(pool, at, i, first):
        some(pool, max_done, at.U(i, 0))
        row = i if at.name != "attn2b" else i + 2
        pool.dma_start(bias[:, :, :, :].rearrange("p a t k -> p (a t k)"),
                       at.table[bass.ds(row, 1)].rearrange("a p n -> (a p) n")).then_inc(bias_in, 16)
        some(pool, qk_tp, at.U(i, 0))
        pool.tensor_copy(stq[:, :, :], at.z[:, :, bass.ds(i * 512 + at.q_col, 512)]).then_inc(staged, 1)
        col = 0
        for k_col, per, width in at.k_parts:
            pool.tensor_copy(stk[:, :, col:col + width], at.z[:, :, bass.ds(i * per + k_col, width)]).then_inc(staged, 1)
            col += width
        if at.name == "attn1":
            some(pool, pv_mm, at.U(i, 0))
            pool.tensor_copy(stv[:, :], vcmp[:, bass.ds(i, 1), :].rearrange("n a d -> n (a d)")).then_inc(staged, 1)
        if at.masked:
            pool.wait_ge(bias_in, i * 16 + (at.round0 + 1) * 16)
            part = bias[:, :, :, :].rearrange("p a t k -> p (a t) k")
            pool.tensor_tensor(part, part, mask3[:, :].unsqueeze(1).broadcast_to([P, 8, S]), ALU.add)\
                .then_inc(bias_ok, 1)

    def pe_round(pe, at, i):
        for s in range(at.n + 3):
            if s < at.n:
                u, r = s, s % 2
                pe.wait_ge(staged, i * at.stages + (at.stage0 + at.stages))
                some(pe, qk_ev, at.U(i, u - 1))
                hh, kk = at.units[u][1], at.units[u][2]
                for t in range(TOK):
                    mm = pe.transpose(tp[r][:, t * P:(t + 1) * P], stq[:, t, hh * HD:(hh + 1) * HD], ident[:, :])
                if kk is not None:
                    for t in range(TOK):
                        mm = pe.transpose(tp[r][:, S + t * P:S + (t + 1) * P], stk[:, t, kk * HD:(kk + 1) * HD],
                                          ident[:, :])
                mm.then_inc(qk_tp, 1)
            if 0 <= s - 1 < at.n:
                u, r = s - 1, (s - 1) % 2
                pe.wait_ge(qk_ev, at.U(i, u + 1))
                some(pe, max_done, at.U(i, u - 1))
                for t in range(TOK):
                    rhs = qkT[:, r, S:2 * S] if at.full[u] else kcmpT[:, bass.ds(i * NCMP, NCMP)]
                    mm = pe.matmul(pa[:, r, t * S:t * S + keys(at, u)], qkT[:, r, t * P:(t + 1) * P], rhs,
                                   start=True, stop=True)
                mm.then_inc(s_mm, 1)
            if 0 <= s - 2 < at.n:
                u, r = s - 2, (s - 2) % 2
                if at.full[u]:
                    pe.wait_ge(exp_done, at.U(i, u + 1))
                else:
                    pe.wait_ge(pmask, at.M(i, u + 1))
                some(pe, p_ev, at.U(i, u - 1))
                for t in range(TOK):
                    if at.full[u]:
                        for kb in range(S // P):
                            mm = pe.transpose(pa[:, 2 + r, kb * S + t * P:kb * S + (t + 1) * P],
                                              prob[:, r, t, kb * P:(kb + 1) * P], ident[:, :])
                    else:
                        mm = pe.transpose(pa[0:NCMP, 2 + r, t * P:(t + 1) * P], prob[:, r, t, 0:NCMP], ident[:, :])
                mm.then_inc(p_tp, 1)
            if 0 <= s - 3 < at.n:
                u, r = s - 3, (s - 3) % 2
                pe.wait_ge(p_ev, at.U(i, u + 1))
                some(pe, y_done, at.U(i, u - 1))
                for t in range(TOK):
                    if at.full[u]:
                        c0, per = at.units[u][3]
                        for kb in range(S // P):
                            mm = pe.matmul(acc[r][:, t * P:(t + 1) * P], prT[:, r, kb, t * P:(t + 1) * P],
                                           at.z[:, kb, bass.ds(i * per + c0, HD)],
                                           start=(kb == 0), stop=(kb == S // P - 1))
                    else:
                        mm = pe.matmul(acc[r][:, t * P:(t + 1) * P], prT[0:NCMP, r, 0, t * P:(t + 1) * P],
                                       stv[:, :], start=True, stop=True)
                mm.then_inc(pv_mm, 1)

    def act_round(act, at, i):
        for s in range(at.n + 2):
            if 0 <= s - 1 < at.n:
                u, r = s - 1, (s - 1) % 2
                act.wait_ge(neg_done, at.U(i, u + 1))
                some(act, rden_done, at.U(i, u - 1))
                w = keys(at, u) + (1 if at.sink else 0)
                for t in range(TOK):
                    e = act.activation(prob[:, r, t, 0:w], prob[:, r, t, 0:w], ACT.Exp, bias=small[:, 1, r, t:t + 1],
                                       accum_out=small[:, 2, r, t:t + 1])
                e.then_inc(exp_done, 1)
            if 0 <= s - 2 < at.n:
                u, r = s - 2, (s - 2) % 2
                act.wait_ge(p_tp, at.U(i, u + 1))
                some(act, pv_mm, at.U(i, u - 1))
                if at.full[u]:
                    act.activation(prT[:, r].rearrange("p a b -> p (a b)"), pa[:, 2 + r, :], ACT.Copy).then_inc(p_ev, 1)
                else:
                    act.activation(prT[0:NCMP, r, 0, :], pa[0:NCMP, 2 + r, 0:S], ACT.Copy).then_inc(p_ev, 1)

    def dve_round(dve, at, i):
        for s in range(at.n + 3):
            if s < at.n:
                u, r = s, s % 2
                dve.wait_ge(qk_tp, at.U(i, u + 1))
                some(dve, s_mm, at.U(i, u - 1))
                if at.full[u]:
                    dve.tensor_copy(qkT[:, r, S:2 * S], tp[r][:, S:2 * S])
                dve.tensor_scalar(qkT[:, r, 0:S], tp[r][:, 0:S], QSCALE, None, ALU.mult).then_inc(qk_ev, 1)
            if 0 <= s - 1 < at.n:
                u, r = s - 1, (s - 1) % 2
                hh = at.units[u][1]
                w = keys(at, u)
                dve.wait_ge(s_mm, at.U(i, u + 1))
                some(dve, p_tp, at.U(i, u - 1))
                if at.masked:
                    dve.wait_ge(bias_ok, i + (MASKED0 + 1))
                else:
                    dve.wait_ge(bias_in, i * 16 + (at.round0 + 1) * 16)
                sink = sinks[:, bass.ds(i * 4 + hh, 1)] if at.sink else None
                if at.sink:
                    for t in range(TOK):
                        dve.tensor_copy(prob[:, r, t, S:S + 1], sink)
                if at.full[u]:
                    dve.memset(small[:, 5, r], 0.0)
                    for t in range(TOK):
                        m = dve.tensor_tensor_reduce(prob[:, r, t, 0:w], pa[:, r, t * S:t * S + w], bias[:, hh, t, :],
                                                     1.0, -3.0e38, ALU.add, ALU.max, small[:, 0, r, t:t + 1])
                    m.then_inc(max_done, 1)
                else:
                    dve.tensor_tensor(prob[:, r, :, 0:w], pa[:, r, :].rearrange("p (t k) -> p t k", t=TOK)[:, :, 0:w],
                                      bias_c[:, bass.ds(i * 4 + hh, 1), :, :].rearrange("p a t n -> p (a t) n"),
                                      ALU.add).then_inc(biased, 1)
                    dve.wait_ge(biased, at.M(i, u + 1))
                    dve.tensor_reduce(small[:, 0, r], prob[:, r, :, 0:w], AX_X, ALU.max).then_inc(max_done, 1)
                dve.wait_ge(max_done, at.U(i, u + 1))
                some(dve, exp_done, at.U(i, u - 1))
                if at.sink:
                    dve.tensor_scalar(small[:, 1, r], small[:, 0, r], sink, -1.0, ALU.max, ALU.mult).then_inc(neg_done, 1)
                else:
                    dve.tensor_scalar(small[:, 1, r], small[:, 0, r], -1.0, None, ALU.mult).then_inc(neg_done, 1)
            if 0 <= s - 2 < at.n:
                u, r = s - 2, (s - 2) % 2
                dve.wait_ge(exp_done, at.U(i, u + 1))
                if not at.full[u]:
                    dve.tensor_tensor(prob[:, r, :, 0:NCMP], prob[:, r, :, 0:NCMP], valid_c[:, :, :], ALU.mult)\
                        .then_inc(pmask, 1)
                some(dve, y_done, at.U(i, u - 1))
                dve.reciprocal(small[:, 3, r], small[:, 2, r]).then_inc(rden_done, 1)
                if at.name == "attn1":
                    gate = z1[:, :, bass.ds(i * 4 + (C_GATES + at.units[u][4] * NH + at.units[u][1]), 1)]
                    dve.wait_ge(rden_done, at.U(i, u + 1))
                    dve.tensor_tensor(small[:, 4, r], small[:, 3, r], gate.rearrange("p t a -> p (t a)"), ALU.mult)\
                        .then_inc(coef_done, 1)
            if 0 <= s - 3 < at.n:
                u, r = s - 3, (s - 3) % 2
                hh = at.units[u][1]
                dve.wait_ge(pv_mm, at.U(i, u + 1))
                if at.name == "attn1":
                    dve.wait_ge(coef_done, at.U(i, u + 1))
                    if at.full[u]:
                        dve.wait_ge(y_done, at.U(i, u))
                else:
                    dve.wait_ge(rden_done, at.U(i, u + 1))
                for t in range(TOK):
                    y = at.z[:, t, bass.ds(i * 512 + ((at.y_col or 0) + hh * HD), HD)]
                    o = acc[r][:, t * P:(t + 1) * P]
                    if at.name != "attn1":
                        gate = at.z[:, t, bass.ds(i * 512 + (at.silu_col + hh * HD), HD)]
                        d = dve.scalar_tensor_tensor(out=y, in0=o, scalar=small[:, 3, r, t:t + 1], in1=gate,
                                                     op0=ALU.mult, op1=ALU.mult)
                    elif at.full[u]:
                        d = dve.scalar_tensor_tensor(out=y, in0=o, scalar=small[:, 4, r, t:t + 1], in1=y,
                                                     op0=ALU.mult, op1=ALU.add)
                    else:
                        d = dve.tensor_scalar(y, o, small[:, 4, r, t:t + 1], None, ALU.mult)
                d.then_inc(y_done, 1)


    def act_product(act, name, ends, first=None, last=False):
        C0, A0 = CHUNK0[name], ACC0[name]
        split_act(act, C0, AHEAD)
        if first:
            first()
        for n in range(AHEAD + 1, AHEAD + GT):
            split_act(act, C0, n)
        c = 0
        for count, end in ends:
            if c == 0:
                if end:
                    end(C0, A0, 0)
                c, count = 1, count - 1
            if last and c + count == dict(ORDER)[name]:
                count -= 1
            if count:
                with act.Fori(c, c + count) as j:
                    for n in range(AHEAD, AHEAD + GT):
                        split_act(act, j + C0, n)
                    if end:
                        end(j + C0, j + A0, j)
            c += count
        if last:
            split_act(act, C0 + c, AHEAD)
            if ends[-1][1]:
                ends[-1][1](C0 + c, A0 + c, c)

    def dve_product(dve, name, end=None, first=None, last=False, after=None):
        C0, A0, n_chunks = CHUNK0[name], ACC0[name], dict(ORDER)[name]
        split_dve(dve, C0, AHEAD)
        if first:
            first()
        for n in range(AHEAD + 1, AHEAD + GT):
            split_dve(dve, C0, n)
        if after:
            after()
        if end:
            end(C0, A0, 0)
        stop = n_chunks - (1 if last else 0)
        if stop > 1:
            with dve.Fori(1, stop) as j:
                for n in range(AHEAD, AHEAD + GT):
                    split_dve(dve, j + C0, n)
                if end:
                    end(j + C0, j + A0, j)
        if last:
            split_dve(dve, C0 + stop, AHEAD)
            end(C0 + stop, A0 + stop, stop)

    def pe_product(pe, name, lhs, src=None, ready=None, x_ready=None):
        C0, A0, n_chunks = CHUNK0[name], ACC0[name], dict(ORDER)[name]
        if src is not None:
            pe_first(pe, C0, A0, TILE0[name], lhs, src, ready)
        else:
            x_ready()
            pe_chunk(pe, C0, A0, lhs)
        if n_chunks > 1:
            with pe.Fori(1, n_chunks) as j:
                pe_chunk(pe, j + C0, j + A0, lhs)

    aT, hT = (aT_hi, aT_lo), (hidT_hi, hidT_lo)
    MLP_N = D * 4 // D

    def freed(eng, name, n, t=None):
        for tt in (range(TOK) if t is None else [t]):
            eng.wait_ge(acc_free[tt], ACC0[name] + n)

    def after_residual(pe, name, skip=0):
        def ready(kt):
            if kt % GT == 0:
                freed(pe, name, skip + kt // GT + 1)
        return ready

    def after_gate(pe, layer):
        def ready(kt):
            if kt % GT == 0:
                pe.wait_ge(h_done, layer * 8 + 2 * (kt // GT + 1))
        return ready

    def once(wait):
        def ready(kt):
            if kt == 0:
                wait()
        return ready

    def pe_mlp(pe, l, prev):
        name = f"mlp{l}"
        C0, A0, T0 = CHUNK0[name], ACC0[name], TILE0[name]
        ready = after_residual(pe, prev)
        for kt in range(KT):
            pe_tile(pe, T0, kt, h, ready)
        pe.wait_ge(tlo_done, T0 + KT)
        with pe.Fori(0, MLP_N) as j:
            with pe.Fori(0, NCH) as c:
                pe_chunk(pe, c + j * 8 + C0, c + j * 8 + A0, aT)

            def ready(kt):
                if kt % GT == 0:
                    pe.wait_ge(hid_done, j * 8 + (l * 32 + 2 * (kt // GT + 1)))
            pe_first(pe, j * 8 + (C0 + NCH), j * 8 + (A0 + NCH), j * KT + (T0 + KT), hT, hid, ready)
            with pe.Fori(1, NCH) as c:
                pe_chunk(pe, c + j * 8 + (C0 + NCH), c + j * 8 + (A0 + NCH), hT)

    def act_mlp(act, l, m, gain, squares):
        name = f"mlp{l}"
        C0, A0, T0 = CHUNK0[name], ACC0[name], TILE0[name]
        act_tiles(act, T0, aT_hi, gain)
        squares()
        act_root(act, m)
        with act.Fori(0, MLP_N) as j:
            with act.Fori(0, NCH) as c:
                for n in range(AHEAD, AHEAD + GT):
                    split_act(act, c + j * 8 + C0, n)
                act_project(act, c + j * 8 + C0, c + j * 8 + A0, m, lambda t: hid[:, t, bass.ds(c * NW, NW)], ACT.Relu)
            split_act(act, j * 8 + (C0 + NCH), AHEAD)
            act_tiles(act, j * KT + (T0 + KT), hidT_hi, None)
            for n in range(AHEAD + 1, AHEAD + GT):
                split_act(act, j * 8 + (C0 + NCH), n)
            with act.Fori(1, NCH) as c:
                for n in range(AHEAD, AHEAD + GT):
                    split_act(act, c + j * 8 + (C0 + NCH), n)

    def pool_mlp(pool, l):
        name = f"mlp{l}"
        A0 = ACC0[name]
        with pool.Fori(0, MLP_N) as j:
            with pool.Fori(0, NCH) as c:
                for t in range(TOK):
                    pool.wait_ge(acc_free[t], c + j * 8 + (A0 + 1))
                    part = hid[:, t, bass.ds(c * NW, NW)]
                    pool.tensor_tensor(part, part, part, ALU.mult).then_inc(hid_done, 1)

    def dve_mlp(dve, l, m, gain):
        name = f"mlp{l}"
        C0, A0, T0 = CHUNK0[name], ACC0[name], TILE0[name]
        dve_tiles(dve, T0, aT_hi, aT_lo, gain)
        dve_means(dve, m, 1e-6)
        dve_rstd(dve, m)
        with dve.Fori(0, MLP_N) as j:
            with dve.Fori(0, NCH) as c:
                for n in range(AHEAD, AHEAD + GT):
                    split_dve(dve, c + j * 8 + C0, n)
            split_dve(dve, j * 8 + (C0 + NCH), AHEAD)
            dve_tiles(dve, j * KT + (T0 + KT), hidT_hi, hidT_lo, None)
            for n in range(AHEAD + 1, AHEAD + GT):
                split_dve(dve, j * 8 + (C0 + NCH), n)
            dve_residual(dve, j * 8 + (C0 + NCH), j * 8 + (A0 + NCH), 0)
            with dve.Fori(1, NCH) as c:
                for n in range(AHEAD, AHEAD + GT):
                    split_dve(dve, c + j * 8 + (C0 + NCH), n)
                dve_residual(dve, c + j * 8 + (C0 + NCH), c + j * 8 + (A0 + NCH), c * NW)

    def act_proj(act, l, z_dead):
        C0, A0 = CHUNK0[f"proj{l}"], ACC0[f"proj{l}"]
        act.wait_ge(p_in, 16 * (l + 1))
        act.activation(pT_hi[:, :, :], pT[:, :, :], ACT.Copy).then_inc(p_hi, 1)
        for n in range(NCH):
            split_act(act, C0, AHEAD + n)
            for t in range(TOK):
                if t == 0:
                    act.wait_ge(acc0_done, A0 + n + 1)
                else:
                    act.wait_ge(group_used, C0 * GT + n + 1)
                act.activation(proj[:, t, n * NW:(n + 1) * NW], acc[t][:, :], ACT.Copy).then_inc(acc_free[t], 1)

    def dve_proj(dve, l):
        dve.wait_ge(p_hi, l + 1)
        dve.tensor_tensor(pT_lo[:, :, :], pT[:, :, :], pT_hi[:, :, :].bitcast(F32), ALU.subtract).then_inc(p_lo, 1)
        for n in range(NCH):
            split_dve(dve, CHUNK0[f"proj{l}"], AHEAD + n)

    def pe_proj(pe, l):
        C0, A0 = CHUNK0[f"proj{l}"], ACC0[f"proj{l}"]
        pe.wait_ge(p_lo, l + 1)
        for n in range(NCH):
            pe.wait_ge(split_done, C0 * GT + n + 1)
            for t in range(TOK):
                pe.wait_ge(acc_free[t], A0 + n)
                for kt in range(2):
                    for a, w in ((pT_hi, w_hi), (pT_hi, w_lo), (pT_lo, w_hi)):
                        mm = pe.matmul(acc[t][:, :], a[:, kt, t * P:(t + 1) * P], w[:, n, kt, :],
                                       start=(kt == 0 and a is pT_hi and w is w_hi), stop=(kt == 1 and a is pT_lo))
                if t == 0:
                    mm.then_inc(acc0_done, 1)
            mm.then_inc(group_used, 1)

    def act_gate_end(act, l, m):
        def end(C, A_, c):
            if not isinstance(c, int) or c > 0:
                act.wait_ge(h_done, c * 2 + l * 8)
            act_project(act, C, A_, m, lambda t: hid[:, t, 0:NW], ACT.Sigmoid)
        return end

    def pool_gate(pool, l):
        A0 = ACC0[f"gate{l}"]
        with pool.Fori(0, NCH) as c:
            for t in range(TOK):
                pool.wait_ge(acc_free[t], c + (A0 + 1))
                pool.tensor_tensor(hid[:, t, 0:NW], hid[:, t, 0:NW], proj[:, t, bass.ds(c * NW, NW)], ALU.mult)\
                    .then_inc(gp_done, 1)

    def dve_gate_end(dve, l):
        def end(C, A_, c):
            for t in range(TOK):
                dve.wait_ge(gp_done, c * 2 + (l * 8 + t + 1))
                part = h[:, t, bass.ds(c * NW, NW)] if not isinstance(c, int) else h[:, t, c * NW:(c + 1) * NW]
                dve.tensor_tensor(part, part, hid[:, t, 0:NW], ALU.add).then_inc(h_done, 1)
        return end

    def residual_end(dve):
        return lambda C, A_, c: dve_residual(dve, C, A_, c * NW)

    def put(z, base=0):
        return lambda c: (lambda t: z[:, t, bass.ds(c * NW + base, NW)])

    def project_end(act, m, z, func=ACT.Copy):
        return lambda C, A_, c: act_project(act, C, A_, m, put(z)(c), func)

    def act_norm(act, m, wait):
        wait()
        if m > 0:
            act.wait_ge(ms_done, m)
        for t in range(TOK):
            if t > 0:
                act.wait_ge(sq_done, TOK * m + t)
            act.activation(pa[:, :, :].rearrange("p a b -> p (a b)"), h[:, t, :], ACT.Square,
                           accum_out=stat[:, 0, t:t + 1]).then_inc(sq_done, 1)

    block = ctx.enter_context(nc.Block())

    @block.sync
    def _(sp):
        for g in range(RAW):
            sp.dma_start(raw[:, g].rearrange("p a b -> p (a b)"), wstream[g]).then_inc(landed[g], 16)
        with sp.Fori(1, NC * GT // RAW) as i:
            for g in range(RAW):
                sp.wait_ge(split_done, i * RAW + (g + 1 - RAW))
                sp.dma_start(raw[:, g].rearrange("p a b -> p (a b)"),
                             wstream[bass.ds(i * RAW + g, 1)].rearrange("g p n -> (g p) n")).then_inc(landed[g], 16)
        sp.wait_ge(fin_done, 2)
        sp.dma_start(out.rearrange("b (t p) d -> p (b t) d", p=P), h[:, :, :]).then_inc(out_done, 16)
        sp.wait_ge(out_done, 16)
        sp.wait_ge(rpb_out, 16 * RPB_DMAS)

    @block.gpsimd
    def _(pool):
        pool.memset(bd[:, :, :, :], 0.0).then_inc(bd_zero, 1)
        pool.wait_ge(bd_zero, 1)
        for n, w in enumerate((A["w_r"], A["w_i"])):
            for half in range(2):
                pool.dma_start(bd[half * 64:half * 64 + 64, n, :, half * 64:half * 64 + 64],
                               w.rearrange("(j a) i o -> a i j o", a=2)[half]).then_inc(bd_in, 16)
        b3 = A["bias3"]
        for hh in range(NH):
            for r in range(4):
                t, half = r // 2, r % 2
                src = bass.AP(tensor=A["rpb"].tensor, offset=(hh * 15 + 7 - r) * 64 * 128 + 63,
                              ap=[[127, 64], [64 * 128, 4], [1, 64]])
                dst = b3[hh // 4, half * 64:half * 64 + 64, bass.ds((hh % 4) * 512 + t * S, S)]\
                    .rearrange("p (k c) -> p k c", k=4)
                pool.dma_start(dst, src).then_inc(rpb_out, 16)
        pool.wait_ge(m_tp, 17)
        pool.memset(uT[:, :, 0:PADP], 0.0).then_inc(pads_zero, 1)
        pool.wait_ge(m_ev_act, 12)
        pool.wait_ge(m_ev_dve, 12)
        pool.wait_ge(pads_zero, 1)
        N = PADP + S
        pool.tensor_tensor(pw0[:, :, 1:N], uT[:, :, 1:N], uT[:, :, 0:N - 1], ALU.add).then_inc(pool_step, 1)
        pool.wait_ge(pool_step, 1)
        pool.tensor_tensor(pw1[:, :, 3:N], pw0[:, 2:8, 3:N], pw0[:, 2:8, 1:N - 2], ALU.add).then_inc(pool_step, 1)
        pool.wait_ge(pool_step, 2)
        pool.tensor_tensor(pw0[:, 4:8, 7:N], pw1[:, 2:6, 7:N], pw1[:, 2:6, 3:N - 4], ALU.add).then_inc(pool_step, 1)
        pool.wait_ge(pool_step, 3)
        pool.tensor_tensor(pw1[:, 4:6, 15:N], pw0[:, 6:8, 15:N], pw0[:, 6:8, 7:N - 8], ALU.add).then_inc(pool_step, 1)
        pool.wait_ge(pool_step, 4)
        for g, s in enumerate((pw0[:, 0:2], pw1[:, 0:2], pw0[:, 4:6], pw1[:, 4:6])):
            win = 2 << g
            pool.tensor_tensor(s[:, :, PADP:2 * PADP], s[:, :, PADP:2 * PADP],
                               invcnt[:, g, :].unsqueeze(1).broadcast_to([P, 2, PADP]), ALU.mult).then_inc(pool_step, 1)
            pool.tensor_scalar(s[:, :, 2 * PADP:], s[:, :, 2 * PADP:], 1.0 / win, None, ALU.mult).then_inc(pool_step, 1)
            pool.wait_ge(pool_step, 4 + 3 * g + 2)
            pool.tensor_tensor(uT[:, 2 * g:2 * g + 2, PADP:], s[:, :, PADP:], uT[:, 2 * g:2 * g + 2, PADP:],
                               ALU.subtract).then_inc(pool_step, 1)
        pool.wait_ge(mix_lo, 9)
        pool.wait_ge(pool_mm, 8)
        pool.dma_start(pT[:, :, :], A["pT"][0].rearrange("(k p) s -> p k s", p=P)).then_inc(p_in, 16)
        pool_mlp(pool, 0)
        pool_gate(pool, 0)
        freed(pool, "c_in", 1)
        pool.dma_start(cw2[:, 0], A["w2_k"].rearrange("(f p) d -> p f d", p=P)).then_inc(cmp_in, 16)
        pool.dma_start(cw2[:, 1], A["w2_v"].rearrange("(f p) d -> p f d", p=P)).then_inc(cmp_in, 16)
        pool.dma_start(posT[:, :, :], A["posT"].rearrange("a d l -> d a l")).then_inc(cmp_in, 16)
        pool.wait_ge(cmp_in, 48)
        freed(pool, "c_tail", 1)
        pool.memset(blk[:, :, NKV * NCMP:], 0.0).then_inc(blk_done, 1)
        for kv in range(2):
            pool.wait_ge(c_ev, kv * 4 + 4)
            if kv == 1:
                pool.wait_ge(blk_lo_done, 1)
            for g in range(NKV):
                v = cT[:, kv, g, :].rearrange("p (m j) -> p j m", j=16)
                for a in range(2):
                    b = pool.tensor_tensor(
                        blk[:, 16 * a:16 * a + 16, g * NCMP:(g + 1) * NCMP], v[:, :, a:a + NCMP],
                        posT[:, kv, 16 * a:16 * a + 16].unsqueeze(2).broadcast_to([P, 16, NCMP]), ALU.add)
            b.then_inc(blk_done, 1)
        pool.wait_ge(blk_lo_done, 2)
        pool.wait_ge(group_used, (CHUNK0["cmp_v"] + 2) * GT)
        pool.wait_ge(cmp_ev, 2)
        pool_round(pool, attn1, 0, True)
        with pool.Fori(1, attn1.rounds) as i:
            pool_round(pool, attn1, i, False)
        pool.wait_ge(tlo_done, TILE0["c_out"] + KT)
        pool.dma_start(pT[:, :, :], A["pT"][1].rearrange("(k p) s -> p k s", p=P)).then_inc(p_in, 16)
        pool_mlp(pool, 1)
        pool_gate(pool, 1)
        pool.dma_start(gfull[:, :], A["g1"]).then_inc(g_in, 16)
        freed(pool, "ab2_in", 13)
        with pool.Fori(0, attn2a.rounds) as i:
            pool_round(pool, attn2a, i, True)
        with pool.Fori(0, attn2b.rounds) as i:
            pool_round(pool, attn2b, i, True)
        freed(pool, "c2_in", 16)
        pool.wait_ge(rpb_out, 16 * RPB_DMAS)
        with pool.Fori(0, attn3.rounds) as i:
            pool_round(pool, attn3, i, True)
        pool.wait_ge(tlo_done, TILE0["c2_out"] + KT)
        pool.dma_start(gfull[:, :], A["g2"]).then_inc(g_in, 16)

    @block.scalar
    def _(act):
        loads = [(ident[:, :], A["ident"]), (xT[:, :, :], A["xT"].rearrange("(k p) s -> p k s", p=P)),
                 (gains[:, :, :], A["gains"]), (h[:, :, :], A["x"].rearrange("b (t p) d -> p (b t) d", p=P)),
                 (vecs[:, :, :], A["vecs"]), (invcnt[:, :, :], A["invcnt"]), (pool_w[:, :, :], A["pool_w"]),
                 (sinks[:, :], A["sinks"]), (bias_c[:, :, :, :], A["bias_c"]), (valid_c[:, :, :], A["valid_c"]),
                 (mask3[:, :], A["mask3"])]
        assert len(loads) == LOADS
        for dst, src in loads:
            act.dma_start(dst, src).then_inc(const_in, 16)
        for n in range(AHEAD):
            split_act(act, 0, n)
        act.wait_ge(const_in, 16 * LOADS)
        act.wait_ge(dve_chain, 1)
        act.activation(soft[:, 1], soft[:, 0], ACT.Exp, scale=-1.0).then_inc(soft_exp, 1)

        def first():
            for kt in range(KT):
                act.activation(aT_hi[:, kt], xT[:, kt], ACT.Copy, scale=gains[:, 0, kt:kt + 1]).then_inc(x_hi, 1)
            act_norm(act, 0, lambda: None)
            act_root(act, 0)
        act_product(act, "ab_in", [(2, project_end(act, 0, z0)), (2, project_end(act, 0, z0, ACT.Gelu_apprx_tanh)),
                                   (2, project_end(act, 0, z0))], first)
        for j in range(0, 3 * LT, 2):
            act.wait_ge(m_tp, j + 1)
            dst = xr[:, j, PADC:] if j < LT else gateT[:, j - LT, :] if j < 2 * LT else uT[:, j - 2 * LT, PADP:]
            act.activation(dst, tp[0][:, 0:S], ACT.Copy).then_inc(m_ev_act, 1)
        for j in range(LT):
            act.wait_ge(gates_mm, j + 1)
            act.activation(rg[:, j], pa[:, 2 * (j % 2), 0:S], ACT.Sigmoid, bias=vecs[:, 5, j:j + 1])
            act.activation(ig[:, j], pa[:, 2 * (j % 2) + 1, 0:S], ACT.Sigmoid, bias=vecs[:, 6, j:j + 1])\
                .then_inc(gates_sg, 1)
        act.wait_ge(gates_sg, LT)
        for j in range(LT):
            act.activation(dec[:, j], rg[:, j], ACT.Exp, scale=soft[:, 3, j:j + 1])
            e = act.activation(th[:, j], rg[:, j], ACT.Tanh, scale=soft[:, 2, j:j + 1])
        e.then_inc(decay_done, 1)
        act.wait_ge(lru_dve, 3)
        act.activation(th[:, :, :], th[:, :, :], ACT.Sqrt, scale=2.0).then_inc(lru_root, 1)
        act.wait_ge(lru_dve, 7)
        act.activation(aT_hi[:, 0:LT, :], xc[:, :, :], ACT.Copy).then_inc(mix_hi, 1)
        for j in range(LT):
            act.wait_ge(pool_mm, j + 1)
            act.activation(aT_hi[:, LT + j, :], tp[j % 2][:, 0:S], ACT.Copy, scale=vecs[:, 8, j:j + 1])\
                .then_inc(mix_hi, 1)
        act_product(act, "ab_out", [(4, None)])
        act_proj(act, 0, None)
        act_mlp(act, 0, 1, 1, lambda: act_norm(act, 1, lambda: freed(act, "ab_out", 4)))

        def first():
            act_tiles(act, TILE0["gate0"], aT_hi, 2)
            act_norm(act, 2, lambda: freed(act, "mlp0", 32))
            act_root(act, 2)
        act_product(act, "gate0", [(4, act_gate_end(act, 0, 2))], first)

        def first():
            act_tiles(act, TILE0["c_in"], aT_hi, 3)
            act_norm(act, 3, lambda: act.wait_ge(h_done, 8))
            act_root(act, 3)
        act_product(act, "c_in", [(10, project_end(act, 3, z1))], first)
        C, A_ = CHUNK0["c_tail"], ACC0["c_tail"]
        for n in range(AHEAD, AHEAD + GT):
            split_act(act, C, n)
        act_project(act, C, A_, 3, lambda t: z1[:, t, C_GATES:W_C], ACT.Sigmoid, width=W_C - C_GATES)
        for kv in range(2):
            C, A_ = CHUNK0[("cmp_k", "cmp_v")[kv]], ACC0[("cmp_k", "cmp_v")[kv]]
            if kv == 1:
                act.wait_ge(group_used, C * GT)
            act.wait_ge(blk_done, 2 + kv)
            act.activation(blk_hi[:, :, :], blk[:, :, :], ACT.Copy).then_inc(blk_hi_done, 1)
            for cc in range(2):
                for n in range(AHEAD, AHEAD + GT):
                    split_act(act, C + cc, n)
            act.wait_ge(group_used, (C + 2) * GT)
            if kv == 1:
                act.wait_ge(chid_tp, 1)
            act.activation(chid[:, :], acc[0][0:NKV * NCMP, :], ACT.Gelu_apprx_tanh).then_inc(chid_done, 1)
        act_round(act, attn1, 0)
        with act.Fori(1, attn1.rounds) as i:
            act_round(act, attn1, i)
        act_product(act, "c_out", [(4, None)], lambda: act_tiles(act, TILE0["c_out"], aT_hi, None))
        act_proj(act, 1, None)
        act_mlp(act, 1, 4, 4, lambda: act_norm(act, 4, lambda: freed(act, "c_out", 4)))

        def first():
            act_tiles(act, TILE0["gate1"], aT_hi, 5)
            act_norm(act, 5, lambda: freed(act, "mlp1", 32))
            act_root(act, 5)
        act_product(act, "gate1", [(4, act_gate_end(act, 1, 5))], first)
        act_norm(act, 6, lambda: act.wait_ge(h_done, 16))
        act_root(act, 6)

        def first():
            act_tiles(act, TILE0["ab2_in"], aT_hi, 6)
            act_norm(act, 7, lambda: act.wait_ge(fin_done, 1))
            act_root(act, 7)
        act_product(act, "ab2_in", [(9, project_end(act, 7, z2)), (4, project_end(act, 7, z2, ACT.Silu))], first)
        with act.Fori(0, attn2a.rounds) as i:
            act_round(act, attn2a, i)
        with act.Fori(0, attn2b.rounds) as i:
            act_round(act, attn2b, i)
        act_product(act, "ab2_out", [(4, None)], lambda: act_tiles(act, TILE0["ab2_out"], aT_hi, None))

        def first():
            act_tiles(act, TILE0["c2_in"], aT_hi, 7)
            act_norm(act, 8, lambda: freed(act, "ab2_out", 4))
            act_root(act, 8)
        act_product(act, "c2_in", [(12, project_end(act, 8, z3)), (4, project_end(act, 8, z3, ACT.Silu))], first)
        with act.Fori(0, attn3.rounds) as i:
            act_round(act, attn3, i)
        act_product(act, "c2_out", [(4, None)], lambda: act_tiles(act, TILE0["c2_out"], aT_hi, None), last=True)
        act_norm(act, 9, lambda: freed(act, "c2_out", 4))
        act_root(act, 9)

    @block.vector
    def _(dve):
        chain = [0]

        def link(ins):
            chain[0] += 1
            ins.then_inc(dve_chain, 1)
            dve.wait_ge(dve_chain, chain[0])

        dve.wait_ge(const_in, 16 * LOADS)
        lam, mag, y, sp, neg = vecs[:, 7], soft[:, 0], soft[:, 1], soft[:, 2], soft[:, 3]
        link(dve.scalar_tensor_tensor(out=mag, in0=lam, scalar=-1.0, in1=lam, op0=ALU.mult, op1=ALU.max))
        for n in range(AHEAD):
            split_dve(dve, 0, n)
        dve.wait_ge(soft_exp, 1)
        link(dve.tensor_scalar(sp, y, 2.0, None, ALU.add))
        link(dve.reciprocal(sp, sp))
        link(dve.tensor_tensor(y, y, sp, ALU.mult))
        link(dve.tensor_tensor(mag, y, y, ALU.mult))
        link(dve.tensor_scalar(sp, mag, 1.0 / 19, None, ALU.mult))
        for n in range(17, 1, -2):
            link(dve.scalar_tensor_tensor(out=sp, in0=sp, scalar=1.0 / n, in1=mag, op0=ALU.add, op1=ALU.mult))
        link(dve.scalar_tensor_tensor(out=sp, in0=sp, scalar=1.0, in1=y, op0=ALU.add, op1=ALU.mult))
        link(dve.tensor_scalar(mag, lam, -1.0, 0.0, ALU.mult, ALU.max))
        link(dve.scalar_tensor_tensor(out=sp, in0=sp, scalar=2.0, in1=mag, op0=ALU.mult, op1=ALU.add))
        link(dve.tensor_scalar(neg, sp, -8.0, None, ALU.mult))
        link(dve.tensor_scalar(sp, sp, 8.0, None, ALU.mult))

        def first():
            for kt in range(KT):
                dve.wait_ge(x_hi, kt + 1)
                dve.scalar_tensor_tensor(out=aT_lo[:, kt], in0=xT[:, kt], scalar=gains[:, 0, kt:kt + 1],
                                         in1=aT_hi[:, kt].bitcast(F32), op0=ALU.mult, op1=ALU.subtract).then_inc(x_lo, 1)
            dve_means(dve, 0, 1e-6)
            dve_rstd(dve, 0)
        dve_product(dve, "ab_in", None, first)
        link(dve.memset(xr[:, :, 0:PADC], 0.0))
        for j in range(1, 3 * LT, 2):
            dve.wait_ge(m_tp, j + 1)
            dst = xr[:, j, PADC:] if j < LT else gateT[:, j - LT, :] if j < 2 * LT else uT[:, j - 2 * LT, PADP:]
            dve.tensor_copy(dst, tp[1][:, 0:S]).then_inc(m_ev_dve, 1)
        dve.wait_ge(m_ev_act, LT // 2)
        dve.wait_ge(m_ev_dve, LT // 2)
        for k in range(4):
            for j in range(LT):
                if k == 0:
                    dve.tensor_scalar(xc[:, j], xr[:, j, 0:S], vecs[:, 0, j:j + 1], vecs[:, 4, j:j + 1],
                                      ALU.mult, ALU.add).then_inc(conv_done, 1)
                else:
                    dve.wait_ge(conv_done, LT * (k - 1) + j + 1)
                    dve.scalar_tensor_tensor(out=xc[:, j], in0=xr[:, j, k:k + S], scalar=vecs[:, k, j:j + 1],
                                             in1=xc[:, j], op0=ALU.mult, op1=ALU.add).then_inc(conv_done, 1)
        dve.wait_ge(decay_done, 1)
        dve.tensor_scalar(rg[:, :, :], th[:, :, :], 1.0, None, ALU.add).then_inc(lru_dve, 1)
        dve.wait_ge(lru_dve, 1)
        dve.reciprocal(rg[:, :, :], rg[:, :, :]).then_inc(lru_dve, 1)
        dve.wait_ge(lru_dve, 2)
        dve.tensor_tensor(th[:, :, :], th[:, :, :], rg[:, :, :], ALU.mult).then_inc(lru_dve, 1)
        dve.tensor_tensor(ig[:, :, :], ig[:, :, :], xc[:, :, :], ALU.mult).then_inc(lru_dve, 1)
        dve.wait_ge(lru_root, 1)
        dve.wait_ge(lru_dve, 4)
        dve.tensor_tensor(ig[:, :, :], ig[:, :, :], th[:, :, :], ALU.mult).then_inc(lru_dve, 1)
        dve.wait_ge(lru_dve, 5)
        for j in range(LT):
            s = dve.tensor_tensor_scan(xc[:, j], dec[:, j], ig[:, j], 0.0, ALU.mult, ALU.add)
        s.then_inc(lru_dve, 1)
        dve.wait_ge(lru_dve, 6)
        dve.wait_ge(m_ev_act, LT)
        dve.wait_ge(m_ev_dve, LT)
        dve.tensor_tensor(xc[:, :, :], xc[:, :, :], gateT[:, :, :], ALU.mult).then_inc(lru_dve, 1)
        dve.wait_ge(mix_hi, 1)
        dve.wait_ge(lru_dve, 7)
        dve.tensor_tensor(aT_lo[:, 0:LT, :], xc[:, :, :], aT_hi[:, 0:LT, :].bitcast(F32), ALU.subtract).then_inc(mix_lo, 1)
        for j in range(LT):
            dve.wait_ge(mix_hi, j + 2)
            dve.scalar_tensor_tensor(out=aT_lo[:, LT + j, :], in0=tp[j % 2][:, 0:S], scalar=vecs[:, 8, j:j + 1],
                                     in1=aT_hi[:, LT + j, :].bitcast(F32), op0=ALU.mult, op1=ALU.subtract)\
                .then_inc(mix_lo, 1)
        dve_product(dve, "ab_out", residual_end(dve))
        dve_proj(dve, 0)
        dve_mlp(dve, 0, 1, 1)

        def norm_first(name, gain, m, eps):
            def first():
                dve_tiles(dve, TILE0[name], aT_hi, aT_lo, gain)
                if m is not None:
                    dve_means(dve, m, eps)
                    dve_rstd(dve, m)
            return first
        dve_product(dve, "gate0", dve_gate_end(dve, 0), norm_first("gate0", 2, 2, 1e-6))
        dve_product(dve, "c_in", None, norm_first("c_in", 3, 3, 1e-6))
        for n in range(AHEAD, AHEAD + GT):
            split_dve(dve, CHUNK0["c_tail"], n)
        for n in range(8):
            dve.wait_ge(c_tp, n + 1)
            dve.tensor_copy(cT[:, n // 4, n % 4, :], tp[n % 2][:, 0:S]).then_inc(c_ev, 1)
        for kv in range(2):
            C, A_ = CHUNK0[("cmp_k", "cmp_v")[kv]], ACC0[("cmp_k", "cmp_v")[kv]]
            dve.wait_ge(blk_hi_done, kv + 1)
            dve.tensor_tensor(blk_lo[:, :, :], blk[:, :, :], blk_hi[:, :, :].bitcast(F32), ALU.subtract)\
                .then_inc(blk_lo_done, 1)
            for cc in range(2):
                for n in range(AHEAD, AHEAD + GT):
                    split_dve(dve, C + cc, n)
            dve.wait_ge(chid_tp, kv + 1)
            if kv == 1:
                dve.wait_ge(cmp_mm, 1)
            dve.tensor_copy(chidT[:, :, :], tp[0][:, 0:HID // P * NKV * NCMP]
                            .rearrange("p (f n) -> p f n", f=HID // P)).then_inc(chid_ev, 1)
            dve.wait_ge(cmp_mm, kv + 1)
            if kv == 0:
                dve.tensor_copy(kcmpT[:, :], tp[1][:, 0:NKV * NCMP]).then_inc(cmp_ev, 1)
            else:
                dve.tensor_copy(vcmp[:, :, :], tp[1][0:NCMP, :].rearrange("n (g d) -> n g d", g=NKV)).then_inc(cmp_ev, 1)
        dve_round(dve, attn1, 0)
        with dve.Fori(1, attn1.rounds) as i:
            dve_round(dve, attn1, i)
        dve_product(dve, "c_out", residual_end(dve), norm_first("c_out", None, None, None))
        dve_proj(dve, 1)
        dve_mlp(dve, 1, 4, 4)
        dve_product(dve, "gate1", dve_gate_end(dve, 1), norm_first("gate1", 5, 5, 1e-6))

        def final(m, n, eps):
            dve_means(dve, m, eps)
            dve_rstd(dve, m)
            dve.wait_ge(rstd_done, m + 1)
            dve.wait_ge(g_in, 16 * n)
            for t in range(TOK):
                f = dve.scalar_tensor_tensor(out=h[:, t, :], in0=h[:, t, :], scalar=rstd[:, t:t + 1], in1=gfull[:, :],
                                             op0=ALU.mult, op1=ALU.mult)
            f.then_inc(fin_done, 1)
        final(6, 1, 1e-6)
        dve_product(dve, "ab2_in", None, norm_first("ab2_in", 6, 7, 1e-5))
        with dve.Fori(0, attn2a.rounds) as i:
            dve_round(dve, attn2a, i)
        with dve.Fori(0, attn2b.rounds) as i:
            dve_round(dve, attn2b, i)
        dve_product(dve, "ab2_out", residual_end(dve), norm_first("ab2_out", None, None, None))
        dve_product(dve, "c2_in", None, norm_first("c2_in", 7, 8, 1e-5))
        with dve.Fori(0, attn3.rounds) as i:
            dve_round(dve, attn3, i)
        dve_product(dve, "c2_out", residual_end(dve), norm_first("c2_out", None, None, None), last=True)
        final(9, 2, 1e-5)

    @block.tensor
    def _(pe):
        pe.wait_ge(x_lo, KT)
        pe_product(pe, "ab_in", aT, x_ready=lambda: None)
        freed(pe, "ab_in", 6)
        for j in range(3 * LT):
            if j >= 2:
                pe.wait_ge((m_ev_act, m_ev_dve)[j % 2], j // 2)
            for t in range(TOK):
                mm = pe.transpose(tp[j % 2][:, t * P:(t + 1) * P], z0[:, t, j * P:(j + 1) * P], ident[:, :])
            mm.then_inc(m_tp, 1)
        pe.wait_ge(bd_in, 64)
        for j in range(LT):
            pe.wait_ge(conv_done, 3 * LT + j + 1)
            if j >= 2:
                pe.wait_ge(gates_sg, j - 1)
            for n in range(2):
                mm = pe.matmul(pa[:, 2 * (j % 2) + n, 0:S], bd[:, n, j, :], xc[:, j, :], start=True, stop=True)
            mm.then_inc(gates_mm, 1)
        for j in range(LT):
            g, jo = j // 2, j % 2
            pe.wait_ge(pool_step, 4 + 3 * g + 3)
            pe.wait_ge(m_ev_act, 12)
            pe.wait_ge(m_ev_dve, 12)
            if j >= 2:
                pe.wait_ge(mix_lo, j)
            for i2 in range(2):
                mm = pe.matmul(tp[j % 2][:, 0:S], pool_w[:, 2 * g + i2, jo * P:(jo + 1) * P],
                               uT[:, 2 * g + i2, PADP:], start=(i2 == 0), stop=(i2 == 1))
            mm.then_inc(pool_mm, 1)
        pe_product(pe, "ab_out", aT, x_ready=lambda: pe.wait_ge(mix_lo, LT + 1))
        pe_proj(pe, 0)
        pe_mlp(pe, 0, "ab_out")
        pe_product(pe, "gate0", aT, h, after_residual(pe, "mlp0", 28))
        pe_product(pe, "c_in", aT, h, after_gate(pe, 0))
        C, A_ = CHUNK0["c_tail"], ACC0["c_tail"]
        pe_chunk(pe, C, A_, aT, width=W_C - C_GATES)
        freed(pe, "c_in", 10)
        for n in range(8):
            if n >= 2:
                pe.wait_ge(c_ev, n - 1)
            for t in range(TOK):
                mm = pe.transpose(tp[n % 2][:, t * P:(t + 1) * P], z1[:, t, D + n * P:D + (n + 1) * P], ident[:, :])
            mm.then_inc(c_tp, 1)
        M = NKV * NCMP
        pe.wait_ge(c_ev, 8)
        for kv in range(2):
            C, A_ = CHUNK0[("cmp_k", "cmp_v")[kv]], ACC0[("cmp_k", "cmp_v")[kv]]
            pe.wait_ge(blk_lo_done, kv + 1)
            for n in range(2 * GT):
                pe.wait_ge(split_done, C * GT + n + 1)
                if n == 0:
                    freed(pe, "c_tail", 1)
                    if kv == 1:
                        pe.wait_ge(chid_done, 1)
                for i in range(GT):
                    tok = GT * n + i
                    for a, w in ((blk_hi, w_hi), (blk_hi, w_lo), (blk_lo, w_hi)):
                        mm = pe.matmul(acc[0][0:BW, :], a[:, tok, 0:BW], w[:, n % RING, i, :],
                                       start=(tok == 0 and a is blk_hi and w is w_hi), stop=(tok == CL - 1 and a is blk_lo))
                mm.then_inc(group_used, 1)
            pe.wait_ge(cmp_in, 48)
            pe.wait_ge(chid_done, kv + 1)
            if kv == 1:
                pe.wait_ge(cmp_ev, 1)
            for f in range(HID // P):
                mm = pe.transpose(tp[0][:, f * M:(f + 1) * M], chid[:, f * P:(f + 1) * P], ident[0:M, 0:M])
            mm.then_inc(chid_tp, 1)
            pe.wait_ge(chid_ev, kv + 1)
            if kv == 0:
                for f in range(HID // P):
                    mm = pe.matmul(tp[1][:, 0:M], cw2[:, 0, f, :], chidT[:, f, :], start=(f == 0), stop=(f == HID // P - 1))
            else:
                for g in range(NKV):
                    for f in range(HID // P):
                        mm = pe.matmul(tp[1][0:NCMP, g * HD:(g + 1) * HD], chidT[:, f, g * NCMP:(g + 1) * NCMP],
                                       cw2[:, 1, f, :], start=(f == 0), stop=(f == HID // P - 1))
            mm.then_inc(cmp_mm, 1)
        pe.wait_ge(cmp_ev, 2)
        pe_round(pe, attn1, 0)
        with pe.Fori(1, attn1.rounds) as i:
            pe_round(pe, attn1, i)
        pe_product(pe, "c_out", aT, z1, once(lambda: pe.wait_ge(y_done, attn2a.unit0)))
        pe_proj(pe, 1)
        pe_mlp(pe, 1, "c_out")
        pe_product(pe, "gate1", aT, h, after_residual(pe, "mlp1", 28))
        pe_product(pe, "ab2_in", aT, h, once(lambda: pe.wait_ge(fin_done, 1)))
        with pe.Fori(0, attn2a.rounds) as i:
            pe_round(pe, attn2a, i)
        with pe.Fori(0, attn2b.rounds) as i:
            pe_round(pe, attn2b, i)
        pe_product(pe, "ab2_out", aT, z2, once(lambda: pe.wait_ge(y_done, attn3.unit0)))
        pe_product(pe, "c2_in", aT, h, after_residual(pe, "ab2_out"))
        with pe.Fori(0, attn3.rounds) as i:
            pe_round(pe, attn3, i)
        pe_product(pe, "c2_out", aT, z3, once(lambda: pe.wait_ge(y_done, attn3.unit0 + 16)))

    ctx.close()


LOADS = 11
RPB_DMAS = NH * 4
BW = 68



def _stream(w, rows=None):
    k, n = w.shape
    if n % NW:
        w = np.pad(w, ((0, 0), (0, NW - n % NW)))
        n = w.shape[1]
    return w.reshape(k // (GT * P), GT, P, n // NW, NW).transpose(3, 0, 2, 1, 4).reshape(-1, P, GT * NW)


def _layout(a):
    f = np.float32
    a = {k: np.asarray(v) for k, v in a.items()}
    parts = []

    def mlp(l):
        up, down = a["mlp_w_up"][l], a["mlp_w_down"][l]
        for q in range(4):
            parts.append(_stream(up[:, q * D:(q + 1) * D]))
            parts.append(_stream(down[q * D:(q + 1) * D]))

    def proj(l):
        w = a["ple_w_proj"][l].reshape(2, P, NCH, NW).transpose(2, 1, 0, 3).reshape(NCH, P, 2 * NW)
        parts.append(np.pad(w, ((0, 0), (0, 0), (0, 2 * NW))))

    parts += [_stream(a["ab_w_in"][0]), _stream(a["ab_w_out"][0])]
    proj(0)
    mlp(0)
    parts += [_stream(a["ple_w_gate"][0]), _stream(a["c_w_in"][0])]
    parts += [_stream(a[k][0].reshape(CL * HD, HID)) for k in ("c_cmp_w1_k", "c_cmp_w1_v")]
    parts.append(_stream(a["c_w_out"][0]))
    proj(1)
    mlp(1)
    parts += [_stream(a["ple_w_gate"][1]), _stream(a["w_in_ab_2"][0]), _stream(a["w_out_ab_2"][0]),
              _stream(a["w_in_c_2"][0]), _stream(a["w_out_c_2"][0])]
    o = {"wstream": np.concatenate(parts)}
    assert o["wstream"].shape[0] == NC * GT

    def column(v, n):
        return v.reshape(n, P).T

    o["x"] = a["x"]
    o["xT"] = a["x"][0].T
    o["pT"] = a["p"][:, 0].transpose(0, 2, 1)
    g = [a["ln_mix_g"][0], a["ln_mlp_g"][0], a["ln_ple_g"][0], a["ln_mix_g"][1], a["ln_mlp_g"][1], a["ln_ple_g"][1],
         a["ln_ab_2"][0], a["ln_c_2"][0]]
    o["gains"] = np.stack([column(v, KT) for v in g], 1)
    v = [*a["ab_conv_w"][0], a["ab_conv_b"][0], a["ab_b_rgate"][0], a["ab_b_igate"][0], a["ab_lambda"][0],
         a["ab_pool_scale"][0]]
    o["vecs"] = np.stack([column(x, LT) for x in v], 1)
    o["pool_w"] = a["ab_pool_w"][0].reshape(LT, P, S).transpose(1, 0, 2)
    o["w_r"], o["w_i"] = a["ab_w_rgate"][0], a["ab_w_igate"][0]
    o["w2_k"], o["w2_v"] = a["c_cmp_w2_k"][0], a["c_cmp_w2_v"][0]
    o["posT"] = np.stack([a["c_cmp_pos_k"][0].T, a["c_cmp_pos_v"][0].T])
    o["sinks"] = np.broadcast_to(a["sink_a_2"][0], (P, 8))
    o["g1"] = np.broadcast_to(a["ln_final_g"], (P, D))
    o["g2"] = np.broadcast_to(a["ln_f_2"], (P, D))
    o["rpb"] = np.tile(np.pad(a["rpb_c_2"][0], ((0, 0), (0, 0), (48, 49))), (1, 1, 64))

    t = np.arange(S)
    dist = t[:, None] - t[None, :]
    slope = np.exp2(-8.0 * np.arange(1, NH + 1) / NH)
    neg = -1e30

    def table(b):
        return b.reshape(4, 4, TOK, P, S).transpose(0, 3, 1, 2, 4).reshape(4, P, 4 * TOK * S).astype(f)

    o["ident"] = np.eye(P, dtype=f)
    o["bias1"] = table(np.where(dist >= 0, -slope[:, None, None] * dist, neg))
    far = np.abs(dist)
    times = sum(((far <= w // 2) & (dist % d == 0)).astype(int) for w, d in ((128, 1), (512, 4), (2048, 16)))
    b = np.where(far <= 128, -slope[:, None, None] * far, neg)
    b[8:] = np.where(times > 0, -slope[8:, None, None] * far + np.log(np.maximum(times, 1)), neg)
    o["bias2"] = table(b)
    end = np.arange(NCMP) * 16 + CL - 1
    dc = t[:, None] - end[None, :]
    bc = np.where(dc >= 0, -slope[:, None, None] * dc, neg)
    o["bias_c"] = bc.reshape(NH, TOK, P, NCMP).transpose(2, 0, 1, 3).astype(f)
    o["valid_c"] = (dc >= 0).reshape(TOK, P, NCMP).transpose(1, 0, 2).astype(f)
    c = np.arange(64)
    c0 = np.clip(c - 8, 0, 48)
    inside = (c[None, :] >= c0[:, None]) & (c[None, :] < c0[:, None] + 16)
    o["mask3"] = np.tile(np.where(inside, 0.0, neg), (2, 4)).astype(f)
    cnt = np.minimum(np.arange(PADP) + 1, np.array([2, 4, 8, 16])[:, None])
    o["invcnt"] = np.broadcast_to((1.0 / cnt).astype(f), (P, 4, PADP))
    return {k: np.ascontiguousarray(v) for k, v in o.items()}


def kernel(**inputs):
    import concourse.bacc as bacc
    from concourse.bass_utils import run_bass_kernel_spmd

    arrays = _layout(inputs)
    nc = bacc.Bacc("TRN2", target_bir_lowering=False, num_devices=1)
    A = {k: nc.dram_tensor(f"in_{k}", v.shape, mybir.dt.from_np(v.dtype), kind="ExternalInput").ap()
         for k, v in arrays.items()}
    A["bias3"] = nc.dram_tensor("bias3", (4, P, 4 * TOK * S), F32, kind="Internal").ap()
    out = nc.dram_tensor("out", (1, S, D), F32, kind="ExternalOutput").ap()
    build(nc, A, out)
    r = run_bass_kernel_spmd(nc, [{f"in_{k}": v for k, v in arrays.items()}], core_ids=[0])
    return r.results[0]["out"]
```

```python
from contextlib import ExitStack

import numpy as np

import concourse.bass as bass
from concourse import mybir

ALU = mybir.AluOpType
ACT = mybir.ActivationFunctionType
AX_X = mybir.AxisListType.X
F32 = mybir.dt.float32
F32R = mybir.dt.float32r

P = 128
S = 256
TOK = S // P
D = 2048
KT = D // P
NW = 512
GT = 4
NCH = D // NW
HD = 128
NH = 16
QSCALE = float(HD) ** -0.5
RAW, RING = 2, 4
AHEAD = 3
LRU = 1024
LT = LRU // P
PADC = 3
PADP = 16
NCMP = 15
NKV = 4
CL = 32
HID = 512
C_GATES = D + 6 * 512
NB3 = 3
W_C = C_GATES + NB3 * NH

ORDER = [("ab_in", 6), ("ab_out", 4), ("proj0", 1), ("mlp0", 32), ("gate0", 4),
         ("c_in", 10), ("c_tail", 1), ("cmp_k", 2), ("cmp_v", 2), ("c_out", 4), ("proj1", 1),
         ("mlp1", 32), ("gate1", 4),
         ("ab2_in", 13), ("ab2_out", 4), ("c2_in", 16), ("c2_out", 4)]
CHUNK0 = {}
NC = 0
for _name, _n in ORDER:
    CHUNK0[_name] = NC
    NC += _n

ACC0 = {}
_a = 0
for _name, _n in ORDER:
    ACC0[_name] = _a
    _a += 4 if _name.startswith("proj") else 0 if _name.startswith("cmp") else _n

TILE0 = {}
_t = 0
for _name, _n in [("x", KT), ("ab_out", KT), ("hidden0", 4 * KT), ("mlp0", KT), ("gate0", KT), ("y1", KT), ("c_out", KT),
                  ("hidden1", 4 * KT), ("mlp1", KT), ("ab2_in", KT), ("ab2_out", KT), ("c2_in", KT),
                  ("c2_out", KT)]:
    TILE0[_name] = _t
    _t += _n


def build(nc, A, out):
    ctx = ExitStack()

    def sb(name, shape, dt=F32, stack=None):
        return (stack or ctx).enter_context(nc.sbuf_tensor(name, shape, dt))

    def overlay(*tensors):
        with ExitStack() as stack:
            return [sb(*t, stack=stack) for t in tensors]

    def bank(name):
        return ctx.enter_context(nc.psum_tensor(name, [P, 512], F32))

    def sem(name):
        return ctx.enter_context(nc.semaphore(name))

    raw = sb("raw", [P, RAW, GT, NW])
    w_hi = sb("w_hi", [P, RING, GT, NW], F32R)
    w_lo = sb("w_lo", [P, RING, GT, NW], F32R)
    h = sb("h", [P, TOK, D])
    ident = sb("ident", [P, P])
    gains = sb("gains", [P, 8, KT])
    stat = sb("stat", [P, 3, TOK])
    rstd = sb("rstd", [P, TOK])
    small = sb("small", [P, 8, 2, TOK])
    sinks = sb("sinks", [P, 8])
    bias_c = sb("bias_c", [P, NH, TOK, NCMP])
    valid_c = sb("valid_c", [P, TOK, NCMP])
    mask3 = sb("mask3", [P, S])
    kcmpT = sb("kcmpT", [P, NKV * NCMP])
    vcmp = sb("vcmp", [NCMP, NKV, HD])

    xc, rg, ig, th, _, xr, uT, pool_w = overlay(
        ("xc", [P, LT, S]), ("rg", [P, LT, S]), ("ig", [P, LT, S]), ("th", [P, LT, S]), ("part_", [P, TOK, NW]),
        ("xr", [P, LT, PADC + S]), ("uT", [P, LT, PADP + S]), ("pool_w", [P, LT, S]))
    xT, = overlay(("xT", [P, KT, S]))
    _, pw0, pw1 = overlay(("xc_", [P, LT, S]), ("pw0", [P, LT, PADP + S]), ("pw1", [P, LT - 2, PADP + S]))
    z1, cT, chid, chidT, cw2, posT = overlay(
        ("z1", [P, TOK, W_C]), ("cT", [P, 2, NKV, S]), ("chid", [NKV * NCMP, HID]),
        ("chidT", [P, HID // P, NKV * NCMP]), ("cw2", [P, 2, HID // P, HD]), ("posT", [P, 2, CL]))
    z2, = overlay(("z2", [P, TOK, 6656]))
    z3, = overlay(("z3", [P, TOK, 8192]))
    bT_hi, bT_lo, part, gpart, proj, pT_hi, pT_lo, pT = overlay(
        ("bT_hi", [P, KT, S], F32R), ("bT_lo", [P, KT, S], F32R), ("part", [P, TOK, NW]), ("gpart", [P, TOK, NW]),
        ("proj", [P, TOK, D]), ("pT_hi", [P, 2, S], F32R), ("pT_lo", [P, 2, S], F32R), ("pT", [P, 2, S]))
    gfull, = overlay(("gfull", [P, D]))
    sb("region_z", [P, 16384])

    aT_hi, aT_lo = overlay(("aT_hi", [P, KT, S], F32R), ("aT_lo", [P, KT, S], F32R))
    blk, blk_hi, blk_lo = overlay(
        ("blk", [P, CL, BW]), ("blk_hi", [P, CL, BW], F32R), ("blk_lo", [P, CL, BW], F32R))
    stq, stk, stv, bias, qkT, prob, prT = overlay(
        ("stq", [P, TOK, 4, HD]), ("stk", [P, TOK, 4, HD]), ("stv", [NCMP, 4, HD]), ("bias", [P, 4, TOK, S]), ("qkT", [P, 2, 2 * S]),
        ("prob", [P, 2, TOK, S + 2]), ("prT", [P, 2, TOK, S]))
    sb("region_a", [P, 8192])

    bd = sb("bd", [P, 2, LT, P])
    vecs = sb("vecs", [P, 9, LT])
    soft = sb("soft", [P, 4, LT])
    invcnt = sb("invcnt", [P, 4, PADP])

    acc = [bank(f"acc{t}") for t in range(TOK)]
    tp = [bank(f"tp{t}") for t in range(2)]
    pa = ctx.enter_context(nc.psum_tensor("pa", [P, 4, 512], F32))

    landed = [sem(f"landed{i}") for i in range(RAW)]
    hi_done = sem("hi_done")
    split_done = sem("split_done")
    group_used = sem("group_used")
    acc0_done = sem("acc0_done")
    acc1_done = sem("acc1_done")
    acc_free = [sem(f"acc_free{t}") for t in range(TOK)]
    tp_done = sem("tp_done")
    thi_done = sem("thi_done")
    tlo_done = sem("tlo_done")
    kept = sem("kept")
    h_done = sem("h_done")
    hid_done = sem("hid_done")
    gp_done = sem("gp_done")
    sq_done = sem("sq_done")
    ms_done = sem("ms_done")
    root_done = sem("root_done")
    rstd_done = sem("rstd_done")
    x_in = sem("x_in")
    const_in = sem("const_in")
    bd_zero = sem("bd_zero")
    bd_in = sem("bd_in")
    dve_chain = sem("dve_chain")
    soft_exp = sem("soft_exp")
    m_tp = sem("m_tp")
    m_ev = sem("m_ev")
    gated = sem("gated")
    conv_step = sem("conv_step")
    conv_done = sem("conv_done")
    gates_mm = sem("gates_mm")
    gates_sg = sem("gates_sg")
    tanh_done = sem("tanh_done")
    decay_done = sem("decay_done")
    lru_dve = sem("lru_dve")
    lru_root = sem("lru_root")
    mix_hi = sem("mix_hi")
    mix_lo = sem("mix_lo")
    pads_zero = sem("pads_zero")
    pool_step = sem("pool_step")
    pool_mm = sem("pool_mm")
    p_in = sem("p_in")
    p_hi = sem("p_hi")
    p_lo = sem("p_lo")
    proj_done = sem("proj_done")
    cmp_in = sem("cmp_in")
    c_tp = sem("c_tp")
    c_ev = sem("c_ev")
    blk_done = sem("blk_done")
    blk_hi_done = sem("blk_hi_done")
    blk_lo_done = sem("blk_lo_done")
    chid_done = sem("chid_done")
    chid_tp = sem("chid_tp")
    chid_ev = sem("chid_ev")
    cmp_mm = sem("cmp_mm")
    cmp_ev = sem("cmp_ev")
    bias_in = [sem(f"bias_in{i}") for i in range(4)]
    bias_ok = sem("bias_ok")
    staged = [sem(f"staged{i}") for i in range(4)]
    qk_tp = sem("qk_tp")
    qk_ev = sem("qk_ev")
    s_mm = sem("s_mm")
    sink_in = sem("sink_in")
    max_done = sem("max_done")
    biased = sem("biased")
    neg_done = sem("neg_done")
    exp_done = sem("exp_done")
    pmask = sem("pmask")
    rden_done = sem("rden_done")
    coef_done = sem("coef_done")
    p_tp = sem("p_tp")
    p_ev = sem("p_ev")
    pv_mm = sem("pv_mm")
    y_done = sem("y_done")
    g_in = sem("g_in")
    fin_done = sem("fin_done")
    rpb_out = sem("rpb_out")
    out_done = sem("out_done")

    wstream = A["wstream"]

    def split_act(act, C, n):
        act.wait_ge(landed[n % RAW], (C * 2 + n // RAW + 1) * 16)
        if not isinstance(C, int) or C * GT + n >= RING:
            act.wait_ge(group_used, C * GT + (n - RING + 1))
        act.activation(w_hi[:, n % RING], raw[:, n % RAW], ACT.Copy).then_inc(hi_done, 1)

    def split_dve(dve, C, n):
        dve.wait_ge(hi_done, C * GT + (n + 1))
        dve.tensor_tensor(w_lo[:, n % RING], raw[:, n % RAW], w_hi[:, n % RING].bitcast(F32),
                          ALU.subtract).then_inc(split_done, 1)


    def pe_group(pe, C, A0, n, lhs, tiles=None, then=None, width=NW, turn=None):
        hi, lo = lhs
        pe.wait_ge(split_done, C * GT + (n + 1))
        for t in range(TOK):
            if n == 0 and not (isinstance(A0, int) and A0 == 0):
                pe.wait_ge(acc_free[t], A0)
            for i in range(GT):
                kt = GT * n + i
                if tiles is not None and t == 0:
                    pe.wait_ge(tlo_done, tiles + (kt + 1))
                for a, w in ((hi, w_hi), (hi, w_lo), (lo, w_hi)):
                    mm = pe.matmul(acc[t][:, 0:width], a[:, kt, t * P:(t + 1) * P], w[:, n, i, 0:width],
                                   start=(kt == 0 and a is hi and w is w_hi),
                                   stop=(kt == KT - 1 and a is lo))
                if t == 0 and then is not None:
                    then(i)
                if turn is not None and n == 1 and i % 2 == 1:
                    turn(2 * t + i // 2)
            if t == 0 and n == GT - 1:
                mm.then_inc(acc0_done, 1)
        mm.then_inc(group_used, 1)

    def pe_chunk(pe, C, A0, lhs, width=NW, turn=None, before=None):
        for n in range(GT):
            if before:
                before(n)
            pe_group(pe, C, A0, n, lhs, width=width, turn=turn)

    def pe_tile(pe, T0, kt, src, ready):
        if ready is not None:
            ready(kt)
        pe.wait_ge(tlo_done, T0 + (kt - 1))
        for t in range(TOK):
            mm = pe.transpose(tp[kt % 2][:, t * P:(t + 1) * P], src[:, t, kt * P:(kt + 1) * P], ident[:, :])
        mm.then_inc(tp_done, 1)

    def pe_first(pe, C, A0, T0, lhs, src, ready):
        for kt in range(GT):
            pe_tile(pe, T0, kt, src, ready)
        for n in range(GT):
            def then(i, n=n):
                if n < GT - 1:
                    pe_tile(pe, T0, GT * (n + 1) + i, src, ready)
            pe_group(pe, C, A0, n, lhs, tiles=T0, then=then)


    class Turn:
        def __init__(self, run, dst, gain, ready):
            self.T0, self.dst, self.gain, self.ready = TILE0[run], dst, gain, ready

    def pe_turn(pe, tr, c):
        def turn(i):
            if i == 0:
                tr.ready(pe, c)
            pe.wait_ge(tlo_done, c * 4 + (tr.T0 + i - 1))
            for t in range(TOK):
                mm = pe.transpose(tp[i % 2][:, t * P:(t + 1) * P], part[:, t, i * P:(i + 1) * P], ident[:, :])
            mm.then_inc(tp_done, 1)
        return turn

    def at_tile(x, c, i):
        return x[:, 4 * c + i] if isinstance(c, int) else x[:, bass.ds(c * 4 + i, 1)].rearrange("p a s -> p (a s)")

    def gain_of(tr, c, i):
        if tr.gain is None:
            return 1.0
        return gains[:, tr.gain, 4 * c + i:4 * c + i + 1] if isinstance(c, int) else \
            gains[:, tr.gain, bass.ds(c * 4 + i, 1)]

    def act_turn(act, tr, c):
        for i in range(GT):
            act.wait_ge(tp_done, c * 4 + (tr.T0 - KT + i + 1))
            act.activation(at_tile(tr.dst[0], c, i), tp[i % 2][:, 0:S], ACT.Copy, scale=gain_of(tr, c, i))\
                .then_inc(thi_done, 1)

    def dve_turn(dve, tr, c):
        for i in range(GT):
            dve.wait_ge(thi_done, c * 4 + (tr.T0 + i + 1))
            dve.scalar_tensor_tensor(
                out=at_tile(tr.dst[1], c, i), in0=tp[i % 2][:, 0:S], scalar=gain_of(tr, c, i),
                in1=at_tile(tr.dst[0], c, i).bitcast(F32), op0=ALU.mult, op1=ALU.subtract).then_inc(tlo_done, 1)


    def act_tiles(act, T0, hi, gain):
        for kt in range(KT):
            act.wait_ge(tp_done, T0 - KT + (kt + 1))
            act.activation(hi[:, kt], tp[kt % 2][:, 0:S], ACT.Copy,
                           scale=1.0 if gain is None else gains[:, gain, kt:kt + 1]).then_inc(thi_done, 1)

    def dve_tiles(dve, T0, hi, lo, gain):
        for kt in range(KT):
            dve.wait_ge(thi_done, T0 + (kt + 1))
            dve.scalar_tensor_tensor(
                out=lo[:, kt], in0=tp[kt % 2][:, 0:S], scalar=1.0 if gain is None else gains[:, gain, kt:kt + 1],
                in1=hi[:, kt].bitcast(F32), op0=ALU.mult, op1=ALU.subtract).then_inc(tlo_done, 1)


    def dve_means(dve, m, eps):
        dve.wait_ge(sq_done, TOK * (m + 1))
        dve.tensor_scalar(stat[:, 1], stat[:, 0], 1.0 / D, eps, ALU.mult, ALU.add).then_inc(ms_done, 1)

    def act_root(act, m):
        act.wait_ge(ms_done, m + 1)
        act.activation(stat[:, 2], stat[:, 1], ACT.Sqrt).then_inc(root_done, 1)

    def dve_rstd(dve, m):
        dve.wait_ge(root_done, m + 1)
        dve.reciprocal(rstd[:, :], stat[:, 2]).then_inc(rstd_done, 1)


    def act_project(act, C, A0, m, dst, func=ACT.Copy, width=NW):
        for t in range(TOK):
            if t == 0:
                act.wait_ge(acc0_done, A0 + 1)
                act.wait_ge(rstd_done, m + 1)
            else:
                act.wait_ge(group_used, C * GT + GT)
            act.activation(dst(t), acc[t][:, 0:width], func, scale=rstd[:, t:t + 1]).then_inc(acc_free[t], 1)

    def act_keep(act, A0, col):
        for t in range(TOK):
            act.wait_ge(acc_free[t], A0 + 1)
            act.activation(h[:, t, bass.ds(col, NW)], part[:, t, :], ACT.Copy).then_inc(kept, 1)

    def dve_residual(dve, C, A0, col, to_part=False):
        for t in range(TOK):
            if t == 0:
                dve.wait_ge(acc0_done, A0 + 1)
            else:
                dve.wait_ge(group_used, C * GT + GT)
            old = h[:, t, bass.ds(col, NW)]
            dve.tensor_tensor(part[:, t, :] if to_part else old, acc[t][:, :], old, ALU.add).then_inc(acc_free[t], 1)


    class Attention:

        def __init__(self, rounds, units, z, q_col, k_parts, unit0, cmp0, stage0, round0, table, gated=False,
                     silu_col=None, y_col=0, sink=False, masked=False, table0=0):
            self.rounds, self.units, self.z, self.q_col, self.k_parts = rounds, units, z, q_col, k_parts
            self.unit0, self.cmp0, self.stage0, self.round0 = unit0, cmp0, stage0, round0
            self.table, self.table0, self.gated, self.silu_col = table, table0, gated, silu_col
            self.y_col, self.sink, self.masked = y_col, sink, masked
            self.n = len(units)
            self.per_head = self.n // 4
            self.full = [u[0] == S for u in units]
            self.copies = 1 + len(k_parts(0)) + (1 if gated else 0)

        def U(self, i, u):
            return i * self.n + (self.unit0 + u)

        def M(self, i, u):
            n = u - sum(self.full[0:u]) if u >= 0 else -4
            return i * (self.n - sum(self.full)) + (self.cmp0 + n)

        def in_slot(self, i):
            return i * (16 * self.copies) + 16 * (self.stage0 + self.copies)

    units1 = []
    for hh in range(4):
        ks = 2 * (hh % 2)
        units1 += [(S, hh, ks, (D + 3 * 512, HD), 1), (S, hh, ks + 1, (D + 5 * 512, HD), 2), (NCMP, hh, None, None, 0)]
    attn1 = Attention(NKV, units1, z1, 0, lambda hh: [(D + 2 * 512, HD, 2 * (hh % 2)), (D + 4 * 512, HD, 2 * (hh % 2) + 1)],
                      unit0=0, cmp0=0, stage0=0, round0=0, table=A["bias1"], gated=True)
    attn2a = Attention(2, [(S, hh, hh, (1280, HD), None) for hh in range(4)], z2, 0, lambda hh: [(1024, HD, hh)],
                       unit0=48, cmp0=16, stage0=16, round0=4, table=A["bias2"], silu_col=4608, sink=True)
    attn2b = Attention(2, [(S, hh, hh, (3584 + hh * HD, 512), None) for hh in range(4)], z2, 1536,
                       lambda hh: [(2560 + hh * HD, 512, hh)], unit0=56, cmp0=16, stage0=20, round0=6,
                       table=A["bias2"], table0=2, silu_col=5632, y_col=1024)
    attn3 = Attention(4, [(S, hh, hh, (4096 + hh * HD, 512), None) for hh in range(4)], z3, 0,
                      lambda hh: [(2048 + hh * HD, 512, hh)], unit0=64, cmp0=16, stage0=24, round0=8,
                      table=A["bias3"], silu_col=6144, masked=True)

    def some(eng, s, value, least=1):
        if not isinstance(value, int) or value >= least:
            eng.wait_ge(s, value)

    def sp_round(sp, at, i):
        for hh in range(4):
            last_use = at.U(i, (hh + 1) * at.per_head - at.n)
            some(sp, qk_tp, last_use if not at.gated else at.U(i, (hh + 3) * at.per_head - at.n) if hh < 2
                 else at.U(i, (hh - 1) * at.per_head))
            sp.dma_start(stq[:, :, hh, :], at.z[:, :, bass.ds(i * 512 + (at.q_col + hh * HD), HD)])\
                .then_inc(staged[hh], 16)
            for col, per, slot in at.k_parts(hh):
                sp.dma_start(stk[:, :, slot, :], at.z[:, :, bass.ds(i * per + col, HD)]).then_inc(staged[hh], 16)
            if at.gated:
                some(sp, pv_mm, last_use)
                sp.dma_start(stv[:, hh, :], vcmp[:, bass.ds(i, 1), :].rearrange("n a d -> n (a d)"))\
                    .then_inc(staged[hh], 16)
            some(sp, max_done, last_use)
            sp.dma_start(bias[:, hh].rearrange("p t k -> p (t k)"),
                         at.table[bass.ds(i + at.table0, 1), :, hh * 512:(hh + 1) * 512].rearrange("a p n -> (a p) n"))\
                .then_inc(bias_in[hh], 16)

    def pool_mask(pool, at, i):
        for hh in range(4):
            pool.wait_ge(bias_in[hh], i * 16 + (at.round0 + 1) * 16)
            pool.tensor_tensor(bias[:, hh], bias[:, hh], mask3[:, :].unsqueeze(1).broadcast_to([P, TOK, S]), ALU.add)\
                .then_inc(bias_ok, 1)

    def pe_qk(pe, at, i, u):
        r, hh, kk = u % 2, at.units[u][1], at.units[u][2]
        pe.wait_ge(staged[hh], at.in_slot(i))
        some(pe, qk_ev, at.U(i, u - 1))
        for t in range(TOK):
            mm = pe.transpose(tp[r][:, t * P:(t + 1) * P], stq[:, t, hh, :], ident[:, :])
        if kk is not None:
            for t in range(TOK):
                mm = pe.transpose(tp[r][:, S + t * P:S + (t + 1) * P], stk[:, t, kk, :], ident[:, :])
        mm.then_inc(qk_tp, 1)

    def pe_scores(pe, at, i, u):
        r, w = u % 2, at.units[u][0]
        pe.wait_ge(qk_ev, at.U(i, u + 1))
        some(pe, max_done, at.U(i, u - 1))
        for t in range(TOK):
            rhs = qkT[:, r, S:2 * S] if at.full[u] else kcmpT[:, bass.ds(i * NCMP, NCMP)]
            mm = pe.matmul(pa[:, r, t * S:t * S + w], qkT[:, r, t * P:(t + 1) * P], rhs, start=True, stop=True)
        mm.then_inc(s_mm, 1)

    def pe_turn_p(pe, at, i, u):
        r = u % 2
        if at.full[u]:
            pe.wait_ge(exp_done, at.U(i, u + 1))
        else:
            pe.wait_ge(pmask, at.M(i, u + 1))
        some(pe, p_ev, at.U(i, u - 1))
        for t in range(TOK):
            if at.full[u]:
                for kb in range(S // P):
                    mm = pe.transpose(pa[:, 2 + r, kb * S + t * P:kb * S + (t + 1) * P],
                                      prob[:, r, t, kb * P:(kb + 1) * P], ident[:, :])
            else:
                mm = pe.transpose(pa[0:NCMP, 2 + r, t * P:(t + 1) * P], prob[:, r, t, 0:NCMP], ident[:, :])
        mm.then_inc(p_tp, 1)

    def pe_apply(pe, at, i, u):
        r = u % 2
        pe.wait_ge(p_ev, at.U(i, u + 1))
        some(pe, y_done, at.U(i, u - 1))
        for t in range(TOK):
            if at.full[u]:
                c0, per = at.units[u][3]
                for kb in range(S // P):
                    mm = pe.matmul(acc[r][:, t * P:(t + 1) * P], prT[:, r, kb, t * P:(t + 1) * P],
                                   at.z[:, kb, bass.ds(i * per + c0, HD)], start=(kb == 0), stop=(kb == S // P - 1))
            else:
                mm = pe.matmul(acc[r][:, t * P:(t + 1) * P], prT[0:NCMP, r, 0, t * P:(t + 1) * P],
                               stv[:, at.units[u][1], :], start=True, stop=True)
        mm.then_inc(pv_mm, 1)

    def act_qk(act, at, i, u):
        r = u % 2
        w = 2 * S if at.full[u] else S
        act.wait_ge(qk_tp, at.U(i, u + 1))
        some(act, s_mm, at.U(i, u - 1))
        act.activation(qkT[:, r, 0:w], tp[r][:, 0:w], ACT.Copy, scale=QSCALE ** 0.5).then_inc(qk_ev, 1)

    def act_exp(act, at, i, u):
        r, w = u % 2, at.units[u][0] + (1 if at.sink else 0)
        act.wait_ge(neg_done, at.U(i, u + 1))
        some(act, rden_done, at.U(i, u - 1))
        for t in range(TOK):
            e = act.activation(prob[:, r, t, 0:w], prob[:, r, t, 0:w], ACT.Exp, bias=small[:, 1, r, t:t + 1],
                               accum_out=small[:, 2, r, t:t + 1])
        e.then_inc(exp_done, 1)

    def act_turn_p(act, at, i, u):
        r = u % 2
        act.wait_ge(p_tp, at.U(i, u + 1))
        some(act, pv_mm, at.U(i, u - 1))
        if at.full[u]:
            act.activation(prT[:, r].rearrange("p a b -> p (a b)"), pa[:, 2 + r, :], ACT.Copy).then_inc(p_ev, 1)
        else:
            act.activation(prT[0:NCMP, r, 0, :], pa[0:NCMP, 2 + r, 0:S], ACT.Copy).then_inc(p_ev, 1)

    def dve_max(dve, at, i, u):
        w, hh, r = at.units[u][0], at.units[u][1], u % 2
        dve.wait_ge(s_mm, at.U(i, u + 1))
        some(dve, p_tp, at.U(i, u - 1))
        if at.masked:
            dve.wait_ge(bias_ok, i * 4 + (hh + 1))
        else:
            dve.wait_ge(bias_in[hh], i * 16 + (at.round0 + 1) * 16)
        sink = sinks[:, bass.ds(i * 4 + hh, 1)] if at.sink else None
        if at.sink:
            for t in range(TOK):
                dve.tensor_copy(prob[:, r, t, S:S + 1], sink)
        if at.full[u]:
            dve.memset(small[:, 5, r], 0.0)
            for t in range(TOK):
                m = dve.tensor_tensor_reduce(prob[:, r, t, 0:w], pa[:, r, t * S:t * S + w], bias[:, hh, t, :],
                                             1.0, -3.0e38, ALU.add, ALU.max, small[:, 0, r, t:t + 1])
            m.then_inc(max_done, 1)
        else:
            dve.tensor_tensor(prob[:, r, :, 0:w], pa[:, r, :].rearrange("p (t k) -> p t k", t=TOK)[:, :, 0:w],
                              bias_c[:, bass.ds(i * 4 + hh, 1), :, :].rearrange("p a t n -> p (a t) n"),
                              ALU.add).then_inc(biased, 1)
            dve.wait_ge(biased, at.M(i, u + 1))
            dve.tensor_reduce(small[:, 0, r], prob[:, r, :, 0:w], AX_X, ALU.max).then_inc(max_done, 1)
        dve.wait_ge(max_done, at.U(i, u + 1))
        some(dve, exp_done, at.U(i, u - 1))
        if at.sink:
            dve.tensor_scalar(small[:, 1, r], small[:, 0, r], sink, -1.0, ALU.max, ALU.mult).then_inc(neg_done, 1)
        else:
            dve.tensor_scalar(small[:, 1, r], small[:, 0, r], -1.0, None, ALU.mult).then_inc(neg_done, 1)

    def dve_factor(dve, at, i, u):
        r = u % 2
        dve.wait_ge(exp_done, at.U(i, u + 1))
        if not at.full[u]:
            dve.tensor_tensor(prob[:, r, :, 0:NCMP], prob[:, r, :, 0:NCMP], valid_c[:, :, :], ALU.mult)\
                .then_inc(pmask, 1)
        some(dve, y_done, at.U(i, u - 1))
        dve.reciprocal(small[:, 3, r], small[:, 2, r]).then_inc(rden_done, 1)
        if at.gated:
            gate = z1[:, :, bass.ds(i * 4 + (C_GATES + at.units[u][4] * NH + at.units[u][1]), 1)]
            dve.wait_ge(rden_done, at.U(i, u + 1))
            dve.tensor_tensor(small[:, 4, r], small[:, 3, r], gate.rearrange("p t a -> p (t a)"), ALU.mult)\
                .then_inc(coef_done, 1)

    def dve_y(dve, at, i, u):
        r, hh = u % 2, at.units[u][1]
        begins = u % at.per_head == 0
        dve.wait_ge(pv_mm, at.U(i, u + 1))
        if at.gated:
            dve.wait_ge(coef_done, at.U(i, u + 1))
            if not begins:
                dve.wait_ge(y_done, at.U(i, u))
        else:
            dve.wait_ge(rden_done, at.U(i, u + 1))
        for t in range(TOK):
            y = at.z[:, t, bass.ds(i * 512 + (at.y_col + hh * HD), HD)]
            o = acc[r][:, t * P:(t + 1) * P]
            if not at.gated:
                gate = at.z[:, t, bass.ds(i * 512 + (at.silu_col + hh * HD), HD)]
                d = dve.scalar_tensor_tensor(out=y, in0=o, scalar=small[:, 3, r, t:t + 1], in1=gate,
                                             op0=ALU.mult, op1=ALU.mult)
            elif begins:
                d = dve.tensor_scalar(y, o, small[:, 4, r, t:t + 1], None, ALU.mult)
            else:
                d = dve.scalar_tensor_tensor(out=y, in0=o, scalar=small[:, 4, r, t:t + 1], in1=y,
                                             op0=ALU.mult, op1=ALU.add)
        d.then_inc(y_done, 1)

    def in_rounds(eng, at, stages):
        def steps(i, first, last, carried):
            for s in range(first, last):
                for lag, stage in stages:
                    u = s - lag
                    if 0 <= u < at.n:
                        stage(eng, at, i + 1 if carried else i, u)
                    elif u < 0 and carried:
                        stage(eng, at, i, u + at.n)
        steps(0, 0, at.n, False)
        with eng.Fori(0, at.rounds - 1) as i:
            steps(i, 0, at.n, True)
        steps(at.rounds - 1, at.n, at.n + 3, False)

    def pe_attention(pe, at):
        in_rounds(pe, at, [(0, pe_qk), (1, pe_scores), (2, pe_turn_p), (3, pe_apply)])

    def act_attention(act, at):
        in_rounds(act, at, [(0, act_qk), (2, act_turn_p), (1, act_exp)])

    def dve_attention(dve, at):
        in_rounds(dve, at, [(2, dve_factor), (1, dve_max), (3, dve_y)])

    def each_round(eng, at, body):
        body(eng, at, 0)
        with eng.Fori(1, at.rounds) as i:
            body(eng, at, i)



    def act_splits(act, C, tr=None, c=None):
        for n in range(AHEAD, AHEAD + GT):
            if n == AHEAD + 2 and tr is not None:
                act_turn(act, tr, c)
            split_act(act, C, n)

    def dve_splits(dve, C, tr=None, c=None):
        for n in range(AHEAD, AHEAD + GT):
            if n == AHEAD + 2 and tr is not None:
                dve_turn(dve, tr, c)
            split_dve(dve, C, n)

    def act_product(act, name, ends, first=None, last=False, turn=None, turn0=None, after=None):
        C0, A0 = CHUNK0[name], ACC0[name]
        if first:
            split_act(act, C0, AHEAD)
            first()
            for n in range(AHEAD + 1, AHEAD + GT):
                split_act(act, C0, n)
        else:
            act_splits(act, C0, turn0, NCH - 1)
        if after:
            after()
        c = 0
        for count, end in ends:
            if c == 0:
                if end:
                    end(C0, A0, 0)
                c, count = 1, count - 1
            if last and c + count == dict(ORDER)[name]:
                count -= 1
            if count:
                with act.Fori(c - 1, c + count - 1) as j:
                    act_splits(act, j + (C0 + 1), turn, j)
                    if end:
                        end(j + (C0 + 1), j + (A0 + 1), j + 1)
            c += count
        if last:
            split_act(act, C0 + c, AHEAD)
            if ends[-1][1]:
                ends[-1][1](C0 + c, A0 + c, c)

    def dve_product(dve, name, end=None, first=None, last=False, turn=None, turn0=None, after=None):
        C0, A0, n_chunks = CHUNK0[name], ACC0[name], dict(ORDER)[name]
        if first:
            split_dve(dve, C0, AHEAD)
            first()
            for n in range(AHEAD + 1, AHEAD + GT):
                split_dve(dve, C0, n)
        else:
            dve_splits(dve, C0, turn0, NCH - 1)
        if after:
            after()
        if end:
            end(C0, A0, 0)
        stop = n_chunks - (1 if last else 0)
        if stop > 1:
            with dve.Fori(0, stop - 1) as j:
                dve_splits(dve, j + (C0 + 1), turn, j)
                if end:
                    end(j + (C0 + 1), j + (A0 + 1), j + 1)
        if last:
            split_dve(dve, C0 + stop, AHEAD)
            end(C0 + stop, A0 + stop, stop)

    def pe_product(pe, name, lhs, src=None, run=None, ready=None, x_ready=None, turn=None, turn0=None,
                   x_tiles=False):
        C0, A0, n_chunks = CHUNK0[name], ACC0[name], dict(ORDER)[name]
        if src is not None:
            pe_first(pe, C0, A0, TILE0[run], lhs, src, ready)
        else:
            if x_ready:
                x_ready()
            for n in range(GT):
                if x_tiles:
                    pe.wait_ge(tlo_done, GT * (n + 1))
                if turn0 and n == GT - 1:
                    pe.wait_ge(tlo_done, turn0.T0 + KT)
                pe_group(pe, C0, A0, n, lhs, turn=pe_turn(pe, turn0, NCH - 1) if turn0 else None)
        if n_chunks > 1:
            with pe.Fori(0, n_chunks - 1) as j:
                pe_chunk(pe, j + (C0 + 1), j + (A0 + 1), lhs, turn=pe_turn(pe, turn, j) if turn else None)

    aT, bT = (aT_hi, aT_lo), (bT_hi, bT_lo)
    MLP_N = 4

    def freed(eng, name, n, t=None):
        for tt in (range(TOK) if t is None else [t]):
            eng.wait_ge(acc_free[tt], ACC0[name] + n)

    def by_residual(name, skip=0):
        def ready(pe, c):
            for t in range(TOK):
                pe.wait_ge(acc_free[t], c + (ACC0[name] + skip + 1))
        return ready

    def by_gate(layer):
        def ready(pe, c):
            pe.wait_ge(h_done, c * 2 + (layer * 8 + 2))
        return ready

    turn_out = [Turn("ab_out", bT, 1, by_residual("ab_out")), Turn("c_out", bT, 4, by_residual("c_out"))]
    turn_mlp = [Turn("mlp0", bT, 2, by_residual("mlp0", 28)), Turn("mlp1", bT, 5, by_residual("mlp1", 28))]
    turn_gate = Turn("gate0", aT, 3, by_gate(0))
    out_name = ("ab_out", "c_out")

    def after_residual(pe, name, skip=0):
        def ready(kt):
            if kt % GT == 0:
                freed(pe, name, skip + kt // GT + 1)
        return ready

    def once(wait):
        def ready(kt):
            if kt == 0:
                wait()
        return ready


    def hidden(l, j):
        def ready(pe, c):
            pe.wait_ge(hid_done, c * 2 + j * 8 + (l * 32 + 2))
        tr = Turn(f"hidden{l}", aT, None, ready)
        tr.T0 = j * KT + tr.T0
        return tr

    def quarters(eng, body):
        with eng.Fori(0, MLP_N - 1) as j:
            body(j, False)
        body(MLP_N - 1, True)

    def pe_mlp(pe, l):
        C0, A0 = CHUNK0[f"mlp{l}"], ACC0[f"mlp{l}"]

        def quarter(j, last):
            tr = hidden(l, j)
            pe_chunk(pe, j * 8 + C0, j * 8 + A0, bT)
            with pe.Fori(0, NCH - 1) as c:
                pe_chunk(pe, c + j * 8 + (C0 + 1), c + j * 8 + (A0 + 1), bT, turn=pe_turn(pe, tr, c))
            for n in range(GT):
                if n == GT - 1:
                    pe.wait_ge(tlo_done, tr.T0 + KT)
                pe_group(pe, j * 8 + (C0 + NCH), j * 8 + (A0 + NCH), n, aT, turn=pe_turn(pe, tr, NCH - 1))
            with pe.Fori(0, NCH - 1) as c:
                pe_chunk(pe, c + j * 8 + (C0 + NCH + 1), c + j * 8 + (A0 + NCH + 1), aT,
                         turn=pe_turn(pe, turn_mlp[l], c) if last else None)
        quarters(pe, quarter)

    def act_mlp(act, l, m):
        C0, A0 = CHUNK0[f"mlp{l}"], ACC0[f"mlp{l}"]

        def relu(j, c):
            act_project(act, c + j * 8 + C0, c + j * 8 + A0, m, lambda t: part[:, t, :], ACT.Relu)

        def quarter(j, last):
            tr = hidden(l, j)
            act_splits(act, j * 8 + C0)
            relu(j, 0)
            with act.Fori(0, NCH - 1) as c:
                act_splits(act, c + j * 8 + (C0 + 1), tr, c)
                relu(j, c + 1)
            act_splits(act, j * 8 + (C0 + NCH), tr, NCH - 1)
            if last:
                act_keep(act, A0 + 28, 0)
            with act.Fori(0, NCH - 1) as c:
                act_splits(act, c + j * 8 + (C0 + NCH + 1), turn_mlp[l] if last else None, c)
                if last:
                    act_keep(act, c + (A0 + 29), c * NW + NW)
        quarters(act, quarter)

    def pool_mlp(pool, l):
        A0 = ACC0[f"mlp{l}"]
        with pool.Fori(0, MLP_N) as j:
            with pool.Fori(0, NCH) as c:
                for t in range(TOK):
                    pool.wait_ge(acc_free[t], c + j * 8 + (A0 + 1))
                    pool.tensor_tensor(part[:, t, :], part[:, t, :], part[:, t, :], ALU.mult).then_inc(hid_done, 1)

    def dve_mlp(dve, l):
        C0, A0 = CHUNK0[f"mlp{l}"], ACC0[f"mlp{l}"]

        def quarter(j, last):
            tr = hidden(l, j)
            dve_splits(dve, j * 8 + C0)
            with dve.Fori(0, NCH - 1) as c:
                dve_splits(dve, c + j * 8 + (C0 + 1), tr, c)
            dve_splits(dve, j * 8 + (C0 + NCH), tr, NCH - 1)
            dve_residual(dve, j * 8 + (C0 + NCH), j * 8 + (A0 + NCH), 0, last)
            with dve.Fori(0, NCH - 1) as c:
                dve_splits(dve, c + j * 8 + (C0 + NCH + 1), turn_mlp[l] if last else None, c)
                dve_residual(dve, c + j * 8 + (C0 + NCH + 1), c + j * 8 + (A0 + NCH + 1), c * NW + NW, last)
        quarters(dve, quarter)

    def act_proj(act, l, m):
        C0, A0 = CHUNK0[f"proj{l}"], ACC0[f"proj{l}"]
        act.wait_ge(p_in, 16 * (l + 1))
        act.activation(pT_hi[:, :, :], pT[:, :, :], ACT.Copy).then_inc(p_hi, 1)
        for n in range(NCH):
            split_act(act, C0, AHEAD + n)
            if n == 1:
                act_turn(act, turn_out[l], NCH - 1)
            if n == 2:
                act_norm(act, m, lambda: act.wait_ge(kept, 8 + 24 * l))
            if n == 3:
                act_root(act, m)
            for t in range(TOK):
                if t == 0:
                    act.wait_ge(acc0_done, A0 + n + 1)
                else:
                    act.wait_ge(group_used, C0 * GT + n + 1)
                act.activation(proj[:, t, n * NW:(n + 1) * NW], acc[t][:, :], ACT.Copy).then_inc(acc_free[t], 1)

    def dve_proj(dve, l, m):
        dve.wait_ge(p_hi, l + 1)
        dve.tensor_tensor(pT_lo[:, :, :], pT[:, :, :], pT_hi[:, :, :].bitcast(F32), ALU.subtract).then_inc(p_lo, 1)
        for n in range(NCH):
            if n == 1:
                dve_turn(dve, turn_out[l], NCH - 1)
            split_dve(dve, CHUNK0[f"proj{l}"], AHEAD + n)
        dve_means(dve, m, 1e-6)
        dve_rstd(dve, m)

    def pe_proj(pe, l):
        C0, A0 = CHUNK0[f"proj{l}"], ACC0[f"proj{l}"]
        pe.wait_ge(p_lo, l + 1)
        for n in range(NCH):
            pe.wait_ge(split_done, C0 * GT + n + 1)
            for t in range(TOK):
                pe.wait_ge(acc_free[t], A0 + n)
                for kt in range(2):
                    for a, w in ((pT_hi, w_hi), (pT_hi, w_lo), (pT_lo, w_hi)):
                        mm = pe.matmul(acc[t][:, :], a[:, kt, t * P:(t + 1) * P], w[:, n, kt, :],
                                       start=(kt == 0 and a is pT_hi and w is w_hi), stop=(kt == 1 and a is pT_lo))
                if t == 0:
                    mm.then_inc(acc0_done, 1)
            mm.then_inc(group_used, 1)
            if n == 1:
                for i in range(GT):
                    pe_turn(pe, turn_out[l], NCH - 1)(i)
        pe.wait_ge(tlo_done, turn_out[l].T0 + KT)

    def act_gate_end(act, l, m):
        def end(C, A_, c):
            if not isinstance(c, int) or c > 0:
                act.wait_ge(h_done, c * 2 + l * 8)
            act_project(act, C, A_, m, lambda t: gpart[:, t, :], ACT.Sigmoid)
            if l == 0:
                for t in range(TOK):
                    act.wait_ge(h_done, c * 2 + (t + 1))
                    act.activation(h[:, t, bass.ds(c * NW, NW)], part[:, t, :], ACT.Copy).then_inc(kept, 1)
        return end

    def pool_gate(pool, l):
        A0 = ACC0[f"gate{l}"]
        with pool.Fori(0, NCH) as c:
            for t in range(TOK):
                pool.wait_ge(acc_free[t], c + (A0 + 1))
                pool.tensor_tensor(gpart[:, t, :], gpart[:, t, :], proj[:, t, bass.ds(c * NW, NW)], ALU.mult)\
                    .then_inc(gp_done, 1)

    def dve_gate_end(dve, l):
        def end(C, A_, c):
            for t in range(TOK):
                dve.wait_ge(gp_done, c * 2 + (l * 8 + t + 1))
                old = h[:, t, bass.ds(c * NW, NW)]
                dve.tensor_tensor(part[:, t, :] if l == 0 else old, old, gpart[:, t, :], ALU.add).then_inc(h_done, 1)
        return end

    def residual_end(dve, to_part=False):
        return lambda C, A_, c: dve_residual(dve, C, A_, c * NW, to_part)

    def keep_end(act):
        return lambda C, A_, c: act_keep(act, A_, c * NW)

    def put(z, base=0):
        return lambda c: (lambda t: z[:, t, bass.ds(c * NW + base, NW)])

    def project_end(act, m, z, func=ACT.Copy):
        return lambda C, A_, c: act_project(act, C, A_, m, put(z)(c), func)

    def act_norm(act, m, wait):
        wait()
        if m > 0:
            act.wait_ge(ms_done, m)
        for t in range(TOK):
            if t > 0:
                act.wait_ge(sq_done, TOK * m + t)
            act.activation(pa[:, :, :].rearrange("p a b -> p (a b)"), h[:, t, :], ACT.Square,
                           accum_out=stat[:, 0, t:t + 1]).then_inc(sq_done, 1)

    block = ctx.enter_context(nc.Block())

    @block.sync
    def _(sp):
        for g in range(RAW):
            sp.dma_start(raw[:, g].rearrange("p a b -> p (a b)"), wstream[g]).then_inc(landed[g], 16)

        def stream(first, last):
            with sp.Fori(first, last) as i:
                for g in range(RAW):
                    sp.wait_ge(split_done, i * RAW + (g + 1 - RAW))
                    sp.dma_start(raw[:, g].rearrange("p a b -> p (a b)"),
                                 wstream[bass.ds(i * RAW + g, 1)].rearrange("g p n -> (g p) n"))\
                        .then_inc(landed[g], 16)

        at1, at2, at3 = (CHUNK0[x] * GT // RAW + 2 for x in ("c_out", "ab2_out", "c2_out"))
        stream(1, at1)
        freed(sp, "c_tail", 1)
        sp.wait_ge(cmp_ev, 2)
        each_round(sp, attn1, sp_round)
        stream(at1, at2)
        freed(sp, "ab2_in", 13)
        each_round(sp, attn2a, sp_round)
        each_round(sp, attn2b, sp_round)
        stream(at2, at3)
        freed(sp, "c2_in", 16)
        sp.wait_ge(rpb_out, 16 * RPB_DMAS)
        each_round(sp, attn3, sp_round)
        stream(at3, NC * GT // RAW)
        sp.wait_ge(fin_done, 2)
        sp.dma_start(out.rearrange("b (t p) d -> p (b t) d", p=P), h[:, :, :]).then_inc(out_done, 16)
        sp.wait_ge(out_done, 16)
        sp.wait_ge(rpb_out, 16 * RPB_DMAS)

    @block.gpsimd
    def _(pool):
        pool.memset(bd[:, :, :, :], 0.0).then_inc(bd_zero, 1)
        pool.wait_ge(bd_zero, 1)
        for n, w in enumerate((A["w_r"], A["w_i"])):
            for half in range(2):
                pool.dma_start(bd[half * 64:half * 64 + 64, n, :, half * 64:half * 64 + 64],
                               w.rearrange("(j a) i o -> a i j o", a=2)[half]).then_inc(bd_in, 16)
        pool.memset(uT[:, :, 0:PADP], 0.0).then_inc(pads_zero, 1)
        pool.wait_ge(m_ev, 2 * LT)
        pool.wait_ge(pads_zero, 1)
        pool.wait_ge(lru_dve, 2 * LRU_STEPS)
        N = PADP + S
        pool.tensor_tensor(pw0[:, :, 1:N], uT[:, :, 1:N], uT[:, :, 0:N - 1], ALU.add).then_inc(pool_step, 1)
        pool.wait_ge(pool_step, 1)
        pool.tensor_tensor(pw1[:, :, 3:N], pw0[:, 2:8, 3:N], pw0[:, 2:8, 1:N - 2], ALU.add).then_inc(pool_step, 1)
        pool.wait_ge(pool_step, 2)
        pool.tensor_tensor(pw0[:, 4:8, 7:N], pw1[:, 2:6, 7:N], pw1[:, 2:6, 3:N - 4], ALU.add).then_inc(pool_step, 1)
        pool.wait_ge(pool_step, 3)
        pool.tensor_tensor(pw1[:, 4:6, 15:N], pw0[:, 6:8, 15:N], pw0[:, 6:8, 7:N - 8], ALU.add).then_inc(pool_step, 1)
        pool.wait_ge(pool_step, 4)
        for g, s in enumerate((pw0[:, 0:2], pw1[:, 0:2], pw0[:, 4:6], pw1[:, 4:6])):
            win = 2 << g
            pool.tensor_tensor(s[:, :, PADP:2 * PADP], s[:, :, PADP:2 * PADP],
                               invcnt[:, g, :].unsqueeze(1).broadcast_to([P, 2, PADP]), ALU.mult).then_inc(pool_step, 1)
            pool.tensor_scalar(s[:, :, 2 * PADP:], s[:, :, 2 * PADP:], 1.0 / win, None, ALU.mult).then_inc(pool_step, 1)
            pool.wait_ge(pool_step, 4 + 3 * g + 2)
            pool.tensor_tensor(uT[:, 2 * g:2 * g + 2, PADP:], s[:, :, PADP:], uT[:, 2 * g:2 * g + 2, PADP:],
                               ALU.subtract).then_inc(pool_step, 1)
        pool.wait_ge(mix_lo, 6)
        pool.wait_ge(pool_mm, 8)
        pool.dma_start(pT[:, :, :], A["pT"][0].rearrange("(k p) s -> p k s", p=P)).then_inc(p_in, 16)
        b3 = A["bias3"]
        for hh in range(NH):
            for r in range(4):
                t, half = r // 2, r % 2
                src = bass.AP(tensor=A["rpb"].tensor, offset=(hh * 15 + 7 - r) * 64 * 128 + 63,
                              ap=[[127, 64], [64 * 128, 4], [1, 64]])
                dst = b3[hh // 4, half * 64:half * 64 + 64, bass.ds((hh % 4) * 512 + t * S, S)]\
                    .rearrange("p (k c) -> p k c", k=4)
                pool.dma_start(dst, src).then_inc(rpb_out, 16)
        pool_mlp(pool, 0)
        pool_gate(pool, 0)
        freed(pool, "c_in", 1)
        pool.dma_start(cw2[:, 0], A["w2_k"].rearrange("(f p) d -> p f d", p=P)).then_inc(cmp_in, 16)
        pool.dma_start(cw2[:, 1], A["w2_v"].rearrange("(f p) d -> p f d", p=P)).then_inc(cmp_in, 16)
        pool.dma_start(posT[:, :, :], A["posT"].rearrange("a d l -> d a l")).then_inc(cmp_in, 16)
        pool.wait_ge(cmp_in, 48)
        freed(pool, "c_tail", 1)
        pool.memset(blk[:, :, NKV * NCMP:], 0.0).then_inc(blk_done, 1)
        for kv in range(2):
            pool.wait_ge(c_ev, kv * 4 + 4)
            if kv == 1:
                pool.wait_ge(blk_lo_done, 1)
            for g in range(NKV):
                v = cT[:, kv, g, :].rearrange("p (m j) -> p j m", j=16)
                for a in range(2):
                    b = pool.tensor_tensor(
                        blk[:, 16 * a:16 * a + 16, g * NCMP:(g + 1) * NCMP], v[:, :, a:a + NCMP],
                        posT[:, kv, 16 * a:16 * a + 16].unsqueeze(2).broadcast_to([P, 16, NCMP]), ALU.add)
            b.then_inc(blk_done, 1)
        pool.wait_ge(tlo_done, TILE0["y1"] + KT)
        pool.dma_start(pT[:, :, :], A["pT"][1].rearrange("(k p) s -> p k s", p=P)).then_inc(p_in, 16)
        pool_mlp(pool, 1)
        pool_gate(pool, 1)
        pool.dma_start(gfull[:, :], A["g1"]).then_inc(g_in, 16)
        each_round(pool, attn3, pool_mask)
        pool.wait_ge(tlo_done, TILE0["c2_out"] + KT)
        pool.dma_start(gfull[:, :], A["g2"]).then_inc(g_in, 16)

    @block.scalar
    def _(act):
        act.dma_start(xT[:, :, :], A["xT"].rearrange("(k p) s -> p k s", p=P)).then_inc(x_in, 16)
        act.dma_start(gains[:, :, :], A["gains"]).then_inc(x_in, 16)
        loads = [(ident[:, :], A["ident"]), (h[:, :, :], A["x"].rearrange("b (t p) d -> p (b t) d", p=P)),
                 (vecs[:, :, :], A["vecs"]), (invcnt[:, :, :], A["invcnt"]), (pool_w[:, :, :], A["pool_w"]),
                 (sinks[:, :], A["sinks"]), (bias_c[:, :, :, :], A["bias_c"]), (valid_c[:, :, :], A["valid_c"]),
                 (mask3[:, :], A["mask3"])]
        assert len(loads) == LOADS
        for dst, src in loads:
            act.dma_start(dst, src).then_inc(const_in, 16)
        for n in range(AHEAD):
            split_act(act, 0, n)
            if n == 0:
                act.wait_ge(x_in, 32)
                for kt in range(KT):
                    act.activation(aT_hi[:, kt], xT[:, kt], ACT.Copy, scale=gains[:, 0, kt:kt + 1]).then_inc(thi_done, 1)

        def first():
            act.wait_ge(const_in, 16 * LOADS)
            act_norm(act, 0, lambda: None)
            act.wait_ge(dve_chain, 1)
            act.activation(soft[:, 1], soft[:, 0], ACT.Exp, scale=-1.0).then_inc(soft_exp, 1)
            act_root(act, 0)
        def mixer_tiles(c):
            for i in range(GT):
                k = GT * c + i
                act.wait_ge(m_tp, k + 1)
                dst = xr[:, k, PADC:] if k < LT else uT[:, k - LT, PADP:]
                act.activation(dst, tp[k % 2][:, 0:S], ACT.Copy).then_inc(m_ev, 1)

        def decays(half):
            for q in range(GT):
                j = GT * half + q
                act.wait_ge(gates_mm, j + 1)
                act.activation(rg[:, j], pa[:, q, 0:S], ACT.Sigmoid, bias=vecs[:, 5, j:j + 1])
                act.activation(ig[:, j], pa[:, q, S:2 * S], ACT.Sigmoid, bias=vecs[:, 6, j:j + 1]).then_inc(gates_sg, 1)
            act.wait_ge(gates_sg, GT * (half + 1))
            tiles = range(GT * half, GT * (half + 1))
            for j in tiles:
                e = act.activation(th[:, j], rg[:, j], ACT.Tanh, scale=soft[:, 2, j:j + 1])
            e.then_inc(tanh_done, 1)
            for j in tiles:
                e = act.activation(rg[:, j], rg[:, j], ACT.Exp, scale=soft[:, 3, j:j + 1])
            e.then_inc(decay_done, 1)

        def root(half):
            act.wait_ge(lru_dve, LRU_STEPS * half + 3)
            t = th[:, GT * half:GT * (half + 1), :]
            act.activation(t, t, ACT.Sqrt, scale=2.0).then_inc(lru_root, 1)

        def round_lru(half):
            act.wait_ge(gated, GT * (half + 1))
            act.wait_ge(group_used, CHUNK0["ab_in"] * GT + 5 * GT + 3 + half)
            act.activation(aT_hi[:, LT + GT * half:LT + GT * (half + 1), :], xc[:, GT * half:GT * (half + 1), :],
                           ACT.Copy).then_inc(mix_hi, 1)
        C0, A0 = CHUNK0["ab_in"], ACC0["ab_in"]
        for c in range(6):
            split_act(act, C0 + c, AHEAD)
            if c == 0:
                first()
            split_act(act, C0 + c, AHEAD + 1)
            if 1 <= c <= 4:
                mixer_tiles(c - 1)
            split_act(act, C0 + c, AHEAD + 2)
            if c in (2, 3):
                decays(c - 2)
            if c in (3, 4):
                root(c - 3)
            split_act(act, C0 + c, AHEAD + 3)
            if c > 0:
                act.wait_ge(m_tp, GT * c)
            act_project(act, C0 + c, A0 + c, 0, lambda t: part[:, t, :], ACT.Copy if c < 4 else ACT.Gelu_apprx_tanh)
            if c == 5:
                for g in range(4):
                    act.wait_ge(pool_mm, 2 * g + 2)
                    act.wait_ge(group_used, (C0 + 5) * GT + g // 2 + 1)
                    for j in (2 * g, 2 * g + 1):
                        e = act.activation(aT_hi[:, j, :], pa[:, g, (j % 2) * S:(j % 2 + 1) * S], ACT.Copy,
                                           scale=vecs[:, 8, j:j + 1])
                    e.then_inc(mix_hi, 1)
        round_lru(0)
        C0, A0 = CHUNK0["ab_out"], ACC0["ab_out"]
        for n in range(AHEAD, AHEAD + GT):
            if n == AHEAD + 2:
                round_lru(1)
            split_act(act, C0, n)
        act_keep(act, A0, 0)
        with act.Fori(0, NCH - 1) as j:
            act_splits(act, j + (C0 + 1), turn_out[0], j)
            act_keep(act, j + (A0 + 1), j * NW + NW)
        act_proj(act, 0, 1)
        act_mlp(act, 0, 1)

        def norm(m, wait):
            def after():
                act_norm(act, m, wait)
                act_root(act, m)
            return after

        def y_tiles(run):
            return lambda: act_tiles(act, TILE0[run], aT_hi, None)
        act_product(act, "gate0", [(4, act_gate_end(act, 0, 2))], turn=turn_gate, turn0=turn_mlp[0],
                    after=norm(2, lambda: act.wait_ge(kept, 16)))
        act_product(act, "c_in", [(10, project_end(act, 3, z1))], turn0=turn_gate,
                    after=norm(3, lambda: act.wait_ge(kept, 24)))
        C, A_ = CHUNK0["c_tail"], ACC0["c_tail"]
        for n in range(AHEAD, AHEAD + GT):
            split_act(act, C, n)
        act_project(act, C, A_, 3, lambda t: z1[:, t, C_GATES:W_C], ACT.Sigmoid, width=W_C - C_GATES)
        for kv in range(2):
            C, A_ = CHUNK0[("cmp_k", "cmp_v")[kv]], ACC0[("cmp_k", "cmp_v")[kv]]
            if kv == 1:
                act.wait_ge(group_used, C * GT)
            act.wait_ge(blk_done, 2 + kv)
            act.activation(blk_hi[:, :, :], blk[:, :, :], ACT.Copy).then_inc(blk_hi_done, 1)
            for cc in range(2):
                for n in range(AHEAD, AHEAD + GT):
                    split_act(act, C + cc, n)
            act.wait_ge(group_used, (C + 2) * GT)
            if kv == 1:
                act.wait_ge(chid_tp, 1)
            act.activation(chid[:, :], acc[0][0:NKV * NCMP, :], ACT.Gelu_apprx_tanh).then_inc(chid_done, 1)
        act_attention(act, attn1)
        act_product(act, "c_out", [(4, keep_end(act))], y_tiles("y1"), turn=turn_out[1])
        act_proj(act, 1, 4)
        act_mlp(act, 1, 4)
        act_product(act, "gate1", [(4, act_gate_end(act, 1, 5))], turn0=turn_mlp[1],
                    after=norm(5, lambda: act.wait_ge(kept, 40)))
        act_norm(act, 6, lambda: act.wait_ge(h_done, 16))
        act_root(act, 6)

        def first():
            act_tiles(act, TILE0["ab2_in"], aT_hi, 6)
            act_norm(act, 7, lambda: act.wait_ge(fin_done, 1))
            act_root(act, 7)
        act_product(act, "ab2_in", [(9, project_end(act, 7, z2)), (4, project_end(act, 7, z2, ACT.Silu))], first)
        act_attention(act, attn2a)
        act_attention(act, attn2b)
        act_product(act, "ab2_out", [(4, None)], lambda: act_tiles(act, TILE0["ab2_out"], aT_hi, None))

        def first():
            act_tiles(act, TILE0["c2_in"], aT_hi, 7)
            act_norm(act, 8, lambda: freed(act, "ab2_out", 4))
            act_root(act, 8)
        act_product(act, "c2_in", [(12, project_end(act, 8, z3)), (4, project_end(act, 8, z3, ACT.Silu))], first)
        act_attention(act, attn3)
        act_product(act, "c2_out", [(4, None)], lambda: act_tiles(act, TILE0["c2_out"], aT_hi, None), last=True)
        act_norm(act, 9, lambda: freed(act, "c2_out", 4))
        act_root(act, 9)

    @block.vector
    def _(dve):
        chain = [0]

        def link(ins):
            chain[0] += 1
            ins.then_inc(dve_chain, 1)
            dve.wait_ge(dve_chain, chain[0])

        lam, mag, y, sp, neg = vecs[:, 7], soft[:, 0], soft[:, 1], soft[:, 2], soft[:, 3]
        for n in range(AHEAD):
            split_dve(dve, 0, n)
            if n == 0:
                dve.wait_ge(x_in, 32)
                for kt in range(KT):
                    dve.wait_ge(thi_done, kt + 1)
                    dve.scalar_tensor_tensor(out=aT_lo[:, kt], in0=xT[:, kt], scalar=gains[:, 0, kt:kt + 1],
                                             in1=aT_hi[:, kt].bitcast(F32), op0=ALU.mult, op1=ALU.subtract)\
                        .then_inc(tlo_done, 1)

        def first():
            dve.wait_ge(const_in, 16 * LOADS)
            link(dve.scalar_tensor_tensor(out=mag, in0=lam, scalar=-1.0, in1=lam, op0=ALU.mult, op1=ALU.max))
            dve_means(dve, 0, 1e-6)
            dve.wait_ge(soft_exp, 1)
            link(dve.tensor_scalar(sp, y, 2.0, None, ALU.add))
            link(dve.reciprocal(sp, sp))
            link(dve.tensor_tensor(y, y, sp, ALU.mult))
            link(dve.tensor_tensor(mag, y, y, ALU.mult))
            link(dve.tensor_scalar(sp, mag, 1.0 / 19, None, ALU.mult))
            for n in range(17, 1, -2):
                link(dve.scalar_tensor_tensor(out=sp, in0=sp, scalar=1.0 / n, in1=mag, op0=ALU.add, op1=ALU.mult))
            link(dve.scalar_tensor_tensor(out=sp, in0=sp, scalar=1.0, in1=y, op0=ALU.add, op1=ALU.mult))
            link(dve.tensor_scalar(mag, lam, -1.0, 0.0, ALU.mult, ALU.max))
            link(dve.scalar_tensor_tensor(out=sp, in0=sp, scalar=2.0, in1=mag, op0=ALU.mult, op1=ALU.add))
            link(dve.tensor_scalar(neg, sp, -8.0, None, ALU.mult))
            link(dve.tensor_scalar(sp, sp, 8.0, None, ALU.mult))
            dve_rstd(dve, 0)
        def conv(half):
            if half == 0:
                dve.wait_ge(m_ev, GT)
            else:
                dve.wait_ge(m_ev, 2 * GT)
            tiles = range(GT * half, GT * (half + 1))
            for k in range(4):
                for q, j in enumerate(tiles):
                    if k == 0:
                        dve.tensor_scalar(xc[:, j], xr[:, j, 0:S], vecs[:, 0, j:j + 1], vecs[:, 4, j:j + 1],
                                          ALU.mult, ALU.add).then_inc(conv_step, 1)
                    else:
                        dve.wait_ge(conv_step, 12 * half + GT * (k - 1) + q + 1)
                        d = dve.scalar_tensor_tensor(out=xc[:, j], in0=xr[:, j, k:k + S], scalar=vecs[:, k, j:j + 1],
                                                     in1=xc[:, j], op0=ALU.mult, op1=ALU.add)
                        d.then_inc(*((conv_done, 4) if k == 3 else (conv_step, 1)))

        def lru_inputs(half):
            a = slice(GT * half, GT * (half + 1))
            w = xr[:, a, 0:S]
            n = LRU_STEPS * half
            dve.wait_ge(tanh_done, half + 1)
            dve.wait_ge(conv_done, 4 * GT * (half + 1))
            dve.tensor_scalar(w, th[:, a, :], 1.0, None, ALU.add).then_inc(lru_dve, 1)
            dve.wait_ge(lru_dve, n + 1)
            dve.reciprocal(w, w).then_inc(lru_dve, 1)
            dve.wait_ge(lru_dve, n + 2)
            dve.tensor_tensor(th[:, a, :], th[:, a, :], w, ALU.mult).then_inc(lru_dve, 1)
            dve.wait_ge(gates_sg, GT * (half + 1))
            dve.tensor_tensor(ig[:, a, :], ig[:, a, :], xc[:, a, :], ALU.mult).then_inc(lru_dve, 1)

        def lru(half):
            a = slice(GT * half, GT * (half + 1))
            n = LRU_STEPS * half
            dve.wait_ge(lru_root, half + 1)
            dve.wait_ge(lru_dve, n + 4)
            dve.tensor_tensor(ig[:, a, :], ig[:, a, :], th[:, a, :], ALU.mult).then_inc(lru_dve, 1)
            dve.wait_ge(lru_dve, n + 5)
            dve.wait_ge(decay_done, half + 1)
            for j in range(GT * half, GT * (half + 1)):
                s = dve.tensor_tensor_scan(xc[:, j], rg[:, j], ig[:, j], 0.0, ALU.mult, ALU.add)
            s.then_inc(lru_dve, 1)

        def gate_tiles(half):
            dve.wait_ge(lru_dve, LRU_STEPS * (half + 1))
            for j in range(GT * half, GT * (half + 1)):
                dve.wait_ge(m_tp, 2 * LT + j + 1)
                dve.tensor_tensor(xc[:, j], tp[j % 2][:, 0:S], xc[:, j], ALU.mult).then_inc(gated, 1)

        def split_lru(half):
            dve.wait_ge(mix_hi, 5 + half)
            a, b = slice(GT * half, GT * (half + 1)), slice(LT + GT * half, LT + GT * (half + 1))
            dve.tensor_tensor(aT_lo[:, b, :], xc[:, a, :], aT_hi[:, b, :].bitcast(F32), ALU.subtract)\
                .then_inc(mix_lo, 1)
        C0 = CHUNK0["ab_in"]
        for c in range(6):
            split_dve(dve, C0 + c, AHEAD)
            if c == 0:
                first()
                link(dve.memset(xr[:, :, 0:PADC], 0.0))
            if c in (3, 4):
                lru_inputs(c - 3)
            split_dve(dve, C0 + c, AHEAD + 1)
            if c in (1, 2):
                conv(c - 1)
            if c == 5:
                gate_tiles(0)
            split_dve(dve, C0 + c, AHEAD + 2)
            if c in (3, 4):
                lru(c - 3)
            split_dve(dve, C0 + c, AHEAD + 3)
        for g in range(4):
            dve.wait_ge(mix_hi, g + 1)
            for j in (2 * g, 2 * g + 1):
                d = dve.scalar_tensor_tensor(out=aT_lo[:, j, :], in0=pa[:, g, (j % 2) * S:(j % 2 + 1) * S],
                                             scalar=vecs[:, 8, j:j + 1], in1=aT_hi[:, j, :].bitcast(F32),
                                             op0=ALU.mult, op1=ALU.subtract)
            d.then_inc(mix_lo, 1)
        split_lru(0)
        C0, A0 = CHUNK0["ab_out"], ACC0["ab_out"]
        for n in range(AHEAD, AHEAD + GT):
            if n == AHEAD + 2:
                gate_tiles(1)
                split_lru(1)
            split_dve(dve, C0, n)
        dve_residual(dve, C0, A0, 0, True)
        with dve.Fori(0, NCH - 1) as j:
            dve_splits(dve, j + (C0 + 1), turn_out[0], j)
            dve_residual(dve, j + (C0 + 1), j + (A0 + 1), j * NW + NW, True)
        dve_proj(dve, 0, 1)
        dve_mlp(dve, 0)

        def norm(m, eps=1e-6):
            def after():
                dve_means(dve, m, eps)
                dve_rstd(dve, m)
            return after

        def norm_first(name, gain, m, eps):
            def first():
                dve_tiles(dve, TILE0[name], aT_hi, aT_lo, gain)
                if m is not None:
                    dve_means(dve, m, eps)
                    dve_rstd(dve, m)
            return first
        dve_product(dve, "gate0", dve_gate_end(dve, 0), turn=turn_gate, turn0=turn_mlp[0], after=norm(2))
        dve_product(dve, "c_in", None, turn0=turn_gate, after=norm(3))
        for n in range(AHEAD, AHEAD + GT):
            split_dve(dve, CHUNK0["c_tail"], n)
        for n in range(8):
            dve.wait_ge(c_tp, n + 1)
            dve.tensor_copy(cT[:, n // 4, n % 4, :], tp[n % 2][:, 0:S]).then_inc(c_ev, 1)
        for kv in range(2):
            C, A_ = CHUNK0[("cmp_k", "cmp_v")[kv]], ACC0[("cmp_k", "cmp_v")[kv]]
            dve.wait_ge(blk_hi_done, kv + 1)
            dve.tensor_tensor(blk_lo[:, :, :], blk[:, :, :], blk_hi[:, :, :].bitcast(F32), ALU.subtract)\
                .then_inc(blk_lo_done, 1)
            for cc in range(2):
                for n in range(AHEAD, AHEAD + GT):
                    split_dve(dve, C + cc, n)
            dve.wait_ge(chid_tp, kv + 1)
            if kv == 1:
                dve.wait_ge(cmp_mm, 1)
            dve.tensor_copy(chidT[:, :, :], tp[0][:, 0:HID // P * NKV * NCMP]
                            .rearrange("p (f n) -> p f n", f=HID // P)).then_inc(chid_ev, 1)
            dve.wait_ge(cmp_mm, kv + 1)
            if kv == 0:
                dve.tensor_scalar(kcmpT[:, :], tp[1][:, 0:NKV * NCMP], QSCALE ** 0.5, None, ALU.mult)\
                    .then_inc(cmp_ev, 1)
            else:
                dve.tensor_copy(vcmp[:, :, :], tp[1][0:NCMP, :].rearrange("n (g d) -> n g d", g=NKV)).then_inc(cmp_ev, 1)
        dve_attention(dve, attn1)
        dve_product(dve, "c_out", residual_end(dve, True), norm_first("y1", None, None, None), turn=turn_out[1])
        dve_proj(dve, 1, 4)
        dve_mlp(dve, 1)
        dve_product(dve, "gate1", dve_gate_end(dve, 1), turn0=turn_mlp[1], after=norm(5))

        def final(m, n, eps):
            dve_means(dve, m, eps)
            dve_rstd(dve, m)
            dve.wait_ge(rstd_done, m + 1)
            dve.wait_ge(g_in, 16 * n)
            for t in range(TOK):
                f = dve.scalar_tensor_tensor(out=h[:, t, :], in0=h[:, t, :], scalar=rstd[:, t:t + 1], in1=gfull[:, :],
                                             op0=ALU.mult, op1=ALU.mult)
            f.then_inc(fin_done, 1)
        final(6, 1, 1e-6)
        dve_product(dve, "ab2_in", None, norm_first("ab2_in", 6, 7, 1e-5))
        dve_attention(dve, attn2a)
        dve_attention(dve, attn2b)
        dve_product(dve, "ab2_out", residual_end(dve), norm_first("ab2_out", None, None, None))
        dve_product(dve, "c2_in", None, norm_first("c2_in", 7, 8, 1e-5))
        dve_attention(dve, attn3)
        dve_product(dve, "c2_out", residual_end(dve), norm_first("c2_out", None, None, None), last=True)
        final(9, 2, 1e-5)

    @block.tensor
    def _(pe):
        def mixer_turn(c):
            def turn(i):
                k = GT * c + i
                if i == 0:
                    freed(pe, "ab_in", c + 1)
                if 2 <= k < 18:
                    pe.wait_ge(m_ev, k - 1)
                elif k >= 18:
                    pe.wait_ge(gated, k - 17)
                for t in range(TOK):
                    mm = pe.transpose(tp[k % 2][:, t * P:(t + 1) * P], part[:, t, i * P:(i + 1) * P], ident[:, :])
                mm.then_inc(m_tp, 1)
            return turn

        def gate_products(half):
            if half == 0:
                pe.wait_ge(bd_in, 64)
            for q in range(GT):
                j = GT * half + q
                pe.wait_ge(conv_done, 4 * (j + 1))
                if half == 1:
                    pe.wait_ge(gates_sg, q + 1)
                for n in range(2):
                    mm = pe.matmul(pa[:, q, n * S:(n + 1) * S], bd[:, n, j, :], xc[:, j, :], start=True, stop=True)
                mm.then_inc(gates_mm, 1)

        def pool_products(tiles):
            pe.wait_ge(gates_sg, LT)
            for j in tiles:
                g, jo = j // 2, j % 2
                pe.wait_ge(pool_step, 4 + 3 * g + 3)
                for i2 in range(2):
                    mm = pe.matmul(pa[:, j // 2, jo * S:(jo + 1) * S], pool_w[:, 2 * g + i2, jo * P:(jo + 1) * P],
                                   uT[:, 2 * g + i2, PADP:], start=(i2 == 0), stop=(i2 == 1))
                mm.then_inc(pool_mm, 1)

        def before_group(c):
            def before(n):
                if c == 0:
                    pe.wait_ge(tlo_done, GT * (n + 1))
                if c in (2, 3) and n == 3:
                    gate_products(c - 2)
                if c == 5 and n >= 2:
                    pool_products(range(4 * (n - 2), 4 * (n - 1)))
            return before
        C0, A0 = CHUNK0["ab_in"], ACC0["ab_in"]
        for c in range(6):
            pe_chunk(pe, C0 + c, A0 + c, aT, turn=mixer_turn(c - 1) if c else None, before=before_group(c))

        def before(n):
            pe.wait_ge(mix_lo, (2, 4, 5, 6)[n])
        C0, A0 = CHUNK0["ab_out"], ACC0["ab_out"]
        pe_chunk(pe, C0, A0, aT, turn=mixer_turn(5), before=before)
        with pe.Fori(0, NCH - 1) as j:
            pe_chunk(pe, j + (C0 + 1), j + (A0 + 1), aT, turn=pe_turn(pe, turn_out[0], j))
        pe_proj(pe, 0)
        pe_mlp(pe, 0)
        pe_product(pe, "gate0", bT, turn0=turn_mlp[0], turn=turn_gate)
        pe_product(pe, "c_in", aT, turn0=turn_gate)
        C, A_ = CHUNK0["c_tail"], ACC0["c_tail"]
        pe_chunk(pe, C, A_, aT, width=W_C - C_GATES)
        freed(pe, "c_in", 10)
        for n in range(8):
            if n >= 2:
                pe.wait_ge(c_ev, n - 1)
            for t in range(TOK):
                mm = pe.transpose(tp[n % 2][:, t * P:(t + 1) * P], z1[:, t, D + n * P:D + (n + 1) * P], ident[:, :])
            mm.then_inc(c_tp, 1)
        M = NKV * NCMP
        pe.wait_ge(c_ev, 8)
        for kv in range(2):
            C, A_ = CHUNK0[("cmp_k", "cmp_v")[kv]], ACC0[("cmp_k", "cmp_v")[kv]]
            pe.wait_ge(blk_lo_done, kv + 1)
            for n in range(2 * GT):
                pe.wait_ge(split_done, C * GT + n + 1)
                if n == 0:
                    freed(pe, "c_tail", 1)
                    if kv == 1:
                        pe.wait_ge(chid_done, 1)
                for i in range(GT):
                    tok = GT * n + i
                    for a, w in ((blk_hi, w_hi), (blk_hi, w_lo), (blk_lo, w_hi)):
                        mm = pe.matmul(acc[0][0:BW, :], a[:, tok, 0:BW], w[:, n % RING, i, :],
                                       start=(tok == 0 and a is blk_hi and w is w_hi), stop=(tok == CL - 1 and a is blk_lo))
                mm.then_inc(group_used, 1)
            pe.wait_ge(cmp_in, 48)
            pe.wait_ge(chid_done, kv + 1)
            if kv == 1:
                pe.wait_ge(cmp_ev, 1)
            for f in range(HID // P):
                mm = pe.transpose(tp[0][:, f * M:(f + 1) * M], chid[:, f * P:(f + 1) * P], ident[0:M, 0:M])
            mm.then_inc(chid_tp, 1)
            pe.wait_ge(chid_ev, kv + 1)
            if kv == 0:
                for f in range(HID // P):
                    mm = pe.matmul(tp[1][:, 0:M], cw2[:, 0, f, :], chidT[:, f, :], start=(f == 0), stop=(f == HID // P - 1))
            else:
                for g in range(NKV):
                    for f in range(HID // P):
                        mm = pe.matmul(tp[1][0:NCMP, g * HD:(g + 1) * HD], chidT[:, f, g * NCMP:(g + 1) * NCMP],
                                       cw2[:, 1, f, :], start=(f == 0), stop=(f == HID // P - 1))
            mm.then_inc(cmp_mm, 1)
        pe.wait_ge(cmp_ev, 2)
        pe_attention(pe, attn1)
        pe_product(pe, "c_out", aT, z1, "y1", once(lambda: pe.wait_ge(y_done, attn2a.unit0)), turn=turn_out[1])
        pe_proj(pe, 1)
        pe_mlp(pe, 1)
        pe_product(pe, "gate1", bT, turn0=turn_mlp[1])
        pe_product(pe, "ab2_in", aT, h, "ab2_in", once(lambda: pe.wait_ge(fin_done, 1)))
        pe_attention(pe, attn2a)
        pe_attention(pe, attn2b)
        pe_product(pe, "ab2_out", aT, z2, "ab2_out", once(lambda: pe.wait_ge(y_done, attn3.unit0)))
        pe_product(pe, "c2_in", aT, h, "c2_in", after_residual(pe, "ab2_out"))
        pe_attention(pe, attn3)
        pe_product(pe, "c2_out", aT, z3, "c2_out", once(lambda: pe.wait_ge(y_done, attn3.unit0 + 16)))

    ctx.close()


LOADS = 9
RPB_DMAS = NH * 4
LRU_STEPS = 6
BW = 68



def _stream(w, rows=None):
    k, n = w.shape
    if n % NW:
        w = np.pad(w, ((0, 0), (0, NW - n % NW)))
        n = w.shape[1]
    return w.reshape(k // (GT * P), GT, P, n // NW, NW).transpose(3, 0, 2, 1, 4).reshape(-1, P, GT * NW)


def _layout(a):
    f = np.float32
    a = {k: np.asarray(v) for k, v in a.items()}
    parts = []

    def mlp(l):
        up, down = a["mlp_w_up"][l], a["mlp_w_down"][l]
        for q in range(4):
            parts.append(_stream(up[:, q * D:(q + 1) * D]))
            parts.append(_stream(down[q * D:(q + 1) * D]))

    def proj(l):
        w = a["ple_w_proj"][l].reshape(2, P, NCH, NW).transpose(2, 1, 0, 3).reshape(NCH, P, 2 * NW)
        parts.append(np.pad(w, ((0, 0), (0, 0), (0, 2 * NW))))

    w_in, w_out = a["ab_w_in"][0], a["ab_w_out"][0]
    parts += [_stream(w_in[:, part:part + LRU]) for part in (0, 2 * LRU, LRU)]
    parts.append(_stream(np.concatenate([w_out[LRU:], w_out[:LRU]])))
    proj(0)
    mlp(0)
    parts += [_stream(a["ple_w_gate"][0]), _stream(a["c_w_in"][0])]
    parts += [_stream(a[k][0].reshape(CL * HD, HID)) for k in ("c_cmp_w1_k", "c_cmp_w1_v")]
    parts.append(_stream(a["c_w_out"][0]))
    proj(1)
    mlp(1)
    parts += [_stream(a["ple_w_gate"][1]), _stream(a["w_in_ab_2"][0]), _stream(a["w_out_ab_2"][0]),
              _stream(a["w_in_c_2"][0]), _stream(a["w_out_c_2"][0])]
    o = {"wstream": np.concatenate(parts)}
    assert o["wstream"].shape[0] == NC * GT

    def column(v, n):
        return v.reshape(n, P).T

    o["x"] = a["x"]
    o["xT"] = a["x"][0].T
    o["pT"] = a["p"][:, 0].transpose(0, 2, 1)
    g = [a["ln_mix_g"][0], a["ln_mlp_g"][0], a["ln_ple_g"][0], a["ln_mix_g"][1], a["ln_mlp_g"][1], a["ln_ple_g"][1],
         a["ln_ab_2"][0], a["ln_c_2"][0]]
    o["gains"] = np.stack([column(v, KT) for v in g], 1)
    v = [*a["ab_conv_w"][0], a["ab_conv_b"][0], a["ab_b_rgate"][0], a["ab_b_igate"][0], a["ab_lambda"][0],
         a["ab_pool_scale"][0]]
    o["vecs"] = np.stack([column(x, LT) for x in v], 1)
    o["pool_w"] = a["ab_pool_w"][0].reshape(LT, P, S).transpose(1, 0, 2)
    o["w_r"], o["w_i"] = a["ab_w_rgate"][0], a["ab_w_igate"][0]
    o["w2_k"], o["w2_v"] = a["c_cmp_w2_k"][0], a["c_cmp_w2_v"][0]
    o["posT"] = np.stack([a["c_cmp_pos_k"][0].T, a["c_cmp_pos_v"][0].T])
    o["sinks"] = np.broadcast_to(a["sink_a_2"][0], (P, 8))
    o["g1"] = np.broadcast_to(a["ln_final_g"], (P, D))
    o["g2"] = np.broadcast_to(a["ln_f_2"], (P, D))
    o["rpb"] = np.tile(np.pad(a["rpb_c_2"][0], ((0, 0), (0, 0), (48, 49))), (1, 1, 64))

    t = np.arange(S)
    dist = t[:, None] - t[None, :]
    slope = np.exp2(-8.0 * np.arange(1, NH + 1) / NH)
    neg = -1e30

    def table(b):
        return b.reshape(4, 4, TOK, P, S).transpose(0, 3, 1, 2, 4).reshape(4, P, 4 * TOK * S).astype(f)

    o["ident"] = np.eye(P, dtype=f)
    o["bias1"] = table(np.where(dist >= 0, -slope[:, None, None] * dist, neg))
    far = np.abs(dist)
    times = sum(((far <= w // 2) & (dist % d == 0)).astype(int) for w, d in ((128, 1), (512, 4), (2048, 16)))
    b = np.where(far <= 128, -slope[:, None, None] * far, neg)
    b[8:] = np.where(times > 0, -slope[8:, None, None] * far + np.log(np.maximum(times, 1)), neg)
    o["bias2"] = table(b)
    end = np.arange(NCMP) * 16 + CL - 1
    dc = t[:, None] - end[None, :]
    bc = np.where(dc >= 0, -slope[:, None, None] * dc, neg)
    o["bias_c"] = bc.reshape(NH, TOK, P, NCMP).transpose(2, 0, 1, 3).astype(f)
    o["valid_c"] = (dc >= 0).reshape(TOK, P, NCMP).transpose(1, 0, 2).astype(f)
    c = np.arange(64)
    c0 = np.clip(c - 8, 0, 48)
    inside = (c[None, :] >= c0[:, None]) & (c[None, :] < c0[:, None] + 16)
    o["mask3"] = np.tile(np.where(inside, 0.0, neg), (2, 4)).astype(f)
    cnt = np.minimum(np.arange(PADP) + 1, np.array([2, 4, 8, 16])[:, None])
    o["invcnt"] = np.broadcast_to((1.0 / cnt).astype(f), (P, 4, PADP))
    return {k: np.ascontiguousarray(v) for k, v in o.items()}


def kernel(**inputs):
    import concourse.bacc as bacc
    from concourse.bass_utils import run_bass_kernel_spmd

    arrays = _layout(inputs)
    nc = bacc.Bacc("TRN2", target_bir_lowering=False, num_devices=1)
    A = {k: nc.dram_tensor(f"in_{k}", v.shape, mybir.dt.from_np(v.dtype), kind="ExternalInput").ap()
         for k, v in arrays.items()}
    A["bias3"] = nc.dram_tensor("bias3", (4, P, 4 * TOK * S), F32, kind="Internal").ap()
    out = nc.dram_tensor("out", (1, S, D), F32, kind="ExternalOutput").ap()
    build(nc, A, out)
    r = run_bass_kernel_spmd(nc, [{f"in_{k}": v for k, v in arrays.items()}], core_ids=[0])
    return r.results[0]["out"]
```

```python
from contextlib import ExitStack

import numpy as np

import concourse.bass as bass
from concourse import mybir

ALU = mybir.AluOpType
ACT = mybir.ActivationFunctionType
AX_X = mybir.AxisListType.X
F32 = mybir.dt.float32
F32R = mybir.dt.float32r

P = 128
S = 256
TOK = S // P
D = 2048
KT = D // P
NW = 512
GT = 4
NCH = D // NW
HD = 128
NH = 16
QSCALE = float(HD) ** -0.5
RAW, RING = 2, 4
AHEAD = 3
LRU = 1024
LT = LRU // P
PADC = 3
PADP = 16
NCMP = 15
NKV = 4
CL = 32
HID = 512
C_GATES = D + 6 * 512
NB3 = 3
NG = NB3 * NH
W_C = C_GATES + NG

ORDER = [("ab_in", 6), ("ab_out", 4), ("proj0", 1), ("mlp0", 32), ("gate0", 4),
         ("c_in", 10), ("cmp_k", 2), ("cmp_v", 2), ("c_out", 4), ("proj1", 1),
         ("mlp1", 32), ("gate1", 4),
         ("ab2_in", 13), ("ab2_out", 4), ("c2_in", 16), ("c2_out", 4)]
CHUNK0 = {}
NC = 0
for _name, _n in ORDER:
    CHUNK0[_name] = NC
    NC += _n

ACC0 = {}
_a = 0
for _name, _n in ORDER:
    ACC0[_name] = _a
    _a += 4 if _name.startswith("proj") else 0 if _name.startswith("cmp") else _n
    if _name == "c_in":
        ACC0["gates"] = _a
        _a += 1

TILE0 = {}
_t = 0
for _name, _n in [("x", KT), ("ab_out", KT), ("hidden0", 4 * KT), ("mlp0", KT), ("gate0", KT), ("y1", KT), ("c_out", KT),
                  ("hidden1", 4 * KT), ("mlp1", KT), ("ab2_in", KT), ("ab2_out", KT), ("c2_in", KT),
                  ("c2_out", KT)]:
    TILE0[_name] = _t
    _t += _n


def build(nc, A, out):
    ctx = ExitStack()

    def sb(name, shape, dt=F32, stack=None):
        return (stack or ctx).enter_context(nc.sbuf_tensor(name, shape, dt))

    def overlay(*tensors):
        with ExitStack() as stack:
            return [sb(*t, stack=stack) for t in tensors]

    def bank(name):
        return ctx.enter_context(nc.psum_tensor(name, [P, 512], F32))

    def sem(name):
        return ctx.enter_context(nc.semaphore(name))

    raw = sb("raw", [P, RAW, GT, NW])
    w_hi = sb("w_hi", [P, RING, GT, NW], F32R)
    w_lo = sb("w_lo", [P, RING, GT, NW], F32R)
    h = sb("h", [P, TOK, D])
    ident = sb("ident", [P, P])
    gains = sb("gains", [P, 8, KT])
    stat = sb("stat", [P, 3, TOK])
    rstd = sb("rstd", [P, TOK])
    small = sb("small", [P, 8, 2, TOK])
    sinks = sb("sinks", [P, 8])
    bias_c = sb("bias_c", [P, NH, TOK, NCMP])
    valid_c = sb("valid_c", [P, TOK, NCMP])
    mask3 = sb("mask3", [P, S])
    kcmpT = sb("kcmpT", [P, NKV * NCMP])
    vcmp = sb("vcmp", [NCMP, NKV, HD])

    xc, rg, ig, th, _, xr, uT, pool_w = overlay(
        ("xc", [P, LT, S]), ("rg", [P, LT, S]), ("ig", [P, LT, S]), ("th", [P, LT, S]), ("part_", [P, TOK, NW]),
        ("xr", [P, LT, PADC + S]), ("uT", [P, LT, PADP + S]), ("pool_w", [P, LT, S]))
    xT, = overlay(("xT", [P, KT, S]))
    _, pw0, pw1 = overlay(("xc_", [P, LT, S]), ("pw0", [P, LT, PADP + S]), ("pw1", [P, LT - 2, PADP + S]))
    z1, cT, chid, chidT, cw2, posT, blk = overlay(
        ("z1", [P, TOK, W_C]), ("cT", [P, 2, NKV, S]), ("chid", [NKV * NCMP, HID]),
        ("chidT", [P, 256]), ("cw2", [P, 2, HID // P, HD]), ("posT", [P, 2, CL]),
        ("blk", [P, BLK]))
    _, gw_hi, gw = overlay(
        ("z1_", [P, TOK * W_C + 2 * NKV * S]), ("gw_hi", [P, GW], F32R), ("gw", [P, GW]))
    _, _, gw_lo = overlay(
        ("z1__", [P, TOK * W_C + 2 * NKV * S]), ("gw_hi_", [P, GW], F32R), ("gw_lo", [P, GW], F32R))

    z2, = overlay(("z2", [P, TOK, 6656]))
    z3, = overlay(("z3", [P, TOK, 8192]))
    bT_hi, bT_lo, part, gpart, proj, pT_hi, pT_lo, pT = overlay(
        ("bT_hi", [P, KT, S], F32R), ("bT_lo", [P, KT, S], F32R), ("part", [P, TOK, NW]), ("gpart", [P, TOK, NW]),
        ("proj", [P, TOK, D]), ("pT_hi", [P, 2, S], F32R), ("pT_lo", [P, 2, S], F32R), ("pT", [P, 2, S]))
    gfull, = overlay(("gfull", [P, D]))
    sb("region_z", [P, 16384])

    aT_hi, aT_lo = overlay(("aT_hi", [P, KT, S], F32R), ("aT_lo", [P, KT, S], F32R))
    k_hi, k_lo, v_hi, v_lo = overlay(
        ("k_hi", [P, BLK], F32R), ("k_lo", [P, BLK], F32R), ("v_hi", [P, BLK], F32R), ("v_lo", [P, BLK], F32R))
    blk_hi, blk_lo = (k_hi, v_hi), (k_lo, v_lo)
    stq, stk, stv, qkT, prob, prT, bias = overlay(
        ("stq", [P, TOK, 4, HD]), ("stk", [P, TOK, 4, HD]), ("stv", [NCMP, 4, HD]), ("qkT", [P, 2, 2 * S]),
        ("prob", [P, 2, TOK, S + 2]), ("prT", [P, 2, TOK, S]), ("bias", [P, 4, TOK, S]))
    sb("region_a", [P, 8192])

    bd = sb("bd", [P, 2, LT, P])
    gatesT = bd[:, 0, 0:2, :].rearrange("p a b -> p (a b)")
    vecs = sb("vecs", [P, 9, LT])
    soft = sb("soft", [P, 4, LT])
    invcnt = sb("invcnt", [P, 4, PADP])

    acc = [bank(f"acc{t}") for t in range(TOK)]
    tp = [bank(f"tp{t}") for t in range(2)]
    pa = ctx.enter_context(nc.psum_tensor("pa", [P, 4, 512], F32))

    landed = [sem(f"landed{i}") for i in range(RAW)]
    hi_done = sem("hi_done")
    split_done = sem("split_done")
    group_used = sem("group_used")
    acc0_done = sem("acc0_done")
    acc1_done = sem("acc1_done")
    acc_free = [sem(f"acc_free{t}") for t in range(TOK)]
    tp_done = sem("tp_done")
    thi_done = sem("thi_done")
    tlo_done = sem("tlo_done")
    kept = sem("kept")
    h_done = sem("h_done")
    hid_done = sem("hid_done")
    gp_done = sem("gp_done")
    sq_done = sem("sq_done")
    ms_done = sem("ms_done")
    root_done = sem("root_done")
    rstd_done = sem("rstd_done")
    x_in = [sem(f"x_in{n}") for n in range(GT)]
    gains_in = sem("gains_in")
    const_in = sem("const_in")
    bd_zero = sem("bd_zero")
    bd_in = sem("bd_in")
    dve_chain = sem("dve_chain")
    soft_exp = sem("soft_exp")
    m_tp = sem("m_tp")
    m_ev = sem("m_ev")
    gated = sem("gated")
    conv_step = sem("conv_step")
    conv_done = sem("conv_done")
    gates_mm = sem("gates_mm")
    gates_sg = sem("gates_sg")
    tanh_done = sem("tanh_done")
    decay_done = sem("decay_done")
    lru_dve = sem("lru_dve")
    lru_root = sem("lru_root")
    mix_hi = sem("mix_hi")
    mix_lo = sem("mix_lo")
    pads_zero = sem("pads_zero")
    pool_step = sem("pool_step")
    pool_mm = sem("pool_mm")
    p_in = sem("p_in")
    p_hi = sem("p_hi")
    p_lo = sem("p_lo")
    proj_done = sem("proj_done")
    cmp_in = sem("cmp_in")
    c_tp = sem("c_tp")
    c_ev = sem("c_ev")
    gw_hi_done = sem("gw_hi_done")
    gw_lo_done = sem("gw_lo_done")
    gates_done = sem("gates_done")
    gates_tp = sem("gates_tp")
    blk_done = sem("blk_done")
    blk_hi_done = sem("blk_hi_done")
    blk_lo_done = sem("blk_lo_done")
    chid_done = sem("chid_done")
    chid_tp = sem("chid_tp")
    chid_ev = sem("chid_ev")
    cmp_mm = sem("cmp_mm")
    cmp_ev = sem("cmp_ev")
    bias_in = [sem(f"bias_in{i}") for i in range(4)]
    bias_ok = sem("bias_ok")
    staged = [sem(f"staged{i}") for i in range(4)]
    staged_v = [sem(f"staged_v{i}") for i in range(4)]
    qk_tp = sem("qk_tp")
    qk_ev = sem("qk_ev")
    s_mm = sem("s_mm")
    sink_in = sem("sink_in")
    max_done = sem("max_done")
    biased = sem("biased")
    neg_done = sem("neg_done")
    exp_done = sem("exp_done")
    pmask = sem("pmask")
    rden_done = sem("rden_done")
    coef_done = sem("coef_done")
    p_tp = sem("p_tp")
    p_ev = sem("p_ev")
    pv_mm = sem("pv_mm")
    y_done = sem("y_done")
    g_in = sem("g_in")
    fin_done = sem("fin_done")
    rpb_out = sem("rpb_out")
    out_done = sem("out_done")

    wstream = A["wstream"]

    def split_act(act, C, n):
        act.wait_ge(landed[n % RAW], (C * 2 + n // RAW + 1) * 16)
        if not isinstance(C, int) or C * GT + n >= RING:
            act.wait_ge(group_used, C * GT + (n - RING + 1))
        act.activation(w_hi[:, n % RING], raw[:, n % RAW], ACT.Copy).then_inc(hi_done, 1)

    def split_dve(dve, C, n):
        dve.wait_ge(hi_done, C * GT + (n + 1))
        dve.tensor_tensor(w_lo[:, n % RING], raw[:, n % RAW], w_hi[:, n % RING].bitcast(F32),
                          ALU.subtract).then_inc(split_done, 1)


    def pe_group(pe, C, A0, n, lhs, tiles=None, then=None, width=NW, turn=None):
        hi, lo = lhs
        pe.wait_ge(split_done, C * GT + (n + 1))
        for t in range(TOK):
            if n == 0 and not (isinstance(A0, int) and A0 == 0):
                pe.wait_ge(acc_free[t], A0)
            for i in range(GT):
                kt = GT * n + i
                if tiles is not None and t == 0:
                    pe.wait_ge(tlo_done, tiles + (kt + 1))
                for a, w in ((hi, w_hi), (hi, w_lo), (lo, w_hi)):
                    mm = pe.matmul(acc[t][:, 0:width], a[:, kt, t * P:(t + 1) * P], w[:, n, i, 0:width],
                                   start=(kt == 0 and a is hi and w is w_hi),
                                   stop=(kt == KT - 1 and a is lo))
                if t == 0 and then is not None:
                    then(i)
                if turn is not None and n == 1 and i % 2 == 1:
                    turn(2 * t + i // 2)
            if t == 0 and n == GT - 1:
                mm.then_inc(acc0_done, 1)
        mm.then_inc(group_used, 1)

    def pe_chunk(pe, C, A0, lhs, width=NW, turn=None, before=None):
        for n in range(GT):
            if before:
                before(n)
            pe_group(pe, C, A0, n, lhs, width=width, turn=turn)

    def pe_tile(pe, T0, kt, src, ready):
        if ready is not None:
            ready(kt)
        pe.wait_ge(tlo_done, T0 + (kt - 1))
        for t in range(TOK):
            mm = pe.transpose(tp[kt % 2][:, t * P:(t + 1) * P], src[:, t, kt * P:(kt + 1) * P], ident[:, :])
        mm.then_inc(tp_done, 1)

    def pe_first(pe, C, A0, T0, lhs, src, ready):
        for kt in range(GT):
            pe_tile(pe, T0, kt, src, ready)
        for n in range(GT):
            def then(i, n=n):
                if n < GT - 1:
                    pe_tile(pe, T0, GT * (n + 1) + i, src, ready)
            pe_group(pe, C, A0, n, lhs, tiles=T0, then=then)


    class Turn:
        def __init__(self, run, dst, gain, ready):
            self.T0, self.dst, self.gain, self.ready = TILE0[run], dst, gain, ready

    def pe_turn(pe, tr, c):
        def turn(i):
            if i == 0:
                tr.ready(pe, c)
            pe.wait_ge(tlo_done, c * 4 + (tr.T0 + i - 1))
            for t in range(TOK):
                mm = pe.transpose(tp[i % 2][:, t * P:(t + 1) * P], part[:, t, i * P:(i + 1) * P], ident[:, :])
            mm.then_inc(tp_done, 1)
        return turn

    def at_tile(x, c, i):
        return x[:, 4 * c + i] if isinstance(c, int) else x[:, bass.ds(c * 4 + i, 1)].rearrange("p a s -> p (a s)")

    def gain_of(tr, c, i):
        if tr.gain is None:
            return 1.0
        return gains[:, tr.gain, 4 * c + i:4 * c + i + 1] if isinstance(c, int) else \
            gains[:, tr.gain, bass.ds(c * 4 + i, 1)]

    def act_turn(act, tr, c):
        for i in range(GT):
            act.wait_ge(tp_done, c * 4 + (tr.T0 - KT + i + 1))
            act.activation(at_tile(tr.dst[0], c, i), tp[i % 2][:, 0:S], ACT.Copy, scale=gain_of(tr, c, i))\
                .then_inc(thi_done, 1)

    def dve_turn(dve, tr, c):
        for i in range(GT):
            dve.wait_ge(thi_done, c * 4 + (tr.T0 + i + 1))
            dve.scalar_tensor_tensor(
                out=at_tile(tr.dst[1], c, i), in0=tp[i % 2][:, 0:S], scalar=gain_of(tr, c, i),
                in1=at_tile(tr.dst[0], c, i).bitcast(F32), op0=ALU.mult, op1=ALU.subtract).then_inc(tlo_done, 1)


    def act_tiles(act, T0, hi, gain, tiles):
        for kt in tiles:
            act.wait_ge(tp_done, T0 - KT + (kt + 1))
            act.activation(hi[:, kt], tp[kt % 2][:, 0:S], ACT.Copy,
                           scale=1.0 if gain is None else gains[:, gain, kt:kt + 1]).then_inc(thi_done, 1)

    def dve_tiles(dve, T0, hi, lo, gain, tiles):
        for kt in tiles:
            dve.wait_ge(thi_done, T0 + (kt + 1))
            dve.scalar_tensor_tensor(
                out=lo[:, kt], in0=tp[kt % 2][:, 0:S], scalar=1.0 if gain is None else gains[:, gain, kt:kt + 1],
                in1=hi[:, kt].bitcast(F32), op0=ALU.mult, op1=ALU.subtract).then_inc(tlo_done, 1)


    def dve_means(dve, m, eps):
        dve.wait_ge(sq_done, TOK * (m + 1))
        dve.tensor_scalar(stat[:, 1], stat[:, 0], 1.0 / D, eps, ALU.mult, ALU.add).then_inc(ms_done, 1)

    def act_root(act, m):
        act.wait_ge(ms_done, m + 1)
        act.activation(stat[:, 2], stat[:, 1], ACT.Sqrt).then_inc(root_done, 1)

    def dve_rstd(dve, m):
        dve.wait_ge(root_done, m + 1)
        dve.reciprocal(rstd[:, :], stat[:, 2]).then_inc(rstd_done, 1)


    def act_project(act, C, A0, m, dst, func=ACT.Copy, width=NW):
        for t in range(TOK):
            if t == 0:
                act.wait_ge(acc0_done, A0 + 1)
                act.wait_ge(rstd_done, m + 1)
            else:
                act.wait_ge(group_used, C * GT + GT)
            act.activation(dst(t), acc[t][:, 0:width], func, scale=rstd[:, t:t + 1]).then_inc(acc_free[t], 1)

    def act_keep(act, A0, col):
        for t in range(TOK):
            act.wait_ge(acc_free[t], A0 + 1)
            act.activation(h[:, t, bass.ds(col, NW)], part[:, t, :], ACT.Copy).then_inc(kept, 1)

    def dve_residual(dve, C, A0, col, to_part=False):
        for t in range(TOK):
            if t == 0:
                dve.wait_ge(acc0_done, A0 + 1)
            else:
                dve.wait_ge(group_used, C * GT + GT)
            old = h[:, t, bass.ds(col, NW)]
            dve.tensor_tensor(part[:, t, :] if to_part else old, acc[t][:, :], old, ALU.add).then_inc(acc_free[t], 1)


    class Attention:

        def __init__(self, rounds, units, z, q_col, k_parts, unit0, cmp0, stage0, round0, table, gated=False,
                     silu_col=None, y_col=0, sink=False, masked=False, table0=0):
            self.rounds, self.units, self.z, self.q_col, self.k_parts = rounds, units, z, q_col, k_parts
            self.unit0, self.cmp0, self.stage0, self.round0 = unit0, cmp0, stage0, round0
            self.table, self.table0, self.gated, self.silu_col = table, table0, gated, silu_col
            self.y_col, self.sink, self.masked = y_col, sink, masked
            self.n = len(units)
            self.per_head = self.n // 4
            self.full = [u[0] == S for u in units]
            self.copies = 1 + len(k_parts(0))

        def U(self, i, u):
            return i * self.n + (self.unit0 + u)

        def M(self, i, u):
            n = u - sum(self.full[0:u]) if u >= 0 else -4
            return i * (self.n - sum(self.full)) + (self.cmp0 + n)

        def in_slot(self, i):
            return i * (16 * self.copies) + 16 * (self.stage0 + self.copies)

    units1 = []
    for hh in range(4):
        ks = 2 * (hh % 2)
        units1 += [(S, hh, ks, (D + 3 * 512, HD), 1), (S, hh, ks + 1, (D + 5 * 512, HD), 2), (NCMP, hh, None, None, 0)]
    attn1 = Attention(NKV, units1, z1, 0, lambda hh: [(D + 2 * 512, HD, 2 * (hh % 2)), (D + 4 * 512, HD, 2 * (hh % 2) + 1)],
                      unit0=0, cmp0=0, stage0=0, round0=0, table=A["bias1"], gated=True)
    attn2a = Attention(2, [(S, hh, hh, (1280, HD), None) for hh in range(4)], z2, 0, lambda hh: [(1024, HD, hh)],
                       unit0=48, cmp0=16, stage0=12, round0=4, table=A["bias2"], silu_col=4608, sink=True)
    attn2b = Attention(2, [(S, hh, hh, (3584 + hh * HD, 512), None) for hh in range(4)], z2, 1536,
                       lambda hh: [(2560 + hh * HD, 512, hh)], unit0=56, cmp0=16, stage0=16, round0=6,
                       table=A["bias2"], table0=2, silu_col=5632, y_col=1024)
    attn3 = Attention(4, [(S, hh, hh, (4096 + hh * HD, 512), None) for hh in range(4)], z3, 0,
                      lambda hh: [(2048 + hh * HD, 512, hh)], unit0=64, cmp0=16, stage0=20, round0=8,
                      table=A["bias3"], silu_col=6144, masked=True)

    def some(eng, s, value, least=1):
        if not isinstance(value, int) or value >= least:
            eng.wait_ge(s, value)

    def sp_round(sp, at, i):
        peeled = at.gated and isinstance(i, int)

        def stage_v(hh):
            sp.dma_start(stv[:, hh, :], vcmp[:, bass.ds(i, 1), :].rearrange("n a d -> n (a d)")).then_inc(staged_v[hh], 16)
        for hh in range(4):
            last_use = at.U(i, (hh + 1) * at.per_head - at.n)
            some(sp, qk_tp, last_use if not at.gated else at.U(i, (hh + 3) * at.per_head - at.n) if hh < 2
                 else at.U(i, (hh - 1) * at.per_head))
            sp.dma_start(stq[:, :, hh, :], at.z[:, :, bass.ds(i * 512 + (at.q_col + hh * HD), HD)])\
                .then_inc(staged[hh], 16)
            for col, per, slot in at.k_parts(hh):
                sp.dma_start(stk[:, :, slot, :], at.z[:, :, bass.ds(i * per + col, HD)]).then_inc(staged[hh], 16)
            if at.gated and not peeled:
                some(sp, pv_mm, last_use)
                stage_v(hh)
            some(sp, max_done, last_use)
            sp.dma_start(bias[:, hh].rearrange("p t k -> p (t k)"),
                         at.table[bass.ds(i + at.table0, 1), :, hh * 512:(hh + 1) * 512].rearrange("a p n -> (a p) n"))\
                .then_inc(bias_in[hh], 16)
        if peeled:
            sp.wait_ge(cmp_ev, 2)
            for hh in range(4):
                stage_v(hh)

    def pool_mask(pool, at, i):
        for hh in range(4):
            pool.wait_ge(bias_in[hh], i * 16 + (at.round0 + 1) * 16)
            pool.tensor_tensor(bias[:, hh], bias[:, hh], mask3[:, :].unsqueeze(1).broadcast_to([P, TOK, S]), ALU.add)\
                .then_inc(bias_ok, 1)

    def pe_qk(pe, at, i, u):
        r, hh, kk = u % 2, at.units[u][1], at.units[u][2]
        pe.wait_ge(staged[hh], at.in_slot(i))
        some(pe, qk_ev, at.U(i, u - 1))
        for t in range(TOK):
            mm = pe.transpose(tp[r][:, t * P:(t + 1) * P], stq[:, t, hh, :], ident[:, :])
        if kk is not None:
            for t in range(TOK):
                mm = pe.transpose(tp[r][:, S + t * P:S + (t + 1) * P], stk[:, t, kk, :], ident[:, :])
        mm.then_inc(qk_tp, 1)

    def pe_scores(pe, at, i, u):
        r, w = u % 2, at.units[u][0]
        pe.wait_ge(qk_ev, at.U(i, u + 1))
        some(pe, max_done, at.U(i, u - 1))
        for t in range(TOK):
            rhs = qkT[:, r, S:2 * S] if at.full[u] else kcmpT[:, bass.ds(i * NCMP, NCMP)]
            mm = pe.matmul(pa[:, r, t * S:t * S + w], qkT[:, r, t * P:(t + 1) * P], rhs, start=True, stop=True)
        mm.then_inc(s_mm, 1)

    def pe_turn_p(pe, at, i, u):
        r = u % 2
        if at.full[u]:
            pe.wait_ge(exp_done, at.U(i, u + 1))
        else:
            pe.wait_ge(pmask, at.M(i, u + 1))
        some(pe, p_ev, at.U(i, u - 1))
        for t in range(TOK):
            if at.full[u]:
                for kb in range(S // P):
                    mm = pe.transpose(pa[:, 2 + r, kb * S + t * P:kb * S + (t + 1) * P],
                                      prob[:, r, t, kb * P:(kb + 1) * P], ident[:, :])
            else:
                mm = pe.transpose(pa[0:NCMP, 2 + r, t * P:(t + 1) * P], prob[:, r, t, 0:NCMP], ident[:, :])
        mm.then_inc(p_tp, 1)

    def pe_apply(pe, at, i, u):
        r = u % 2
        pe.wait_ge(p_ev, at.U(i, u + 1))
        some(pe, y_done, at.U(i, u - 1))
        for t in range(TOK):
            if at.full[u]:
                c0, per = at.units[u][3]
                for kb in range(S // P):
                    mm = pe.matmul(acc[r][:, t * P:(t + 1) * P], prT[:, r, kb, t * P:(t + 1) * P],
                                   at.z[:, kb, bass.ds(i * per + c0, HD)], start=(kb == 0), stop=(kb == S // P - 1))
            else:
                if t == 0:
                    pe.wait_ge(staged_v[at.units[u][1]], i * 16 + 16)
                mm = pe.matmul(acc[r][:, t * P:(t + 1) * P], prT[0:NCMP, r, 0, t * P:(t + 1) * P],
                               stv[:, at.units[u][1], :], start=True, stop=True)
        mm.then_inc(pv_mm, 1)

    def act_qk(act, at, i, u):
        r = u % 2
        w = 2 * S if at.full[u] else S
        act.wait_ge(qk_tp, at.U(i, u + 1))
        some(act, s_mm, at.U(i, u - 1))
        act.activation(qkT[:, r, 0:w], tp[r][:, 0:w], ACT.Copy, scale=QSCALE ** 0.5).then_inc(qk_ev, 1)

    def act_exp(act, at, i, u):
        r, w = u % 2, at.units[u][0] + (1 if at.sink else 0)
        act.wait_ge(neg_done, at.U(i, u + 1))
        some(act, rden_done, at.U(i, u - 1))
        for t in range(TOK):
            e = act.activation(prob[:, r, t, 0:w], prob[:, r, t, 0:w], ACT.Exp, bias=small[:, 1, r, t:t + 1],
                               accum_out=small[:, 2, r, t:t + 1])
        e.then_inc(exp_done, 1)

    def act_turn_p(act, at, i, u):
        r = u % 2
        act.wait_ge(p_tp, at.U(i, u + 1))
        some(act, pv_mm, at.U(i, u - 1))
        if at.full[u]:
            act.activation(prT[:, r].rearrange("p a b -> p (a b)"), pa[:, 2 + r, :], ACT.Copy).then_inc(p_ev, 1)
        else:
            act.activation(prT[0:NCMP, r, 0, :], pa[0:NCMP, 2 + r, 0:S], ACT.Copy).then_inc(p_ev, 1)

    def dve_max(dve, at, i, u):
        w, hh, r = at.units[u][0], at.units[u][1], u % 2
        dve.wait_ge(s_mm, at.U(i, u + 1))
        some(dve, p_tp, at.U(i, u - 1))
        if at.masked:
            dve.wait_ge(bias_ok, i * 4 + (hh + 1))
        else:
            dve.wait_ge(bias_in[hh], i * 16 + (at.round0 + 1) * 16)
        sink = sinks[:, bass.ds(i * 4 + hh, 1)] if at.sink else None
        if at.sink:
            for t in range(TOK):
                dve.tensor_copy(prob[:, r, t, S:S + 1], sink)
        if at.full[u]:
            dve.memset(small[:, 5, r], 0.0)
            for t in range(TOK):
                m = dve.tensor_tensor_reduce(prob[:, r, t, 0:w], pa[:, r, t * S:t * S + w], bias[:, hh, t, :],
                                             1.0, -3.0e38, ALU.add, ALU.max, small[:, 0, r, t:t + 1])
            m.then_inc(max_done, 1)
        else:
            dve.tensor_tensor(prob[:, r, :, 0:w], pa[:, r, :].rearrange("p (t k) -> p t k", t=TOK)[:, :, 0:w],
                              bias_c[:, bass.ds(i * 4 + hh, 1), :, :].rearrange("p a t n -> p (a t) n"),
                              ALU.add).then_inc(biased, 1)
            dve.wait_ge(biased, at.M(i, u + 1))
            dve.tensor_reduce(small[:, 0, r], prob[:, r, :, 0:w], AX_X, ALU.max).then_inc(max_done, 1)
        dve.wait_ge(max_done, at.U(i, u + 1))
        some(dve, exp_done, at.U(i, u - 1))
        if at.sink:
            dve.tensor_scalar(small[:, 1, r], small[:, 0, r], sink, -1.0, ALU.max, ALU.mult).then_inc(neg_done, 1)
        else:
            dve.tensor_scalar(small[:, 1, r], small[:, 0, r], -1.0, None, ALU.mult).then_inc(neg_done, 1)

    def dve_factor(dve, at, i, u):
        r = u % 2
        dve.wait_ge(exp_done, at.U(i, u + 1))
        if not at.full[u]:
            dve.tensor_tensor(prob[:, r, :, 0:NCMP], prob[:, r, :, 0:NCMP], valid_c[:, :, :], ALU.mult)\
                .then_inc(pmask, 1)
        some(dve, y_done, at.U(i, u - 1))
        dve.reciprocal(small[:, 3, r], small[:, 2, r]).then_inc(rden_done, 1)
        if at.gated:
            gate = z1[:, :, bass.ds(i * 4 + (C_GATES + at.units[u][4] * NH + at.units[u][1]), 1)]
            dve.wait_ge(rden_done, at.U(i, u + 1))
            dve.tensor_tensor(small[:, 4, r], small[:, 3, r], gate.rearrange("p t a -> p (t a)"), ALU.mult)\
                .then_inc(coef_done, 1)

    def dve_y(dve, at, i, u):
        r, hh = u % 2, at.units[u][1]
        begins = u % at.per_head == 0
        dve.wait_ge(pv_mm, at.U(i, u + 1))
        if at.gated:
            dve.wait_ge(coef_done, at.U(i, u + 1))
            if not begins:
                dve.wait_ge(y_done, at.U(i, u))
        else:
            dve.wait_ge(rden_done, at.U(i, u + 1))
        for t in range(TOK):
            y = at.z[:, t, bass.ds(i * 512 + (at.y_col + hh * HD), HD)]
            o = acc[r][:, t * P:(t + 1) * P]
            if not at.gated:
                gate = at.z[:, t, bass.ds(i * 512 + (at.silu_col + hh * HD), HD)]
                d = dve.scalar_tensor_tensor(out=y, in0=o, scalar=small[:, 3, r, t:t + 1], in1=gate,
                                             op0=ALU.mult, op1=ALU.mult)
            elif begins:
                d = dve.tensor_scalar(y, o, small[:, 4, r, t:t + 1], None, ALU.mult)
            else:
                d = dve.scalar_tensor_tensor(out=y, in0=o, scalar=small[:, 4, r, t:t + 1], in1=y,
                                             op0=ALU.mult, op1=ALU.add)
        d.then_inc(y_done, 1)

    def in_rounds(eng, at, stages):
        def steps(i, first, last, carried):
            for s in range(first, last):
                for lag, stage in stages:
                    u = s - lag
                    if 0 <= u < at.n:
                        stage(eng, at, i + 1 if carried else i, u)
                    elif u < 0 and carried:
                        stage(eng, at, i, u + at.n)
        steps(0, 0, at.n, False)
        with eng.Fori(0, at.rounds - 1) as i:
            steps(i, 0, at.n, True)
        steps(at.rounds - 1, at.n, at.n + 3, False)

    def pe_attention(pe, at):
        in_rounds(pe, at, [(0, pe_qk), (1, pe_scores), (2, pe_turn_p), (3, pe_apply)])

    def act_attention(act, at):
        in_rounds(act, at, [(0, act_qk), (2, act_turn_p), (1, act_exp)])

    def dve_attention(dve, at):
        in_rounds(dve, at, [(2, dve_factor), (1, dve_max), (3, dve_y)])

    def each_round(eng, at, body):
        body(eng, at, 0)
        with eng.Fori(1, at.rounds) as i:
            body(eng, at, i)



    TILES_BEFORE = {AHEAD + 1: range(0, 8), AHEAD + 2: range(8, 12), AHEAD + 3: range(12, 16)}

    def act_splits(act, C, tr=None, c=None, tiles=None, squares=None):
        for n in range(AHEAD, AHEAD + GT):
            if n == AHEAD + 2 and tr is not None:
                act_turn(act, tr, c)
            if tiles is not None and n > AHEAD:
                tiles(TILES_BEFORE[n])
            if n == AHEAD + 3 and squares:
                squares()
            split_act(act, C, n)

    def dve_splits(dve, C, tr=None, c=None, tiles=None, means=None):
        for n in range(AHEAD, AHEAD + GT):
            if n == AHEAD + 2 and tr is not None:
                dve_turn(dve, tr, c)
            if tiles is not None and n > AHEAD:
                tiles(TILES_BEFORE[n])
            if n == AHEAD + 3 and means:
                means()
            split_dve(dve, C, n)

    def act_product(act, name, ends, tiles=None, last=False, turn=None, turn0=None, squares=None, root=None):
        C0, A0 = CHUNK0[name], ACC0[name]
        act_splits(act, C0, turn0, NCH - 1, tiles, squares)
        if root is not None:
            act_root(act, root)
        c = 0
        for count, end in ends:
            if c == 0:
                if end:
                    end(C0, A0, 0)
                c, count = 1, count - 1
            if last and c + count == dict(ORDER)[name]:
                count -= 1
            if count:
                with act.Fori(c - 1, c + count - 1) as j:
                    act_splits(act, j + (C0 + 1), turn, j)
                    if end:
                        end(j + (C0 + 1), j + (A0 + 1), j + 1)
            c += count
        if last:
            split_act(act, C0 + c, AHEAD)
            if ends[-1][1]:
                ends[-1][1](C0 + c, A0 + c, c)

    def dve_product(dve, name, end=None, tiles=None, last=False, turn=None, turn0=None, norm=None, stop=None):
        C0, A0, n_chunks = CHUNK0[name], ACC0[name], stop or dict(ORDER)[name]
        dve_splits(dve, C0, turn0, NCH - 1, tiles, norm and (lambda: dve_means(dve, *norm)))
        if norm:
            dve_rstd(dve, norm[0])
        if end:
            end(C0, A0, 0)
        stop = n_chunks - (1 if last else 0)
        if stop > 1:
            with dve.Fori(0, stop - 1) as j:
                dve_splits(dve, j + (C0 + 1), turn, j)
                if end:
                    end(j + (C0 + 1), j + (A0 + 1), j + 1)
        if last:
            split_dve(dve, C0 + stop, AHEAD)
            end(C0 + stop, A0 + stop, stop)

    def pe_product(pe, name, lhs, src=None, run=None, ready=None, x_ready=None, turn=None, turn0=None,
                   stop=None):
        C0, A0, n_chunks = CHUNK0[name], ACC0[name], stop or dict(ORDER)[name]
        if src is not None:
            pe_first(pe, C0, A0, TILE0[run], lhs, src, ready)
        else:
            if x_ready:
                x_ready()
            for n in range(GT):
                if turn0 and n == GT - 1:
                    pe.wait_ge(tlo_done, turn0.T0 + KT)
                pe_group(pe, C0, A0, n, lhs, turn=pe_turn(pe, turn0, NCH - 1) if turn0 else None)
        if n_chunks > 1:
            with pe.Fori(0, n_chunks - 1) as j:
                pe_chunk(pe, j + (C0 + 1), j + (A0 + 1), lhs, turn=pe_turn(pe, turn, j) if turn else None)

    aT, bT = (aT_hi, aT_lo), (bT_hi, bT_lo)
    MLP_N = 4

    def freed(eng, name, n, t=None):
        for tt in (range(TOK) if t is None else [t]):
            eng.wait_ge(acc_free[tt], ACC0[name] + n)

    def by_residual(name, skip=0):
        def ready(pe, c):
            for t in range(TOK):
                pe.wait_ge(acc_free[t], c + (ACC0[name] + skip + 1))
        return ready

    def by_gate(layer):
        def ready(pe, c):
            pe.wait_ge(h_done, c * 2 + (layer * 8 + 2))
        return ready

    turn_out = [Turn("ab_out", bT, 1, by_residual("ab_out")), Turn("c_out", bT, 4, by_residual("c_out"))]
    turn_mlp = [Turn("mlp0", bT, 2, by_residual("mlp0", 28)), Turn("mlp1", bT, 5, by_residual("mlp1", 28))]
    turn_gate = Turn("gate0", aT, 3, by_gate(0))
    out_name = ("ab_out", "c_out")

    def after_residual(pe, name, skip=0):
        def ready(kt):
            if kt % GT == 0:
                freed(pe, name, skip + kt // GT + 1)
        return ready

    def once(wait):
        def ready(kt):
            if kt == 0:
                wait()
        return ready


    def hidden(l, j):
        def ready(pe, c):
            pe.wait_ge(hid_done, c * 2 + j * 8 + (l * 32 + 2))
        tr = Turn(f"hidden{l}", aT, None, ready)
        tr.T0 = j * KT + tr.T0
        return tr

    def quarters(eng, body):
        with eng.Fori(0, MLP_N - 1) as j:
            body(j, False)
        body(MLP_N - 1, True)

    def pe_mlp(pe, l):
        C0, A0 = CHUNK0[f"mlp{l}"], ACC0[f"mlp{l}"]

        def quarter(j, last):
            tr = hidden(l, j)
            pe_chunk(pe, j * 8 + C0, j * 8 + A0, bT)
            with pe.Fori(0, NCH - 1) as c:
                pe_chunk(pe, c + j * 8 + (C0 + 1), c + j * 8 + (A0 + 1), bT, turn=pe_turn(pe, tr, c))
            for n in range(GT):
                if n == GT - 1:
                    pe.wait_ge(tlo_done, tr.T0 + KT)
                pe_group(pe, j * 8 + (C0 + NCH), j * 8 + (A0 + NCH), n, aT, turn=pe_turn(pe, tr, NCH - 1))
            with pe.Fori(0, NCH - 1) as c:
                pe_chunk(pe, c + j * 8 + (C0 + NCH + 1), c + j * 8 + (A0 + NCH + 1), aT,
                         turn=pe_turn(pe, turn_mlp[l], c) if last else None)
        quarters(pe, quarter)

    def act_mlp(act, l, m):
        C0, A0 = CHUNK0[f"mlp{l}"], ACC0[f"mlp{l}"]

        def relu(j, c):
            act_project(act, c + j * 8 + C0, c + j * 8 + A0, m, lambda t: part[:, t, :], ACT.Relu)

        def quarter(j, last):
            tr = hidden(l, j)
            act_splits(act, j * 8 + C0)
            relu(j, 0)
            with act.Fori(0, NCH - 1) as c:
                act_splits(act, c + j * 8 + (C0 + 1), tr, c)
                relu(j, c + 1)
            act_splits(act, j * 8 + (C0 + NCH), tr, NCH - 1)
            if last:
                act_keep(act, A0 + 28, 0)
            with act.Fori(0, NCH - 1) as c:
                act_splits(act, c + j * 8 + (C0 + NCH + 1), turn_mlp[l] if last else None, c)
                if last:
                    act_keep(act, c + (A0 + 29), c * NW + NW)
        quarters(act, quarter)

    def pool_mlp(pool, l):
        A0 = ACC0[f"mlp{l}"]
        with pool.Fori(0, MLP_N) as j:
            with pool.Fori(0, NCH) as c:
                for t in range(TOK):
                    pool.wait_ge(acc_free[t], c + j * 8 + (A0 + 1))
                    pool.tensor_tensor(part[:, t, :], part[:, t, :], part[:, t, :], ALU.mult).then_inc(hid_done, 1)

    def dve_mlp(dve, l):
        C0, A0 = CHUNK0[f"mlp{l}"], ACC0[f"mlp{l}"]

        def quarter(j, last):
            tr = hidden(l, j)
            dve_splits(dve, j * 8 + C0)
            with dve.Fori(0, NCH - 1) as c:
                dve_splits(dve, c + j * 8 + (C0 + 1), tr, c)
            dve_splits(dve, j * 8 + (C0 + NCH), tr, NCH - 1)
            dve_residual(dve, j * 8 + (C0 + NCH), j * 8 + (A0 + NCH), 0, last)
            with dve.Fori(0, NCH - 1) as c:
                dve_splits(dve, c + j * 8 + (C0 + NCH + 1), turn_mlp[l] if last else None, c)
                dve_residual(dve, c + j * 8 + (C0 + NCH + 1), c + j * 8 + (A0 + NCH + 1), c * NW + NW, last)
        quarters(dve, quarter)

    def act_round_p(act, l):
        act.wait_ge(p_in, 16 * (l + 1))
        act.activation(pT_hi[:, :, :], pT[:, :, :], ACT.Copy).then_inc(p_hi, 1)

    def dve_split_p(dve, l):
        dve.wait_ge(p_hi, l + 1)
        dve.tensor_tensor(pT_lo[:, :, :], pT[:, :, :], pT_hi[:, :, :].bitcast(F32), ALU.subtract).then_inc(p_lo, 1)

    def act_proj(act, l, m):
        C0, A0 = CHUNK0[f"proj{l}"], ACC0[f"proj{l}"]
        for n in range(NCH):
            split_act(act, C0, AHEAD + n)
            if n == 1:
                act_turn(act, turn_out[l], NCH - 1)
            if n == 2:
                act_norm(act, m, lambda: act.wait_ge(kept, 8 + 24 * l))
            if n == 3:
                act_root(act, m)
            for t in range(TOK):
                if t == 0:
                    act.wait_ge(acc0_done, A0 + n + 1)
                else:
                    act.wait_ge(group_used, C0 * GT + n + 1)
                act.activation(proj[:, t, n * NW:(n + 1) * NW], acc[t][:, :], ACT.Copy).then_inc(acc_free[t], 1)

    def dve_proj(dve, l, m):
        for n in range(NCH):
            if n == 1:
                dve_turn(dve, turn_out[l], NCH - 1)
            split_dve(dve, CHUNK0[f"proj{l}"], AHEAD + n)
        dve_means(dve, m, 1e-6)
        dve_rstd(dve, m)

    def pe_proj(pe, l):
        C0, A0 = CHUNK0[f"proj{l}"], ACC0[f"proj{l}"]
        pe.wait_ge(p_lo, l + 1)
        for n in range(NCH):
            pe.wait_ge(split_done, C0 * GT + n + 1)
            for t in range(TOK):
                pe.wait_ge(acc_free[t], A0 + n)
                for kt in range(2):
                    for a, w in ((pT_hi, w_hi), (pT_hi, w_lo), (pT_lo, w_hi)):
                        mm = pe.matmul(acc[t][:, :], a[:, kt, t * P:(t + 1) * P], w[:, n, kt, :],
                                       start=(kt == 0 and a is pT_hi and w is w_hi), stop=(kt == 1 and a is pT_lo))
                if t == 0:
                    mm.then_inc(acc0_done, 1)
            mm.then_inc(group_used, 1)
            if n == 1:
                for i in range(GT):
                    pe_turn(pe, turn_out[l], NCH - 1)(i)
        pe.wait_ge(tlo_done, turn_out[l].T0 + KT)

    def act_gate_end(act, l, m):
        def end(C, A_, c):
            if not isinstance(c, int) or c > 0:
                act.wait_ge(h_done, c * 2 + l * 8)
            act_project(act, C, A_, m, lambda t: gpart[:, t, :], ACT.Sigmoid)
            if l == 0:
                for t in range(TOK):
                    act.wait_ge(h_done, c * 2 + (t + 1))
                    act.activation(h[:, t, bass.ds(c * NW, NW)], part[:, t, :], ACT.Copy).then_inc(kept, 1)
        return end

    def pool_gate(pool, l):
        A0 = ACC0[f"gate{l}"]
        with pool.Fori(0, NCH) as c:
            for t in range(TOK):
                pool.wait_ge(acc_free[t], c + (A0 + 1))
                pool.tensor_tensor(gpart[:, t, :], gpart[:, t, :], proj[:, t, bass.ds(c * NW, NW)], ALU.mult)\
                    .then_inc(gp_done, 1)

    def dve_gate_end(dve, l):
        def end(C, A_, c):
            for t in range(TOK):
                dve.wait_ge(gp_done, c * 2 + (l * 8 + t + 1))
                old = h[:, t, bass.ds(c * NW, NW)]
                dve.tensor_tensor(part[:, t, :] if l == 0 else old, old, gpart[:, t, :], ALU.add).then_inc(h_done, 1)
        return end

    def residual_end(dve, to_part=False):
        return lambda C, A_, c: dve_residual(dve, C, A_, c * NW, to_part)

    def put(z, base=0):
        return lambda c: (lambda t: z[:, t, bass.ds(c * NW + base, NW)])

    def project_end(act, m, z, func=ACT.Copy):
        return lambda C, A_, c: act_project(act, C, A_, m, put(z)(c), func)

    def act_norm(act, m, wait):
        wait()
        if m > 0:
            act.wait_ge(ms_done, m)
        for t in range(TOK):
            if t > 0:
                act.wait_ge(sq_done, TOK * m + t)
            act.activation(pa[:, :, :].rearrange("p a b -> p (a b)"), h[:, t, :], ACT.Square,
                           accum_out=stat[:, 0, t:t + 1]).then_inc(sq_done, 1)

    block = ctx.enter_context(nc.Block())

    @block.sync
    def _(sp):
        for g in range(RAW):
            sp.dma_start(raw[:, g].rearrange("p a b -> p (a b)"), wstream[g]).then_inc(landed[g], 16)

        def stream(first, last):
            with sp.Fori(first, last) as i:
                for g in range(RAW):
                    sp.wait_ge(split_done, i * RAW + (g + 1 - RAW))
                    sp.dma_start(raw[:, g].rearrange("p a b -> p (a b)"),
                                 wstream[bass.ds(i * RAW + g, 1)].rearrange("g p n -> (g p) n"))\
                        .then_inc(landed[g], 16)

        at1, at2, at3 = (CHUNK0[x] * GT // RAW + 2 for x in ("c_out", "ab2_out", "c2_out"))
        stream(1, at1)
        freed(sp, "gates", 1)
        sp.wait_ge(group_used, CHUNK0["cmp_k"] * GT + CMP_GROUPS)
        each_round(sp, attn1, sp_round)
        stream(at1, at2)
        freed(sp, "ab2_in", 13)
        each_round(sp, attn2a, sp_round)
        each_round(sp, attn2b, sp_round)
        stream(at2, at3)
        freed(sp, "c2_in", 16)
        sp.wait_ge(rpb_out, 16 * RPB_DMAS)
        each_round(sp, attn3, sp_round)
        stream(at3, NC * GT // RAW)
        sp.wait_ge(fin_done, 2)
        sp.dma_start(out.rearrange("b (t p) d -> p (b t) d", p=P), h[:, :, :]).then_inc(out_done, 16)
        sp.wait_ge(out_done, 16)
        sp.wait_ge(rpb_out, 16 * RPB_DMAS)

    @block.gpsimd
    def _(pool):
        pool.memset(bd[:, :, :, :], 0.0).then_inc(bd_zero, 1)
        pool.wait_ge(bd_zero, 1)
        for n, w in enumerate((A["w_r"], A["w_i"])):
            for half in range(2):
                pool.dma_start(bd[half * 64:half * 64 + 64, n, :, half * 64:half * 64 + 64],
                               w.rearrange("(j a) i o -> a i j o", a=2)[half]).then_inc(bd_in, 16)
        pool.memset(uT[:, :, 0:PADP], 0.0).then_inc(pads_zero, 1)
        pool.wait_ge(m_ev, 2 * LT)
        pool.wait_ge(pads_zero, 1)
        pool.wait_ge(lru_dve, 2 * LRU_STEPS)
        N = PADP + S
        pool.tensor_tensor(pw0[:, :, 1:N], uT[:, :, 1:N], uT[:, :, 0:N - 1], ALU.add).then_inc(pool_step, 1)
        pool.wait_ge(pool_step, 1)
        pool.tensor_tensor(pw1[:, :, 3:N], pw0[:, 2:8, 3:N], pw0[:, 2:8, 1:N - 2], ALU.add).then_inc(pool_step, 1)
        pool.wait_ge(pool_step, 2)
        pool.tensor_tensor(pw0[:, 4:8, 7:N], pw1[:, 2:6, 7:N], pw1[:, 2:6, 3:N - 4], ALU.add).then_inc(pool_step, 1)
        pool.wait_ge(pool_step, 3)
        pool.tensor_tensor(pw1[:, 4:6, 15:N], pw0[:, 6:8, 15:N], pw0[:, 6:8, 7:N - 8], ALU.add).then_inc(pool_step, 1)
        pool.wait_ge(pool_step, 4)
        for g, s in enumerate((pw0[:, 0:2], pw1[:, 0:2], pw0[:, 4:6], pw1[:, 4:6])):
            win = 2 << g
            pool.tensor_tensor(s[:, :, PADP:2 * PADP], s[:, :, PADP:2 * PADP],
                               invcnt[:, g, :].unsqueeze(1).broadcast_to([P, 2, PADP]), ALU.mult).then_inc(pool_step, 1)
            pool.tensor_scalar(s[:, :, 2 * PADP:], s[:, :, 2 * PADP:], 1.0 / win, None, ALU.mult).then_inc(pool_step, 1)
            pool.wait_ge(pool_step, 4 + 3 * g + 2)
            pool.tensor_tensor(uT[:, 2 * g:2 * g + 2, PADP:], s[:, :, PADP:], uT[:, 2 * g:2 * g + 2, PADP:],
                               ALU.subtract).then_inc(pool_step, 1)
        pool.wait_ge(mix_lo, 6)
        pool.wait_ge(pool_mm, 8)
        pool.dma_start(pT[:, :, :], A["pT"][0].rearrange("(k p) s -> p k s", p=P)).then_inc(p_in, 16)
        b3 = A["bias3"]
        for hh in range(NH):
            for r in range(4):
                t, half = r // 2, r % 2
                src = bass.AP(tensor=A["rpb"].tensor, offset=(hh * 15 + 7 - r) * 64 * 128 + 63,
                              ap=[[127, 64], [64 * 128, 4], [1, 64]])
                dst = b3[hh // 4, half * 64:half * 64 + 64, bass.ds((hh % 4) * 512 + t * S, S)]\
                    .rearrange("p (k c) -> p k c", k=4)
                pool.dma_start(dst, src).then_inc(rpb_out, 16)
        pool_mlp(pool, 0)
        pool_gate(pool, 0)
        freed(pool, "c_in", 1)
        pool.dma_start(gw[:, :], A["gate_w"]).then_inc(cmp_in, 16)
        pool.dma_start(posT[:, :, :], A["posT"].rearrange("a d l -> d a l")).then_inc(cmp_in, 16)
        pool.wait_ge(cmp_in, 32)
        pool.memset(blk[:, CL * M:], 0.0).then_inc(blk_done, 1)
        for kv in range(2):
            pool.wait_ge(c_ev, kv * 4 + 4)
            if kv == 1:
                pool.wait_ge(gates_done, 1)
                pool.dma_start(cw2[:, 0], A["w2_k"].rearrange("(f p) d -> p f d", p=P)).then_inc(cmp_in, 16)
                pool.dma_start(cw2[:, 1], A["w2_v"].rearrange("(f p) d -> p f d", p=P)).then_inc(cmp_in, 16)
                pool.wait_ge(blk_lo_done, 2)
            for g in range(NKV):
                v = cT[:, kv, g, :].rearrange("p (m j) -> p j m", j=16)
                rows = blk[:, 0:CL * M].rearrange("p (t n) -> p t n", n=M)
                for a in range(2):
                    b = pool.tensor_tensor(
                        rows[:, 16 * a:16 * a + 16, g * NCMP:(g + 1) * NCMP], v[:, :, a:a + NCMP],
                        posT[:, kv, 16 * a:16 * a + 16].unsqueeze(2).broadcast_to([P, 16, NCMP]), ALU.add)
            b.then_inc(blk_done, 1)
        pool.wait_ge(tlo_done, TILE0["y1"] + KT)
        pool.dma_start(pT[:, :, :], A["pT"][1].rearrange("(k p) s -> p k s", p=P)).then_inc(p_in, 16)
        pool_mlp(pool, 1)
        pool_gate(pool, 1)
        pool.dma_start(gfull[:, :], A["g1"]).then_inc(g_in, 16)
        each_round(pool, attn3, pool_mask)
        pool.wait_ge(tlo_done, TILE0["c2_out"] + KT)
        pool.dma_start(gfull[:, :], A["g2"]).then_inc(g_in, 16)

    @block.scalar
    def _(act):
        act.dma_start(gains[:, :, :], A["gains"]).then_inc(gains_in, 16)
        for n in range(GT):
            act.dma_start(xT[:, GT * n:GT * (n + 1), :], A["xT"].rearrange("(g k p) s -> g p k s", p=P, k=GT)[n])\
                .then_inc(x_in[n], 16)
        loads = [(ident[:, :], A["ident"]), (h[:, :, :], A["x"].rearrange("b (t p) d -> p (b t) d", p=P)),
                 (vecs[:, :, :], A["vecs"]), (invcnt[:, :, :], A["invcnt"]), (pool_w[:, :, :], A["pool_w"]),
                 (sinks[:, :], A["sinks"]), (bias_c[:, :, :, :], A["bias_c"]), (valid_c[:, :, :], A["valid_c"]),
                 (mask3[:, :], A["mask3"])]
        assert len(loads) == LOADS
        for dst, src in loads:
            act.dma_start(dst, src).then_inc(const_in, 16)

        def round_x(n):
            if n == 0:
                act.wait_ge(gains_in, 16)
            act.wait_ge(x_in[n], 16)
            for kt in range(GT * n, GT * (n + 1)):
                act.activation(aT_hi[:, kt], xT[:, kt], ACT.Copy, scale=gains[:, 0, kt:kt + 1]).then_inc(thi_done, 1)
        for n in range(AHEAD):
            round_x(n)
            split_act(act, 0, n)
        round_x(AHEAD)

        def first():
            act.wait_ge(const_in, 16 * LOADS)
            act_norm(act, 0, lambda: None)
            act.wait_ge(dve_chain, 1)
            act.activation(soft[:, 1], soft[:, 0], ACT.Exp, scale=-1.0).then_inc(soft_exp, 1)
            act_root(act, 0)
        def mixer_tiles(c):
            for i in range(GT):
                k = GT * c + i
                act.wait_ge(m_tp, k + 1)
                dst = xr[:, k, PADC:] if k < LT else uT[:, k - LT, PADP:]
                act.activation(dst, tp[k % 2][:, 0:S], ACT.Copy).then_inc(m_ev, 1)

        def decays(half):
            for q in range(GT):
                j = GT * half + q
                act.wait_ge(gates_mm, j + 1)
                act.activation(rg[:, j], pa[:, q, 0:S], ACT.Sigmoid, bias=vecs[:, 5, j:j + 1])
                act.activation(ig[:, j], pa[:, q, S:2 * S], ACT.Sigmoid, bias=vecs[:, 6, j:j + 1]).then_inc(gates_sg, 1)
            act.wait_ge(gates_sg, GT * (half + 1))
            tiles = range(GT * half, GT * (half + 1))
            for j in tiles:
                e = act.activation(th[:, j], rg[:, j], ACT.Tanh, scale=soft[:, 2, j:j + 1])
            e.then_inc(tanh_done, 1)
            for j in tiles:
                e = act.activation(rg[:, j], rg[:, j], ACT.Exp, scale=soft[:, 3, j:j + 1])
            e.then_inc(decay_done, 1)

        def root(half):
            act.wait_ge(lru_dve, LRU_STEPS * half + 3)
            t = th[:, GT * half:GT * (half + 1), :]
            act.activation(t, t, ACT.Sqrt, scale=2.0).then_inc(lru_root, 1)

        def round_lru(half):
            act.wait_ge(gated, GT * (half + 1))
            act.wait_ge(group_used, CHUNK0["ab_in"] * GT + 5 * GT + 3 + half)
            act.activation(aT_hi[:, LT + GT * half:LT + GT * (half + 1), :], xc[:, GT * half:GT * (half + 1), :],
                           ACT.Copy).then_inc(mix_hi, 1)
        C0, A0 = CHUNK0["ab_in"], ACC0["ab_in"]
        for c in range(6):
            split_act(act, C0 + c, AHEAD)
            split_act(act, C0 + c, AHEAD + 1)
            if 1 <= c <= 4:
                mixer_tiles(c - 1)
            split_act(act, C0 + c, AHEAD + 2)
            if c in (2, 3):
                decays(c - 2)
            if c in (3, 4):
                root(c - 3)
            split_act(act, C0 + c, AHEAD + 3)
            if c == 0:
                first()
            if c > 0:
                act.wait_ge(m_tp, GT * c)
            act_project(act, C0 + c, A0 + c, 0, lambda t: part[:, t, :], ACT.Copy if c < 4 else ACT.Gelu_apprx_tanh)
            if c == 5:
                for g in range(4):
                    act.wait_ge(pool_mm, 2 * g + 2)
                    act.wait_ge(group_used, (C0 + 5) * GT + g // 2 + 1)
                    for j in (2 * g, 2 * g + 1):
                        e = act.activation(aT_hi[:, j, :], pa[:, g, (j % 2) * S:(j % 2 + 1) * S], ACT.Copy,
                                           scale=vecs[:, 8, j:j + 1])
                    e.then_inc(mix_hi, 1)
        round_lru(0)
        C0, A0 = CHUNK0["ab_out"], ACC0["ab_out"]
        for n in range(AHEAD, AHEAD + GT):
            if n == AHEAD + 2:
                round_lru(1)
            split_act(act, C0, n)
        act_keep(act, A0, 0)
        act_round_p(act, 0)
        with act.Fori(0, NCH - 1) as j:
            act_splits(act, j + (C0 + 1), turn_out[0], j)
            act_keep(act, j + (A0 + 1), j * NW + NW)
        act_proj(act, 0, 1)
        act_mlp(act, 0, 1)

        def tiles_of(run, gain=None):
            return lambda tiles: act_tiles(act, TILE0[run], aT_hi, gain, tiles)
        act_product(act, "gate0", [(4, act_gate_end(act, 0, 2))], turn=turn_gate, turn0=turn_mlp[0],
                    squares=lambda: act_norm(act, 2, lambda: act.wait_ge(kept, 16)), root=2)
        act_product(act, "c_in", [(10, project_end(act, 3, z1))], turn0=turn_gate,
                    squares=lambda: act_norm(act, 3, lambda: act.wait_ge(kept, 24)), root=3)
        act.wait_ge(cmp_in, 32)
        act.activation(gw_hi[:, :], gw[:, :], ACT.Copy).then_inc(gw_hi_done, 1)
        C, B = CHUNK0["cmp_k"], CHUNK0["cmp_k"] * GT

        def round_blocks(kv, part):
            a = BLK_PARTS[part]
            act.activation(blk_hi[kv][:, a], blk[:, a], ACT.Copy).then_inc(blk_hi_done, 1)

        def hidden_end(kv):
            act.wait_ge(group_used, B + (V_GROUP, CMP_GROUPS)[kv])
            if kv == 1:
                act.wait_ge(chid_tp, 1)
            act.activation(chid[:, :], acc[kv][0:M, :], ACT.Gelu_apprx_tanh).then_inc(chid_done, 1)
        split_act(act, C, AHEAD)
        act.wait_ge(gates_done, 1)
        act.wait_ge(blk_done, 2)
        round_blocks(0, 0)
        round_blocks(0, 1)
        for m in range(AHEAD + 1, CMP_GROUPS + AHEAD):
            if m == AHEAD + 2:
                act.wait_ge(gates_tp, 1)
                for t in range(TOK):
                    e = act.activation(z1[:, t, C_GATES:W_C], acc[1][:, t * P:t * P + NG], ACT.Sigmoid,
                                       scale=rstd[:, t:t + 1])
                e.then_inc(acc_free[1], 1)
            if m == V_GROUP:
                act.wait_ge(blk_done, 3)
                round_blocks(1, 0)
                round_blocks(1, 1)
            if m == V_GROUP + AHEAD:
                hidden_end(0)
            if m == CMP_GROUPS:
                hidden_end(1)
            split_act(act, C, m)
        act_attention(act, attn1)
        def out_end(C, A_, c):
            act_keep(act, A_, c * NW)
            if isinstance(c, int):
                act_round_p(act, 1)
        act_product(act, "c_out", [(4, out_end)], tiles_of("y1"), turn=turn_out[1])
        act_proj(act, 1, 4)
        act_mlp(act, 1, 4)
        act_product(act, "gate1", [(4, act_gate_end(act, 1, 5))], turn0=turn_mlp[1],
                    squares=lambda: act_norm(act, 5, lambda: act.wait_ge(kept, 40)), root=5)
        act_norm(act, 6, lambda: act.wait_ge(h_done, 16))
        act_root(act, 6)

        act_product(act, "ab2_in", [(9, project_end(act, 7, z2)), (4, project_end(act, 7, z2, ACT.Silu))],
                    tiles_of("ab2_in", 6), squares=lambda: act_norm(act, 7, lambda: act.wait_ge(fin_done, 1)), root=7)
        act_attention(act, attn2a)
        act_attention(act, attn2b)
        act_product(act, "ab2_out", [(4, None)], tiles_of("ab2_out"))

        act_product(act, "c2_in", [(12, project_end(act, 8, z3)), (4, project_end(act, 8, z3, ACT.Silu))],
                    tiles_of("c2_in", 7), squares=lambda: act_norm(act, 8, lambda: freed(act, "ab2_out", 4)), root=8)
        act_attention(act, attn3)
        act_product(act, "c2_out", [(4, None)], tiles_of("c2_out"), last=True)
        act_norm(act, 9, lambda: freed(act, "c2_out", 4))
        act_root(act, 9)

    @block.vector
    def _(dve):
        chain = [0]

        def link(ins):
            chain[0] += 1
            ins.then_inc(dve_chain, 1)
            dve.wait_ge(dve_chain, chain[0])

        lam, mag, y, sp, neg = vecs[:, 7], soft[:, 0], soft[:, 1], soft[:, 2], soft[:, 3]

        def split_x(n):
            if n == 0:
                dve.wait_ge(gains_in, 16)
            dve.wait_ge(x_in[n], 16)
            for kt in range(GT * n, GT * (n + 1)):
                dve.wait_ge(thi_done, kt + 1)
                dve.scalar_tensor_tensor(out=aT_lo[:, kt], in0=xT[:, kt], scalar=gains[:, 0, kt:kt + 1],
                                         in1=aT_hi[:, kt].bitcast(F32), op0=ALU.mult, op1=ALU.subtract)\
                    .then_inc(tlo_done, 1)
        for n in range(AHEAD):
            split_x(n)
            split_dve(dve, 0, n)
        split_x(AHEAD)

        def first():
            dve.wait_ge(const_in, 16 * LOADS)
            link(dve.scalar_tensor_tensor(out=mag, in0=lam, scalar=-1.0, in1=lam, op0=ALU.mult, op1=ALU.max))
            dve_means(dve, 0, 1e-6)
            dve.wait_ge(soft_exp, 1)
            link(dve.tensor_scalar(sp, y, 2.0, None, ALU.add))
            link(dve.reciprocal(sp, sp))
            link(dve.tensor_tensor(y, y, sp, ALU.mult))
            link(dve.tensor_tensor(mag, y, y, ALU.mult))
            link(dve.tensor_scalar(sp, mag, 1.0 / 19, None, ALU.mult))
            for n in range(17, 1, -2):
                link(dve.scalar_tensor_tensor(out=sp, in0=sp, scalar=1.0 / n, in1=mag, op0=ALU.add, op1=ALU.mult))
            link(dve.scalar_tensor_tensor(out=sp, in0=sp, scalar=1.0, in1=y, op0=ALU.add, op1=ALU.mult))
            link(dve.tensor_scalar(mag, lam, -1.0, 0.0, ALU.mult, ALU.max))
            link(dve.scalar_tensor_tensor(out=sp, in0=sp, scalar=2.0, in1=mag, op0=ALU.mult, op1=ALU.add))
            link(dve.tensor_scalar(neg, sp, -8.0, None, ALU.mult))
            link(dve.tensor_scalar(sp, sp, 8.0, None, ALU.mult))
            dve_rstd(dve, 0)
        def conv(half):
            if half == 0:
                dve.wait_ge(m_ev, GT)
            else:
                dve.wait_ge(m_ev, 2 * GT)
            tiles = range(GT * half, GT * (half + 1))
            for k in range(4):
                for q, j in enumerate(tiles):
                    if k == 0:
                        dve.tensor_scalar(xc[:, j], xr[:, j, 0:S], vecs[:, 0, j:j + 1], vecs[:, 4, j:j + 1],
                                          ALU.mult, ALU.add).then_inc(conv_step, 1)
                    else:
                        dve.wait_ge(conv_step, 12 * half + GT * (k - 1) + q + 1)
                        d = dve.scalar_tensor_tensor(out=xc[:, j], in0=xr[:, j, k:k + S], scalar=vecs[:, k, j:j + 1],
                                                     in1=xc[:, j], op0=ALU.mult, op1=ALU.add)
                        d.then_inc(*((conv_done, 4) if k == 3 else (conv_step, 1)))

        def lru_inputs(half):
            a = slice(GT * half, GT * (half + 1))
            w = xr[:, a, 0:S]
            n = LRU_STEPS * half
            dve.wait_ge(tanh_done, half + 1)
            dve.wait_ge(conv_done, 4 * GT * (half + 1))
            dve.tensor_scalar(w, th[:, a, :], 1.0, None, ALU.add).then_inc(lru_dve, 1)
            dve.wait_ge(lru_dve, n + 1)
            dve.reciprocal(w, w).then_inc(lru_dve, 1)
            dve.wait_ge(lru_dve, n + 2)
            dve.tensor_tensor(th[:, a, :], th[:, a, :], w, ALU.mult).then_inc(lru_dve, 1)
            dve.wait_ge(gates_sg, GT * (half + 1))
            dve.tensor_tensor(ig[:, a, :], ig[:, a, :], xc[:, a, :], ALU.mult).then_inc(lru_dve, 1)

        def lru(half):
            a = slice(GT * half, GT * (half + 1))
            n = LRU_STEPS * half
            dve.wait_ge(lru_root, half + 1)
            dve.wait_ge(lru_dve, n + 4)
            dve.tensor_tensor(ig[:, a, :], ig[:, a, :], th[:, a, :], ALU.mult).then_inc(lru_dve, 1)
            dve.wait_ge(lru_dve, n + 5)
            dve.wait_ge(decay_done, half + 1)
            for j in range(GT * half, GT * (half + 1)):
                s = dve.tensor_tensor_scan(xc[:, j], rg[:, j], ig[:, j], 0.0, ALU.mult, ALU.add)
            s.then_inc(lru_dve, 1)

        def gate_tiles(half):
            dve.wait_ge(lru_dve, LRU_STEPS * (half + 1))
            for j in range(GT * half, GT * (half + 1)):
                dve.wait_ge(m_tp, 2 * LT + j + 1)
                dve.tensor_tensor(xc[:, j], tp[j % 2][:, 0:S], xc[:, j], ALU.mult).then_inc(gated, 1)

        def split_lru(half):
            dve.wait_ge(mix_hi, 5 + half)
            a, b = slice(GT * half, GT * (half + 1)), slice(LT + GT * half, LT + GT * (half + 1))
            dve.tensor_tensor(aT_lo[:, b, :], xc[:, a, :], aT_hi[:, b, :].bitcast(F32), ALU.subtract)\
                .then_inc(mix_lo, 1)
        C0 = CHUNK0["ab_in"]
        for c in range(6):
            split_dve(dve, C0 + c, AHEAD)
            if c in (3, 4):
                lru_inputs(c - 3)
            split_dve(dve, C0 + c, AHEAD + 1)
            if c in (1, 2):
                conv(c - 1)
            if c == 5:
                gate_tiles(0)
            split_dve(dve, C0 + c, AHEAD + 2)
            if c in (3, 4):
                lru(c - 3)
            split_dve(dve, C0 + c, AHEAD + 3)
            if c == 0:
                first()
                link(dve.memset(xr[:, :, 0:PADC], 0.0))
        for g in range(4):
            dve.wait_ge(mix_hi, g + 1)
            for j in (2 * g, 2 * g + 1):
                d = dve.scalar_tensor_tensor(out=aT_lo[:, j, :], in0=pa[:, g, (j % 2) * S:(j % 2 + 1) * S],
                                             scalar=vecs[:, 8, j:j + 1], in1=aT_hi[:, j, :].bitcast(F32),
                                             op0=ALU.mult, op1=ALU.subtract)
            d.then_inc(mix_lo, 1)
        split_lru(0)
        C0, A0 = CHUNK0["ab_out"], ACC0["ab_out"]
        for n in range(AHEAD, AHEAD + GT):
            if n == AHEAD + 2:
                gate_tiles(1)
                split_lru(1)
            split_dve(dve, C0, n)
        dve_residual(dve, C0, A0, 0, True)
        dve_split_p(dve, 0)
        with dve.Fori(0, NCH - 1) as j:
            dve_splits(dve, j + (C0 + 1), turn_out[0], j)
            dve_residual(dve, j + (C0 + 1), j + (A0 + 1), j * NW + NW, True)
        dve_proj(dve, 0, 1)
        dve_mlp(dve, 0)

        def tiles_of(run, gain=None):
            return lambda tiles: dve_tiles(dve, TILE0[run], aT_hi, aT_lo, gain, tiles)
        dve_product(dve, "gate0", dve_gate_end(dve, 0), turn=turn_gate, turn0=turn_mlp[0], norm=(2, 1e-6))
        def kv_tiles(half):
            for n in range(NKV * half, NKV * (half + 1)):
                dve.wait_ge(c_tp, n + 1)
                dve.tensor_copy(cT[:, half, n % NKV, :], tp[n % 2][:, 0:S]).then_inc(c_ev, 1)
        dve_product(dve, "c_in", None, turn0=turn_gate, norm=(3, 1e-6), stop=8)
        for half in range(2):
            for n in range(AHEAD, AHEAD + GT):
                if n == AHEAD + 2:
                    kv_tiles(half)
                split_dve(dve, CHUNK0["c_in"] + 8 + half, n)
        dve.wait_ge(gw_hi_done, 1)
        dve.tensor_tensor(gw_lo[:, :], gw[:, :], gw_hi[:, :].bitcast(F32), ALU.subtract).then_inc(gw_lo_done, 1)

        def split_blocks(kv, part):
            a = BLK_PARTS[part]
            dve.wait_ge(blk_hi_done, 2 * kv + part + 1)
            dve.tensor_tensor(blk_lo[kv][:, a], blk[:, a], blk_hi[kv][:, a].bitcast(F32), ALU.subtract)\
                .then_inc(blk_lo_done, 1)

        def hidden_tiles(kv):
            dve.wait_ge(chid_tp, kv + 1)
            if kv == 1:
                dve.wait_ge(cmp_mm, 1)
            dve.tensor_copy(chidT[:, 0:HID // P * M], tp[0][:, 0:HID // P * M]).then_inc(chid_ev, 1)

        def compressed(kv):
            dve.wait_ge(cmp_mm, kv + 1)
            if kv == 0:
                dve.tensor_scalar(kcmpT[:, :], tp[1][:, 0:M], QSCALE ** 0.5, None, ALU.mult).then_inc(cmp_ev, 1)
            else:
                dve.tensor_copy(vcmp[:, :, :], tp[1][0:NCMP, :].rearrange("n (g d) -> n g d", g=NKV)).then_inc(cmp_ev, 1)
        C = CHUNK0["cmp_k"]
        split_dve(dve, C, AHEAD)
        dve.wait_ge(gates_done, 1)
        dve.tensor_copy(gatesT[0:NG, :], acc[0][0:NG, 0:S]).then_inc(acc_free[0], 1)
        split_blocks(0, 0)
        split_blocks(0, 1)
        for m in range(AHEAD + 1, CMP_GROUPS + AHEAD):
            if m == V_GROUP:
                split_blocks(1, 0)
                split_blocks(1, 1)
            if m == CMP_GROUPS:
                hidden_tiles(1)
                compressed(1)
            split_dve(dve, C, m)
            if m == V_GROUP + 3:
                hidden_tiles(0)
            if m == V_GROUP + 6:
                compressed(0)
        dve_attention(dve, attn1)
        def out_end(C, A_, c):
            dve_residual(dve, C, A_, c * NW, True)
            if isinstance(c, int):
                dve_split_p(dve, 1)
        dve_product(dve, "c_out", out_end, tiles_of("y1"), turn=turn_out[1])
        dve_proj(dve, 1, 4)
        dve_mlp(dve, 1)
        dve_product(dve, "gate1", dve_gate_end(dve, 1), turn0=turn_mlp[1], norm=(5, 1e-6))

        def final(m, n, eps):
            dve_means(dve, m, eps)
            dve_rstd(dve, m)
            dve.wait_ge(rstd_done, m + 1)
            dve.wait_ge(g_in, 16 * n)
            for t in range(TOK):
                f = dve.scalar_tensor_tensor(out=h[:, t, :], in0=h[:, t, :], scalar=rstd[:, t:t + 1], in1=gfull[:, :],
                                             op0=ALU.mult, op1=ALU.mult)
            f.then_inc(fin_done, 1)
        final(6, 1, 1e-6)
        dve_product(dve, "ab2_in", None, tiles_of("ab2_in", 6), norm=(7, 1e-5))
        dve_attention(dve, attn2a)
        dve_attention(dve, attn2b)
        dve_product(dve, "ab2_out", residual_end(dve), tiles_of("ab2_out"))
        dve_product(dve, "c2_in", None, tiles_of("c2_in", 7), norm=(8, 1e-5))
        dve_attention(dve, attn3)
        dve_product(dve, "c2_out", residual_end(dve), tiles_of("c2_out"), last=True)
        final(9, 2, 1e-5)

    @block.tensor
    def _(pe):
        def mixer_turn(c):
            def turn(i):
                k = GT * c + i
                if i == 0:
                    freed(pe, "ab_in", c + 1)
                if 2 <= k < 18:
                    pe.wait_ge(m_ev, k - 1)
                elif k >= 18:
                    pe.wait_ge(gated, k - 17)
                for t in range(TOK):
                    mm = pe.transpose(tp[k % 2][:, t * P:(t + 1) * P], part[:, t, i * P:(i + 1) * P], ident[:, :])
                mm.then_inc(m_tp, 1)
            return turn

        def gate_products(half):
            if half == 0:
                pe.wait_ge(bd_in, 64)
            for q in range(GT):
                j = GT * half + q
                pe.wait_ge(conv_done, 4 * (j + 1))
                if half == 1:
                    pe.wait_ge(gates_sg, q + 1)
                for n in range(2):
                    mm = pe.matmul(pa[:, q, n * S:(n + 1) * S], bd[:, n, j, :], xc[:, j, :], start=True, stop=True)
                mm.then_inc(gates_mm, 1)

        def pool_products(tiles):
            pe.wait_ge(gates_sg, LT)
            for j in tiles:
                g, jo = j // 2, j % 2
                pe.wait_ge(pool_step, 4 + 3 * g + 3)
                for i2 in range(2):
                    mm = pe.matmul(pa[:, j // 2, jo * S:(jo + 1) * S], pool_w[:, 2 * g + i2, jo * P:(jo + 1) * P],
                                   uT[:, 2 * g + i2, PADP:], start=(i2 == 0), stop=(i2 == 1))
                mm.then_inc(pool_mm, 1)

        def before_group(c):
            def before(n):
                if c == 0:
                    pe.wait_ge(tlo_done, GT * (n + 1))
                if c in (2, 3) and n == 3:
                    gate_products(c - 2)
                if c == 5 and n >= 2:
                    pool_products(range(4 * (n - 2), 4 * (n - 1)))
            return before
        C0, A0 = CHUNK0["ab_in"], ACC0["ab_in"]
        for c in range(6):
            pe_chunk(pe, C0 + c, A0 + c, aT, turn=mixer_turn(c - 1) if c else None, before=before_group(c))

        def before(n):
            pe.wait_ge(mix_lo, (2, 4, 5, 6)[n])
        C0, A0 = CHUNK0["ab_out"], ACC0["ab_out"]
        pe_chunk(pe, C0, A0, aT, turn=mixer_turn(5), before=before)
        with pe.Fori(0, NCH - 1) as j:
            pe_chunk(pe, j + (C0 + 1), j + (A0 + 1), aT, turn=pe_turn(pe, turn_out[0], j))
        pe_proj(pe, 0)
        pe_mlp(pe, 0)
        pe_product(pe, "gate0", bT, turn0=turn_mlp[0], turn=turn_gate)
        pe_product(pe, "c_in", aT, turn0=turn_gate, stop=8)
        def kv_turn(half):
            def turn(g):
                n = NKV * half + g
                if n == 0:
                    freed(pe, "c_in", 6)
                if n >= 2:
                    pe.wait_ge(c_ev, n - 1)
                for t in range(TOK):
                    mm = pe.transpose(tp[n % 2][:, t * P:(t + 1) * P], z1[:, t, D + n * P:D + (n + 1) * P], ident[:, :])
                mm.then_inc(c_tp, 1)
            return turn
        for half in range(2):
            pe_chunk(pe, CHUNK0["c_in"] + 8 + half, ACC0["c_in"] + 8 + half, aT, turn=kv_turn(half))
        B = CHUNK0["cmp_k"] * GT
        pe.wait_ge(gw_lo_done, 1)
        freed(pe, "gates", 0)
        for kt in range(KT):
            for a, w in ((aT_hi, gw_hi), (aT_hi, gw_lo), (aT_lo, gw_hi)):
                mm = pe.matmul(acc[0][0:BW, 0:S], w[:, kt * NG:kt * NG + BW], a[:, kt, :],
                               start=(kt == 0 and a is aT_hi and w is gw_hi), stop=(kt == KT - 1 and a is aT_lo))
        mm.then_inc(gates_done, 1)

        def gates_turn():
            pe.wait_ge(acc_free[0], ACC0["gates"] + 1)
            for t in range(TOK):
                mm = pe.transpose(acc[1][:, t * P:t * P + NG], gatesT[0:NG, t * P:(t + 1) * P], ident[0:NG, 0:NG])
                mm.then_inc(acc0_done if t == 0 else gates_tp, 1)

        def hidden_turn(kv):
            pe.wait_ge(chid_done, kv + 1)
            if kv == 0:
                pe.wait_ge(c_ev, 8)
                pe.wait_ge(cmp_in, 64)
            else:
                pe.wait_ge(cmp_ev, 1)
            for f in range(HID // P):
                mm = pe.transpose(tp[0][:, f * M:(f + 1) * M], chid[:, f * P:(f + 1) * P], ident[0:M, 0:M])
            mm.then_inc(chid_tp, 1)

        def second_product(kv):
            pe.wait_ge(chid_ev, kv + 1)
            if kv == 0:
                for f in range(HID // P):
                    mm = pe.matmul(tp[1][:, 0:M], cw2[:, 0, f, :], chidT[:, f * M:(f + 1) * M], start=(f == 0), stop=(f == HID // P - 1))
            else:
                for g in range(NKV):
                    for f in range(HID // P):
                        mm = pe.matmul(tp[1][0:NCMP, g * HD:(g + 1) * HD], chidT[:, f * M + g * NCMP:f * M + (g + 1) * NCMP],
                                       cw2[:, 1, f, :], start=(f == 0), stop=(f == HID // P - 1))
            mm.then_inc(cmp_mm, 1)
        for m in range(CMP_GROUPS):
            kv, n = m // (2 * GT), m % (2 * GT)
            if n == 0:
                pe.wait_ge(acc_free[kv], ACC0["gates"] + 1)
                pe.wait_ge(blk_lo_done, 2 * kv + 1)
            if n == 2:
                pe.wait_ge(blk_lo_done, 2 * kv + 2)
            if m == 1:
                gates_turn()
            if m == V_GROUP + 2:
                hidden_turn(0)
            if m == V_GROUP + 4:
                second_product(0)
            pe.wait_ge(split_done, B + m + 1)
            for i in range(GT):
                tok = GT * n + i
                for a, w in ((blk_hi[kv], w_hi), (blk_hi[kv], w_lo), (blk_lo[kv], w_hi)):
                    mm = pe.matmul(acc[kv][0:BW, :], a[:, tok * M:tok * M + BW], w[:, m % RING, i, :],
                                   start=(tok == 0 and a is blk_hi[kv] and w is w_hi),
                                   stop=(tok == CL - 1 and a is blk_lo[kv]))
            mm.then_inc(group_used, 1)
        hidden_turn(1)
        second_product(1)
        pe.wait_ge(cmp_ev, 2)
        pe_attention(pe, attn1)
        pe_product(pe, "c_out", aT, z1, "y1", once(lambda: pe.wait_ge(y_done, attn2a.unit0)), turn=turn_out[1])
        pe_proj(pe, 1)
        pe_mlp(pe, 1)
        pe_product(pe, "gate1", bT, turn0=turn_mlp[1])
        pe_product(pe, "ab2_in", aT, h, "ab2_in", once(lambda: pe.wait_ge(fin_done, 1)))
        pe_attention(pe, attn2a)
        pe_attention(pe, attn2b)
        pe_product(pe, "ab2_out", aT, z2, "ab2_out", once(lambda: pe.wait_ge(y_done, attn3.unit0)))
        pe_product(pe, "c2_in", aT, h, "c2_in", after_residual(pe, "ab2_out"))
        pe_attention(pe, attn3)
        pe_product(pe, "c2_out", aT, z3, "c2_out", once(lambda: pe.wait_ge(y_done, attn3.unit0 + 16)))

    ctx.close()


LOADS = 9
RPB_DMAS = NH * 4
LRU_STEPS = 6
M = NKV * NCMP
GW = KT * NG + 20
BW = M + 8
BLK = CL * M + 8
BLK_PARTS = slice(0, 8 * M + 8), slice(8 * M + 8, BLK)
V_GROUP, CMP_GROUPS = 8, 16



def _stream(w, rows=None):
    k, n = w.shape
    if n % NW:
        w = np.pad(w, ((0, 0), (0, NW - n % NW)))
        n = w.shape[1]
    return w.reshape(k // (GT * P), GT, P, n // NW, NW).transpose(3, 0, 2, 1, 4).reshape(-1, P, GT * NW)


def _layout(a):
    f = np.float32
    a = {k: np.asarray(v) for k, v in a.items()}
    parts = []

    def mlp(l):
        up, down = a["mlp_w_up"][l], a["mlp_w_down"][l]
        for q in range(4):
            parts.append(_stream(up[:, q * D:(q + 1) * D]))
            parts.append(_stream(down[q * D:(q + 1) * D]))

    def proj(l):
        w = a["ple_w_proj"][l].reshape(2, P, NCH, NW).transpose(2, 1, 0, 3).reshape(NCH, P, 2 * NW)
        parts.append(np.pad(w, ((0, 0), (0, 0), (0, 2 * NW))))

    w_in, w_out = a["ab_w_in"][0], a["ab_w_out"][0]
    parts += [_stream(w_in[:, part:part + LRU]) for part in (0, 2 * LRU, LRU)]
    parts.append(_stream(np.concatenate([w_out[LRU:], w_out[:LRU]])))
    proj(0)
    mlp(0)
    c_in = a["c_w_in"][0]
    parts += [_stream(a["ple_w_gate"][0]), _stream(c_in[:, :C_GATES])]
    parts += [_stream(a[k][0].reshape(CL * HD, HID)) for k in ("c_cmp_w1_k", "c_cmp_w1_v")]
    parts.append(_stream(a["c_w_out"][0]))
    proj(1)
    mlp(1)
    parts += [_stream(a["ple_w_gate"][1]), _stream(a["w_in_ab_2"][0]), _stream(a["w_out_ab_2"][0]),
              _stream(a["w_in_c_2"][0]), _stream(a["w_out_c_2"][0])]
    o = {"wstream": np.concatenate(parts)}
    assert o["wstream"].shape[0] == NC * GT

    def column(v, n):
        return v.reshape(n, P).T

    o["x"] = a["x"]
    o["gate_w"] = np.pad(c_in[:, C_GATES:].reshape(KT, P, NG).transpose(1, 0, 2).reshape(P, KT * NG),
                         ((0, 0), (0, GW - KT * NG)))
    o["xT"] = a["x"][0].T
    o["pT"] = a["p"][:, 0].transpose(0, 2, 1)
    g = [a["ln_mix_g"][0], a["ln_mlp_g"][0], a["ln_ple_g"][0], a["ln_mix_g"][1], a["ln_mlp_g"][1], a["ln_ple_g"][1],
         a["ln_ab_2"][0], a["ln_c_2"][0]]
    o["gains"] = np.stack([column(v, KT) for v in g], 1)
    v = [*a["ab_conv_w"][0], a["ab_conv_b"][0], a["ab_b_rgate"][0], a["ab_b_igate"][0], a["ab_lambda"][0],
         a["ab_pool_scale"][0]]
    o["vecs"] = np.stack([column(x, LT) for x in v], 1)
    o["pool_w"] = a["ab_pool_w"][0].reshape(LT, P, S).transpose(1, 0, 2)
    o["w_r"], o["w_i"] = a["ab_w_rgate"][0], a["ab_w_igate"][0]
    o["w2_k"], o["w2_v"] = a["c_cmp_w2_k"][0], a["c_cmp_w2_v"][0]
    o["posT"] = np.stack([a["c_cmp_pos_k"][0].T, a["c_cmp_pos_v"][0].T])
    o["sinks"] = np.broadcast_to(a["sink_a_2"][0], (P, 8))
    o["g1"] = np.broadcast_to(a["ln_final_g"], (P, D))
    o["g2"] = np.broadcast_to(a["ln_f_2"], (P, D))
    o["rpb"] = np.tile(np.pad(a["rpb_c_2"][0], ((0, 0), (0, 0), (48, 49))), (1, 1, 64))

    t = np.arange(S)
    dist = t[:, None] - t[None, :]
    slope = np.exp2(-8.0 * np.arange(1, NH + 1) / NH)
    neg = -1e30

    def table(b):
        return b.reshape(4, 4, TOK, P, S).transpose(0, 3, 1, 2, 4).reshape(4, P, 4 * TOK * S).astype(f)

    o["ident"] = np.eye(P, dtype=f)
    o["bias1"] = table(np.where(dist >= 0, -slope[:, None, None] * dist, neg))
    far = np.abs(dist)
    times = sum(((far <= w // 2) & (dist % d == 0)).astype(int) for w, d in ((128, 1), (512, 4), (2048, 16)))
    b = np.where(far <= 128, -slope[:, None, None] * far, neg)
    b[8:] = np.where(times > 0, -slope[8:, None, None] * far + np.log(np.maximum(times, 1)), neg)
    o["bias2"] = table(b)
    end = np.arange(NCMP) * 16 + CL - 1
    dc = t[:, None] - end[None, :]
    bc = np.where(dc >= 0, -slope[:, None, None] * dc, neg)
    o["bias_c"] = bc.reshape(NH, TOK, P, NCMP).transpose(2, 0, 1, 3).astype(f)
    o["valid_c"] = (dc >= 0).reshape(TOK, P, NCMP).transpose(1, 0, 2).astype(f)
    c = np.arange(64)
    c0 = np.clip(c - 8, 0, 48)
    inside = (c[None, :] >= c0[:, None]) & (c[None, :] < c0[:, None] + 16)
    o["mask3"] = np.tile(np.where(inside, 0.0, neg), (2, 4)).astype(f)
    cnt = np.minimum(np.arange(PADP) + 1, np.array([2, 4, 8, 16])[:, None])
    o["invcnt"] = np.broadcast_to((1.0 / cnt).astype(f), (P, 4, PADP))
    return {k: np.ascontiguousarray(v) for k, v in o.items()}


def kernel(**inputs):
    import concourse.bacc as bacc
    from concourse.bass_utils import run_bass_kernel_spmd

    arrays = _layout(inputs)
    nc = bacc.Bacc("TRN2", target_bir_lowering=False, num_devices=1)
    A = {k: nc.dram_tensor(f"in_{k}", v.shape, mybir.dt.from_np(v.dtype), kind="ExternalInput").ap()
         for k, v in arrays.items()}
    A["bias3"] = nc.dram_tensor("bias3", (4, P, 4 * TOK * S), F32, kind="Internal").ap()
    out = nc.dram_tensor("out", (1, S, D), F32, kind="ExternalOutput").ap()
    build(nc, A, out)
    r = run_bass_kernel_spmd(nc, [{f"in_{k}": v for k, v in arrays.items()}], core_ids=[0])
    return r.results[0]["out"]
```
